# Optimizing a Trainium2 kernel written in Bass

```python
import math
import jax, jax.numpy as jnp
from jax import lax
import numpy as np

'''One inference step (4 trunk layers) of a YOCO-style hybrid decoder: two Griffin
RG-LRU recurrent layers, then two differential-attention layers that all read ONE
shared K/V produced from the residual stream after the last recurrent layer. Every
layer has a pre-RMSNorm gated ConvFFN (causal width-3 depthwise conv between up-proj
and activation). T5 relative-position bias (32 log buckets per head, one table) is
added to both softmax maps of every differential-attention layer.

Inputs:
  x_prompt (BATCH, SEQ, D_MODEL)          prompt tokens, positions 0..SEQ-1
  x_sample (DEC_BATCH, DEC_SEQ, D_MODEL)  new tokens at positions PAST_LEN..PAST_LEN+DEC_SEQ-1
  state_rglru_h    (N_A_LAYERS, DEC_BATCH, D_RNN)               RG-LRU hidden state
  state_rglru_conv (N_A_LAYERS, DEC_BATCH, RG_CONV_W-1, D_RNN)  last 3 conv-input rows
  state_ffn_conv   (DEPTH, DEC_BATCH, FFN_CONV_W-1, 2*D_FF)     last 2 up-projected rows
  cache_k (N_POOL, PAGE_SIZE, N_HEADS, 2, HEAD_DIM)  paged shared keys (two branches)
  cache_v (N_POOL, PAGE_SIZE, N_HEADS, 2*HEAD_DIM)   paged shared values
  page_table (DEC_BATCH, N_PAGES) int32
  followed by the weights.
Output tuple:
  (y_prompt (BATCH,SEQ,D_MODEL), y_sample (DEC_BATCH,DEC_SEQ,D_MODEL),
   p_rglru_h (N_A_LAYERS,BATCH,D_RNN), p_rglru_conv (N_A_LAYERS,BATCH,3,D_RNN),
   p_ffn_conv (DEPTH,BATCH,2,2*D_FF), p_k (BATCH,SEQ,N_HEADS,2,HEAD_DIM),
   p_v (BATCH,SEQ,N_HEADS,2*HEAD_DIM),
   s_rglru_h (N_A_LAYERS,DEC_BATCH,D_RNN), s_rglru_conv (N_A_LAYERS,DEC_BATCH,3,D_RNN),
   s_ffn_conv (DEPTH,DEC_BATCH,2,2*D_FF), s_k (DEC_BATCH,DEC_SEQ,N_HEADS,2,HEAD_DIM),
   s_v (DEC_BATCH,DEC_SEQ,N_HEADS,2*HEAD_DIM))
'''

D_MODEL = 1024
BATCH = 1
SEQ = 1024
DEPTH = 2
DEC_BATCH = 8
DEC_SEQ = 4
PAST_LEN = 256
PAGE_SIZE = 128

N_A_LAYERS = DEPTH // 2
N_B_LAYERS = DEPTH - N_A_LAYERS
D_RNN = D_MODEL
N_RG_BLOCKS = 8
RG_BLOCK = D_RNN // N_RG_BLOCKS
RG_CONV_W = 4
RG_C = 8.0
HEAD_DIM = 64
N_HEADS = D_MODEL // (2 * HEAD_DIM)
D_K = N_HEADS * 2 * HEAD_DIM
D_V = N_HEADS * 2 * HEAD_DIM
ATTN_SCALE = HEAD_DIM ** -0.5
D_FF = 3 * D_MODEL
FFN_CONV_W = 3
N_BUCKETS = 32
MAX_DISTANCE = 128
Q_BLOCK = 128
EPS = 1e-6
NEG_INF = -1e30

kernel_name = 'yoco_rglru_diffattn_step'

def rmsnorm(x, g):
    xf = x.astype(jnp.float32)
    xf = xf * lax.rsqrt(jnp.mean(xf * xf, axis=-1, keepdims=True) + EPS)
    return (xf * g.astype(jnp.float32)).astype(x.dtype)

def causal_dwconv(x_full, w, b):
    width = w.shape[0]
    t_len = x_full.shape[1] - width + 1
    out = b
    for j in range(width):
        out = out + x_full[:, j:j + t_len] * w[j]
    return out

def block_diag(x, w, b):
    bsz, t_len, _ = x.shape
    xb = x.reshape(bsz, t_len, N_RG_BLOCKS, RG_BLOCK)
    return jnp.einsum('btnc,ncd->btnd', xb, w).reshape(bsz, t_len, D_RNN) + b

def rglru_mixer(x, h0, conv_buf, positions, w_in, conv_w, conv_b, w_a, b_a, w_x, b_x, lam, w_out):
    u = x @ w_in
    gate_branch, rec = u[..., :D_RNN], u[..., D_RNN:]
    x_full = jnp.concatenate([conv_buf.astype(rec.dtype), rec], axis=1)
    xc = causal_dwconv(x_full, conv_w, conv_b)
    new_buf = x_full[:, -(RG_CONV_W - 1):]
    r = jax.nn.sigmoid(block_diag(xc, w_a, b_a).astype(jnp.float32))
    i = jax.nn.sigmoid(block_diag(xc, w_x, b_x).astype(jnp.float32))
    log_a = -RG_C * r * jax.nn.softplus(-lam.astype(jnp.float32))
    reset = (positions == 0)[None, :, None]
    a = jnp.where(reset, 0.0, jnp.exp(log_a))
    mult = jnp.where(reset, 1.0, jnp.sqrt(-jnp.expm1(2.0 * log_a)))
    bterm = mult * i * xc.astype(jnp.float32)
    bterm = bterm.at[:, 0].add(a[:, 0] * h0.astype(jnp.float32))

    def combine(left, right):
        return (left[0] * right[0], right[0] * left[1] + right[1])

    _, h = lax.associative_scan(combine, (a, bterm), axis=1)
    y = (h.astype(x.dtype) * jax.nn.gelu(gate_branch)) @ w_out
    return y, h[:, -1].astype(x.dtype), new_buf

def conv_ffn(x, buf, w_up, conv_w, conv_b, w_down):
    u = x @ w_up
    u_full = jnp.concatenate([buf.astype(u.dtype), u], axis=1)
    uc = causal_dwconv(u_full, conv_w, conv_b)
    new_buf = u_full[:, -(FFN_CONV_W - 1):]
    val, gate = uc[..., :D_FF], uc[..., D_FF:]
    return (jax.nn.gelu(gate) * val) @ w_down, new_buf

def rel_bucket(rel):
    n = jnp.maximum(rel, 0)
    max_exact = N_BUCKETS // 2
    nf = jnp.maximum(n, 1).astype(jnp.float32)
    large = max_exact + (jnp.log(nf / max_exact) / math.log(MAX_DISTANCE / max_exact)
                         * (N_BUCKETS - max_exact)).astype(jnp.int32)
    large = jnp.minimum(large, N_BUCKETS - 1)
    return jnp.where(n < max_exact, n, large)

def diff_attn_core(q, q_pos, segments, rel_bias, lam):
    scores = []
    for k, v, k_pos in segments:
        s = jnp.einsum('bqhcd,bkhcd->bhcqk', q, k).astype(jnp.float32) * ATTN_SCALE
        rel = q_pos[:, None] - k_pos[None, :]
        bias = jnp.transpose(jnp.take(rel_bias, rel_bucket(rel), axis=0), (2, 0, 1)).astype(jnp.float32)
        s = jnp.where((rel >= 0)[None, None, None], s + bias[None, :, None], NEG_INF)
        scores.append(s)
    p = jax.nn.softmax(jnp.concatenate(scores, axis=-1), axis=-1)
    w = p[:, :, 0] - lam * p[:, :, 1]
    out = 0.0
    off = 0
    for k, v, k_pos in segments:
        n = k.shape[1]
        out = out + jnp.einsum('bhqk,bkhe->bqhe', w[..., off:off + n].astype(v.dtype), v)
        off += n
    return out

def diff_attn_layer(x, positions, segments, w_q, lq1, lk1, lq2, lk2, subln, w_o, rel_bias, layer_idx):
    bsz, t_len, _ = x.shape
    q = (x @ w_q).reshape(bsz, t_len, N_HEADS, 2, HEAD_DIM)
    lam_init = 0.8 - 0.6 * math.exp(-0.3 * layer_idx)
    lam = (jnp.exp(jnp.sum(lq1.astype(jnp.float32) * lk1.astype(jnp.float32)))
           - jnp.exp(jnp.sum(lq2.astype(jnp.float32) * lk2.astype(jnp.float32))) + lam_init)
    if t_len % Q_BLOCK == 0:
        nb = t_len // Q_BLOCK
        qb = jnp.moveaxis(q.reshape(bsz, nb, Q_BLOCK, N_HEADS, 2, HEAD_DIM), 1, 0)
        pb = positions.reshape(nb, Q_BLOCK)
        o = lax.map(lambda qp: diff_attn_core(qp[0], qp[1], segments, rel_bias, lam), (qb, pb))
        o = jnp.moveaxis(o, 0, 1).reshape(bsz, t_len, N_HEADS, 2 * HEAD_DIM)
    else:
        o = diff_attn_core(q, positions, segments, rel_bias, lam)
    o = rmsnorm(o, subln) * (1.0 - lam_init)
    return o.reshape(bsz, t_len, D_V) @ w_o

def shared_kv(x, kv_norm, w_kv):
    bsz, t_len, _ = x.shape
    kv = rmsnorm(x, kv_norm) @ w_kv
    k = kv[..., :D_K].reshape(bsz, t_len, N_HEADS, 2, HEAD_DIM)
    v = kv[..., D_K:].reshape(bsz, t_len, N_HEADS, 2 * HEAD_DIM)
    return k, v

def run_trunk(x, pos0, rg_h0, rg_buf0, ffn_buf0, past, p):
    t_len = x.shape[1]
    positions = pos0 + jnp.arange(t_len, dtype=jnp.int32)
    new_h, new_rbuf, new_fbuf = [], [], []
    segments = None
    k_new = None
    v_new = None
    for l in range(DEPTH):
        xn = rmsnorm(x, p['norm_mix'][l])
        if l < N_A_LAYERS:
            y, h_last, rbuf = rglru_mixer(xn, rg_h0[l], rg_buf0[l], positions,
                                          p['rg_w_in'][l], p['rg_conv_w'][l], p['rg_conv_b'][l],
                                          p['rg_w_a'][l], p['rg_b_a'][l], p['rg_w_x'][l], p['rg_b_x'][l],
                                          p['rg_lambda'][l], p['rg_w_out'][l])
            new_h.append(h_last)
            new_rbuf.append(rbuf)
        else:
            if l == N_A_LAYERS:
                k_new, v_new = shared_kv(x, p['kv_norm'], p['w_kv'])
                segments = [(k_new, v_new, positions)]
                if past is not None:
                    pk, pv = past
                    segments = [(pk, pv, jnp.arange(pk.shape[1], dtype=jnp.int32))] + segments
            j = l - N_A_LAYERS
            y = diff_attn_layer(xn, positions, segments, p['attn_w_q'][j], p['lam_q1'][j], p['lam_k1'][j],
                                p['lam_q2'][j], p['lam_k2'][j], p['attn_subln'][j], p['attn_w_o'][j],
                                p['rel_bias'], l)
        x = x + y
        y, fbuf = conv_ffn(rmsnorm(x, p['norm_ffn'][l]), ffn_buf0[l], p['ffn_w_up'][l],
                           p['ffn_conv_w'][l], p['ffn_conv_b'][l], p['ffn_w_down'][l])
        new_fbuf.append(fbuf)
        x = x + y
    return (rmsnorm(x, p['final_norm']), jnp.stack(new_h), jnp.stack(new_rbuf),
            jnp.stack(new_fbuf), k_new, v_new)

def setup_inputs(seed: int = 0) -> dict:
    key = jax.random.key(seed)
    ks = iter(jax.random.split(key, 48))
    f32 = jnp.float32

    def nrm(shape, scale):
        return jax.random.normal(next(ks), shape, f32) * scale

    n_pages = PAST_LEN // PAGE_SIZE
    used = DEC_BATCH * n_pages
    n_pool = used + max(1, used // 4)
    page_table = jax.random.permutation(next(ks), n_pool)[:used].reshape(DEC_BATCH, n_pages).astype(jnp.int32)
    u_lam = jax.random.uniform(next(ks), (N_A_LAYERS, D_RNN), f32, 0.9, 0.999)
    return {
        'x_prompt': nrm((BATCH, SEQ, D_MODEL), 1.0),
        'x_sample': nrm((DEC_BATCH, DEC_SEQ, D_MODEL), 1.0),
        'state_rglru_h': nrm((N_A_LAYERS, DEC_BATCH, D_RNN), 0.5),
        'state_rglru_conv': nrm((N_A_LAYERS, DEC_BATCH, RG_CONV_W - 1, D_RNN), 0.5),
        'state_ffn_conv': nrm((DEPTH, DEC_BATCH, FFN_CONV_W - 1, 2 * D_FF), 0.5),
        'cache_k': nrm((n_pool, PAGE_SIZE, N_HEADS, 2, HEAD_DIM), 1.0),
        'cache_v': nrm((n_pool, PAGE_SIZE, N_HEADS, 2 * HEAD_DIM), 1.0),
        'page_table': page_table,
        'rel_bias': nrm((N_BUCKETS, N_HEADS), 0.3),
        'norm_mix': 1.0 + nrm((DEPTH, D_MODEL), 0.02),
        'norm_ffn': 1.0 + nrm((DEPTH, D_MODEL), 0.02),
        'final_norm': 1.0 + nrm((D_MODEL,), 0.02),
        'rg_w_in': nrm((N_A_LAYERS, D_MODEL, 2 * D_RNN), D_MODEL ** -0.5),
        'rg_conv_w': nrm((N_A_LAYERS, RG_CONV_W, D_RNN), RG_CONV_W ** -0.5),
        'rg_conv_b': nrm((N_A_LAYERS, D_RNN), 0.02),
        'rg_w_a': nrm((N_A_LAYERS, N_RG_BLOCKS, RG_BLOCK, RG_BLOCK), RG_BLOCK ** -0.5),
        'rg_b_a': nrm((N_A_LAYERS, D_RNN), 0.1),
        'rg_w_x': nrm((N_A_LAYERS, N_RG_BLOCKS, RG_BLOCK, RG_BLOCK), RG_BLOCK ** -0.5),
        'rg_b_x': nrm((N_A_LAYERS, D_RNN), 0.1),
        'rg_lambda': jnp.log(u_lam / (1.0 - u_lam)),
        'rg_w_out': nrm((N_A_LAYERS, D_RNN, D_MODEL), D_RNN ** -0.5),
        'kv_norm': 1.0 + nrm((D_MODEL,), 0.02),
        'w_kv': nrm((D_MODEL, D_K + D_V), D_MODEL ** -0.5),
        'attn_w_q': nrm((N_B_LAYERS, D_MODEL, D_K), D_MODEL ** -0.5),
        'lam_q1': nrm((N_B_LAYERS, HEAD_DIM), 0.1),
        'lam_k1': nrm((N_B_LAYERS, HEAD_DIM), 0.1),
        'lam_q2': nrm((N_B_LAYERS, HEAD_DIM), 0.1),
        'lam_k2': nrm((N_B_LAYERS, HEAD_DIM), 0.1),
        'attn_subln': 1.0 + nrm((N_B_LAYERS, 2 * HEAD_DIM), 0.02),
        'attn_w_o': nrm((N_B_LAYERS, D_V, D_MODEL), D_V ** -0.5),
        'ffn_w_up': nrm((DEPTH, D_MODEL, 2 * D_FF), D_MODEL ** -0.5),
        'ffn_conv_w': nrm((DEPTH, FFN_CONV_W, 2 * D_FF), FFN_CONV_W ** -0.5),
        'ffn_conv_b': nrm((DEPTH, 2 * D_FF), 0.02),
        'ffn_w_down': nrm((DEPTH, D_FF, D_MODEL), D_FF ** -0.5),
    }

def reference(x_prompt, x_sample, state_rglru_h, state_rglru_conv, state_ffn_conv, cache_k, cache_v,
              page_table, rel_bias, norm_mix, norm_ffn, final_norm, rg_w_in, rg_conv_w, rg_conv_b,
              rg_w_a, rg_b_a, rg_w_x, rg_b_x, rg_lambda, rg_w_out, kv_norm, w_kv, attn_w_q,
              lam_q1, lam_k1, lam_q2, lam_k2, attn_subln, attn_w_o, ffn_w_up, ffn_conv_w,
              ffn_conv_b, ffn_w_down):
    p = {'rel_bias': rel_bias, 'norm_mix': norm_mix, 'norm_ffn': norm_ffn, 'final_norm': final_norm,
         'rg_w_in': rg_w_in, 'rg_conv_w': rg_conv_w, 'rg_conv_b': rg_conv_b, 'rg_w_a': rg_w_a,
         'rg_b_a': rg_b_a, 'rg_w_x': rg_w_x, 'rg_b_x': rg_b_x, 'rg_lambda': rg_lambda,
         'rg_w_out': rg_w_out, 'kv_norm': kv_norm, 'w_kv': w_kv, 'attn_w_q': attn_w_q,
         'lam_q1': lam_q1, 'lam_k1': lam_k1, 'lam_q2': lam_q2, 'lam_k2': lam_k2,
         'attn_subln': attn_subln, 'attn_w_o': attn_w_o, 'ffn_w_up': ffn_w_up,
         'ffn_conv_w': ffn_conv_w, 'ffn_conv_b': ffn_conv_b, 'ffn_w_down': ffn_w_down}
    dt = x_prompt.dtype
    bp = x_prompt.shape[0]
    yp, hp, rbp, fbp, kp, vp = run_trunk(
        x_prompt, 0,
        jnp.zeros((N_A_LAYERS, bp, D_RNN), dt),
        jnp.zeros((N_A_LAYERS, bp, RG_CONV_W - 1, D_RNN), dt),
        jnp.zeros((DEPTH, bp, FFN_CONV_W - 1, 2 * D_FF), dt),
        None, p)
    bs = x_sample.shape[0]
    past_len = page_table.shape[1] * cache_k.shape[1]
    past_k = jnp.take(cache_k, page_table, axis=0).reshape(bs, past_len, N_HEADS, 2, HEAD_DIM)
    past_v = jnp.take(cache_v, page_table, axis=0).reshape(bs, past_len, N_HEADS, 2 * HEAD_DIM)
    ys, hs, rbs, fbs, ks, vs = run_trunk(x_sample, past_len, state_rglru_h, state_rglru_conv,
                                         state_ffn_conv, (past_k, past_v), p)
    return (yp, ys, hp, rbp, fbp, kp, vp, hs, rbs, fbs, ks, vs)


_drawn_inputs = setup_inputs


def setup_inputs(seed=0):
    import zlib

    import numpy as np

    out = dict(_drawn_inputs(seed))
    spreads = {}
    factors = {'final_norm': 2.89, 'kv_norm': 2.723, 'lam_q1': 5.692, 'lam_k1': 8.0, 'attn_subln': 5.468}
    for name, (base, spread) in spreads.items():
        noise = np.random.default_rng([zlib.crc32(name.encode()), seed]).standard_normal(out[name].shape)
        drawn = base * np.exp(spread * noise) if base else spread * noise
        out[name] = __import__('jax').numpy.asarray(drawn.astype(out[name].dtype))
    for name, factor in factors.items():
        out[name] = (out[name] * factor).astype(out[name].dtype)
    return out
```

```python
from contextlib import ExitStack

import numpy as np

import concourse.bass as bass
from concourse import mybir

P = 128
D = 1024
KT = D // P
SEQ = 1024
NB, NS = 8, 4
TS = NB * NS
T = SEQ + TS
NCH = 3
CH = T // NCH
PAST = 256
PAGE = 128
NPG = PAST // PAGE
NPOOL = 20
NH = 8
HD = 64
DFF = 3072
FT = DFF // P
GROUPS = FT // 2
RW = 4
FW = 3
EPS = 1e-6
NEG = -1e30
BUCKETS, MAXDIST = 32, 128
LAM_INIT = 0.8 - 0.6 * float(np.exp(-0.3))

U_RG = 0
U_OUT = U_RG + 3 * KT
U_F0 = U_OUT + KT
F_UNITS = 6 * GROUPS
U_K = U_F0 + F_UNITS
U_V = U_K + KT
U_Q = U_V + KT
U_O = U_Q + KT
U_F1 = U_O + KT
NU = U_F1 + F_UNITS

A_N0 = 0
A_RG = A_N0 + 1
A_OUT = A_RG + 4 * KT
A_NF0 = A_OUT + KT
A_F0 = A_NF0 + 1
F_ACCS = 12 * GROUPS
A_NKV = A_F0 + F_ACCS
A_K = A_NKV + 1
A_V = A_K + KT
A_Q = A_V + KT
A_O = A_Q + KT
A_NF1 = A_O + KT
A_F1 = A_NF1 + 1
A_NY = A_F1 + F_ACCS


def up_acc(a, g, j):
    return a + j if g == 0 else a + 4 + (g - 1) * 12 + j


def down_acc(a, g, o):
    return a + 4 + g * 12 + (4 if g < GROUPS - 1 else 0) + o


def accs_after():
    out = []
    for n in range(KT):
        b = A_RG + 4 * n
        out += [b + 1, b + 2, b + 4]
    out += [A_OUT + o + 1 for o in range(KT)]

    def ffn(a):
        r = [up_acc(a, 0, j) + 1 for j in range(4)]
        for g in range(GROUPS):
            if g + 1 < GROUPS:
                r += [up_acc(a, g + 1, j) + 1 for j in range(4)]
            r += [down_acc(a, g, 3) + 1, down_acc(a, g, 7) + 1]
        return r

    out += ffn(A_F0)
    for a in (A_K, A_V, A_Q, A_O):
        out += [a + o + 1 for o in range(KT)]
    return out + ffn(A_F1)


AFTER = accs_after()
assert len(AFTER) == NU

C_GMIX0, C_GFFN0, C_GKV, C_GMIX1, C_GFFN1, C_GOUT = (8 * i for i in range(6))
C_RGW = 48
C_RGB = C_RGW + RW * KT
C_BA = C_RGB + KT
C_BX = C_BA + KT
C_LAM = C_BX + KT
C_SUB = C_LAM + KT
C_FW = C_SUB + 1
NFC = (FW + 1) * 2 * FT
NCOL = C_FW + 2 * NFC

REL0 = SEQ - 1
LINE = SEQ + P
SROWS = 2 * NS * NH
NKEY = PAST + NS


def program(nc, I, O, S):
    F32, F32R, I32 = mybir.dt.float32, mybir.dt.float32r, mybir.dt.int32
    ALU, ACT = mybir.AluOpType, mybir.ActivationFunctionType
    X_AXIS = mybir.AxisListType.X

    with ExitStack() as ctx:
        top = [(nc.sbuf_base + 63) // 64 * 64]

        def at(name, shape, dt, offset):
            assert offset + 4 * int(np.prod(shape[1:])) <= nc.sbuf_usable_end, name
            return nc.alloc_sbuf_tensor_at(name, shape, dt, offset=offset)

        def sb(name, shape, dt=F32):
            t = at(name, shape, dt, top[0])
            top[0] += (4 * int(np.prod(shape[1:])) + 31) // 32 * 32
            return t

        b0 = top[0]
        X = sb("x", [P, KT, T])
        a0 = top[0]
        Y = sb("y", [P, KT, T])
        n0 = top[0]
        XNH = sb("xn_hi", [P, KT, T], F32R)
        XNL = sb("xn_lo", [P, KT, T], F32R)
        n1 = top[0]
        WRAW = sb("w_raw", [P, 2, KT, P])
        WHI = sb("w_hi", [P, 2, KT, P], F32R)
        WLO = sb("w_lo", [P, 2, KT, P], F32R)
        COL = sb("columns", [P, NCOL])
        ONES = sb("ones", [P, P])
        IDENT = sb("ident", [P, P])
        EPSC = sb("eps", [P, 1])
        CARRY = sb("carriers", [P, 11])
        HBA = sb("half_b_a", [P, KT])
        HBX = sb("half_b_x", [P, KT])
        SP2 = sb("softplus_twice", [P, KT])
        SPT = sb("softplus_tmp", [P, 4, KT])
        NLAM = sb("neg_lambda", [P, 4])
        SUBG = sb("subln_scaled", [P, 1])
        CROW = sb("sample_row_factor", [P, 1])
        T8 = sb("tmp8", [P, NB])
        RST = sb("rg_conv_state", [P, KT, NB, RW - 1])
        H0 = sb("rg_h_state", [P, KT, NB])
        RTAIL = sb("rg_conv_tails", [P, KT, NB + 1, RW - 1])
        HTAIL = sb("rg_h_tails", [P, KT, NB + 1])
        l0 = top[0]
        LINEW = 1088
        Z = [sb(f"line{i}", [P, LINEW]) for i in range(7)]
        XCH = sb("xc_hi", [P, T], F32R)
        XCL = sb("xc_lo", [P, T], F32R)
        FST = sb("ffn_state", [P, 2 * FT, NB, FW - 1])
        FTAIL = sb("ffn_tails", [P, 2 * FT, NB + 1, FW - 1])

        LAMV = at("lam_vectors", [P, 4, HD], F32, a0)
        LAMP = at("lam_products", [P, 2, HD], F32, a0 + 1024)
        TAB = at("bias_table", [BUCKETS + 1, NH], F32, a0 + 2048)
        HOT = at("one_hot", [BUCKETS + 1, LINE], F32, a0 + 4096)
        BLN = at("bias_line", [NH, LINE], F32, a0 + 4096 + 4 * LINE)
        HHI = at("h_hi", [P, 4, T], F32R, a0)
        HLO = at("h_lo", [P, 4, T], F32R, a0 + 16 * T)
        KTR = at("k_t", [P, KT, T], F32, a0)
        OT = at("o_t", [P, KT, T], F32, a0)
        QT = at("q_t", [P, KT, T], F32, b0)
        v0 = l0 + 4 * 4 * LINEW
        V = at("v", [P, NH, KT, P], F32, v0)
        VS = at("v_sample", [TS, NH, P], F32, v0 + 4 * SEQ * KT)
        VTS = at("v_sample_t", [P, NH, TS], F32, v0 + 4 * SEQ * (KT + 1))
        o = [n0]

        def xa(name, shape, dt=F32):
            t = at(name, shape, dt, o[0])
            o[0] += (4 * int(np.prod(shape[1:])) + 31) // 32 * 32
            assert o[0] <= n1, name
            return t

        PR = xa("probs", [P, 2, 2, SEQ])
        WC = xa("w_comb", [P, SEQ])
        WTS = xa("w_t", [P, 2, SEQ])
        OQ = xa("o_q", [P, 2, 8, P])
        OQS = xa("o_sq", [P, 8, P])
        BIAS = xa("bias_strip", [P, 2, SEQ])
        QS = xa("q_head", [P, 2, SEQ])
        KS = xa("k_head", [P, 2, SEQ])
        MX = xa("maxima", [P, 2, 4])
        SSUM = xa("sums", [P, 2, 2, 8])
        SM = xa("small", [P, 4, 8])
        o[0] = n0
        KC = xa("k_pages", [P, 2, NPG, NH, PAGE])
        VC = xa("v_pages", [P, 2, NPG, NH, P])
        QP = xa("q_padded", [P, 2, NH * (SROWS + 1)])
        SPR = xa("sample_probs", [P, PAST + TS])
        SC1 = xa("sample_c1", [P, NPG, 2, NS * NH])
        SCN = xa("sample_c1_new", [TS, 2, NS * NH])
        SW = xa("sample_w_t", [P, NPG, 2, NS * NH])
        SWN = xa("sample_w_new_t", [TS, 2, NS * NH])
        SBI = xa("sample_bias", [P, NKEY])
        SMK = xa("sample_new_bias", [P, NB // 2, TS])
        SST = xa("sample_stats", [P, 8])
        OSM = xa("o_sample", [P, NH, TS])
        OSQ = xa("o_sample_sq", [P, NH, TS])
        PT = xa("pages", [1, NB * NPG], I32)

        PS = ctx.enter_context(nc.psum_tensor("psum", [P, 8, 512], F32))

        def sem(name):
            return ctx.enter_context(nc.semaphore(name))

        w_in = [sem("w_in0"), sem("w_in1")]
        w_hi, w_lo = sem("w_hi"), sem("w_lo")
        acc_done = sem("acc_done")
        acc_free = [sem("acc_free0"), sem("acc_free1")]
        sq_done, sum_done, xt_done = sem("sq_done"), sem("sum_done"), sem("xt_done")
        nhi_done, nlo_done = sem("nhi_done"), sem("nlo_done")
        x_in, c_in, lam_in, tab_in, rst_in, fst_in = (
            sem(n) for n in ("x_in", "c_in", "lam_in", "tab_in", "rst_in", "fst_in"))
        pool_const, act_const, dve_const, scal_done = (
            sem(n) for n in ("pool_const", "act_const", "dve_const", "scal_done"))
        line_mm, line_read, line_out = (
            sem(n) for n in ("line_mm", "line_read", "line_out"))
        rec_ready, rec_used, xc_ready, xch_ready, xcl_ready, s_ready, sqrt_ready, y_done = (
            sem(n) for n in ("rec_ready", "rec_used", "xc_ready", "xch_ready", "xcl_ready",
                             "s_ready", "sqrt_ready", "y_done"))
        FS = [{n: sem(f"{n}{i}") for n in ("u_ready", "u_used", "vc_ready", "gc_ready", "gg_ready",
                                           "hf_ready", "hh_ready", "hl_ready", "tail_out")}
              for i in range(2)]
        k_out, x_out, x_back = sem("k_out"), sem("x_out"), sem("x_back")
        vt_out = [sem("vt_out0"), sem("vt_out1")]
        vtr_done, vtr_read = sem("vtr_done"), sem("vtr_read")
        head_in = [sem("head_in0"), sem("head_in1")]
        s_done, ttr_done, nm_ready, e_done, wc_done, wt_done, wt_read, pv_done, o_read = (
            sem(n) for n in ("s_done", "ttr_done", "nm_ready", "e_done", "wc_done", "wt_done",
                             "wt_read", "pv_done", "o_read"))
        osq_done, var_done, std_done, on_done, ot_done, ot_read = (
            sem(n) for n in ("osq_done", "var_done", "std_done", "on_done", "ot_done", "ot_read"))
        pages_in, pg_in, sb_in = sem("pages_in"), sem("pg_in"), sem("sb_in")
        qp_done, ss_done, snm_done, sexp_done, spn_done, st_done, sc1_done, sw_done, so_done, so_read = (
            sem(n) for n in ("qp_done", "ss_done", "snm_done", "sexp_done", "spn_done", "st_done",
                             "sc1_done", "sw_done", "so_done", "so_read"))
        sosq_done, sored_done, sostd_done, son_done, ot_full = (
            sem(n) for n in ("sosq_done", "sored_done", "sostd_done", "son_done", "ot_full"))
        rg_out = sem("rg_out")
        y_out = [sem("y_out0"), sem("y_out1")]
        dve_step, act_step = sem("dve_step"), sem("act_step")

        ATT_STEPS = 24

        block = ctx.enter_context(nc.Block())

        def col(c, n=None):
            return COL[:, c:c + 1] if n is None else COL[:, bass.ds(n + c, 1)]

        def as_acc(line):
            return line.rearrange("p (c t) -> p c t", c=NCH)

        def acc(a):
            s = a % 2
            return PS[:, 3 * s:3 * s + 3, 0:CH]

        def tile(region, k, i=None, m=1):
            if i is None:
                return region[:, k, :]
            return region[:, bass.ds(i * m + k, 1), :].rearrange("p a t -> p (a t)")

        def samples(line, hist):
            return line[:, hist + SEQ:hist + SEQ + NB * (hist + NS)].rearrange(
                "p (b s) -> p b s", b=NB)

        def val(base, i=None, m=0):
            return base if i is None else i * m + base

        def wait_acc(eng, a, i=None, m=0):
            eng.wait_ge(acc_done, val(a + 1, i, m))

        def wait_read(eng, a, i=None, m=0):
            eng.wait_ge(acc_free[a % 2], val(a // 2 + 1, i, m // 2))

        def wait_room(eng, a, i=None, m=0):
            if a >= 2:
                wait_read(eng, a - 2, i, m)

        class Steps:

            def __init__(self, eng, s):
                self.eng, self.s, self.n, self.i, self.per = eng, s, 0, None, 0

            def __call__(self, ins):
                ins.then_inc(self.s, 1)
                self.n += 1
                self.eng.wait_ge(self.s, val(self.n, self.i, self.per))

            def enter(self, i, per):
                self.start, self.i, self.per = self.n, i, per

            def leave(self, turns):
                assert self.n == self.start + self.per, (self.n - self.start, self.per)
                self.n = self.start + self.per * turns
                self.i = None

        @block.sync
        def _(sp):
            def load_weights(s, u):
                sp.dma_start(WRAW[:, s], I["w"][bass.ds(u, 1)].rearrange("u p k f -> p (u k) f")
                             ).then_inc(w_in[s], 16)

            def pairs(lo, hi):
                with sp.Fori(lo // 2, hi // 2) as i:
                    for s in range(2):
                        sp.wait_ge(w_lo, i * 2 + s - 1)
                        load_weights(s, i * 2 + s)

            load_weights(0, 0)
            load_weights(1, 1)
            pairs(2, U_O + 2)

            def head(s, h):
                for dst, src in ((QS, QT), (KS, KTR)):
                    sp.dma_start(dst[:, s], src[:, bass.ds(h, 1), 0:SEQ].rearrange("p a t -> p (a t)")
                                 ).then_inc(head_in[s], 16)
                strip = S["line"][bass.ds(h, 1), P - 1:P - 1 + P * (LINE - 1)]
                sp.dma_start(BIAS[:, s], strip.rearrange("h (p m) -> p (h m)", m=LINE - 1)[:, 0:SEQ]
                             ).then_inc(head_in[s], 16)

            sp.wait_ge(line_out, 16)
            wait_read(sp, A_Q + KT - 2)
            wait_read(sp, A_Q + KT - 1)
            head(0, 0)
            head(1, 1)
            with sp.Fori(1, NH // 2) as i:
                for s in range(2):
                    sp.wait_ge(ttr_done, i * 32 - 32 + (2 + (s + 1) * 16))
                    head(s, i * 2 + s)

            sp.wait_ge(ot_read, 1 + 2 * NH)
            sp.dma_start(PT[:, :], I["page_table"]).then_inc(pages_in, 16)
            for b in range(2):
                for r in range(2 * NS):
                    q = b * SROWS + r * NH
                    off = REL0 - PAST - r % NS
                    sp.dma_start(SBI[q:q + NH, :], S["line"][:, off:off + NKEY]).then_inc(sb_in, 16)
            sp.wait_ge(pages_in, 16)
            with sp.Fori(0, NB // 2) as pr:
                sp.wait_ge(so_read, pr + 1)
                for b in range(2):
                    for g in range(NPG):
                        page = sp.value_load(PT[0:1, bass.ds(pr * 4 + (b * 2 + g), 1)], min_val=0,
                                             max_val=NPOOL - 1)
                        sp.dma_start(KC[:, b, g], I["cache_k"][bass.ds(page, 1)].rearrange(
                            "n d h s -> d (n h) s")).then_inc(pg_in, 16)
                        sp.dma_start(VC[:, b, g], I["cache_v"][bass.ds(page, 1)].rearrange(
                            "n s h e -> s (n h) e")).then_inc(pg_in, 16)

            pairs(U_O + 2, NU)
            for k in range(KT):
                sp.wait_ge(xt_done, 5 * KT + k + 1)
                sp.dma_start(O["y"][:, k, :], Z[k % 2][:, 0:T]).then_inc(y_out[k % 2], 16)
            for s in range(2):
                sp.wait_ge(y_out[s], 16 * (KT // 2))
            sp.wait_ge(rg_out, 32)
            sp.wait_ge(k_out, 16)
            for s in range(2):
                sp.wait_ge(vt_out[s], 16 * (KT // 2))
                sp.wait_ge(FS[s]["tail_out"], 16)

        @block.gpsimd
        def _(pool):
            pool.memset(ONES[:, :], 1.0).then_inc(pool_const, 1)
            pool.memset(EPSC[:, :], EPS).then_inc(pool_const, 1)
            pool.memset(IDENT[:, :], 0.0).then_inc(pool_const, 1)
            pool.wait_ge(pool_const, 3)
            pool.affine_select(out=IDENT[:, :], in_=IDENT[:, :], compare_op=ALU.not_equal, fill=1.0,
                               base=0, pattern=[[-1, P]], channel_multiplier=1).then_inc(pool_const, 1)

            def split(u, used, i=None, m=0, stride=0):
                s = u % 2
                if used:
                    pool.wait_ge(acc_done, val(used, i, stride))
                pool.wait_ge(w_in[s], val(16 * (u // 2 + 1), i, 8 * m))
                pool.tensor_tensor(CARRY[:, 0:1], EPSC[:, :], EPSC[:, :], ALU.add)
                pool.tensor_scalar(WHI[:, s], WRAW[:, s], 1.0, 0.0, ALU.mult, ALU.add
                                   ).then_inc(w_hi, 1)
                pool.wait_ge(w_hi, val(u + 1, i, m))
                pool.tensor_tensor(WLO[:, s], WRAW[:, s], WHI[:, s].bitcast(F32), ALU.subtract
                                   ).then_inc(w_lo, 1)

            def straight(lo, hi):
                for u in range(lo, hi):
                    split(u, AFTER[u - 2] if u >= 2 else 0)

            def turns(u0, m, n):
                stride = AFTER[u0 + m] - AFTER[u0]
                used = [AFTER[u0 + j - 2] for j in range(m)]
                assert m % 2 == 0 and all(AFTER[u0 + j + i * m - 2] == used[j] + i * stride
                                          for i in range(n) for j in range(m))
                with pool.Fori(0, n) as i:
                    for j in range(m):
                        split(u0 + j, used[j], i, m, stride)

            def ffn(u0):
                n = (GROUPS - 2) // 2
                straight(u0, u0 + 6)
                turns(u0 + 6, 12, n - 1)
                straight(u0 + 6 + 12 * (n - 1), u0 + F_UNITS)

            straight(0, 6)
            turns(6, 6, KT // 2 - 1)
            straight(U_OUT, U_OUT + 2)
            turns(U_OUT + 2, 2, KT // 2 - 1)
            ffn(U_F0)
            straight(U_K, U_K + 2)
            turns(U_K + 2, 2, KT * 3 // 2 - 1)
            straight(U_O, U_O + 2)
            turns(U_O + 2, 2, KT // 2 - 1)
            ffn(U_F1)

        @block.tensor
        def _(pe):
            def product(s, k, a, hi, lo, start, stop):
                for w, r, first, final in ((WHI, hi, True, False), (WLO, hi, False, False),
                                           (WHI, lo, False, True)):
                    for c in range(NCH):
                        last = pe.matmul(PS[:, 3 * (a % 2) + c, 0:CH], w[:, s, k, :],
                                         r[:, c * CH:(c + 1) * CH],
                                         start=start and first, stop=stop and final)
                return last

            def unit(u, a, i=None, m=0, stride=0, lows=None):
                pe.wait_ge(w_lo, val(u + 1, i, m))
                wait_room(pe, a, i, stride)
                for k in range(KT):
                    if lows is not None:
                        pe.wait_ge(nlo_done, lows + k + 1)
                    last = product(u % 2, k, a, XNH[:, k, :], XNL[:, k, :], k == 0, k == KT - 1)
                last.then_inc(acc_done, 1)

            def plain(u0, a0, lows):
                unit(u0, a0, lows=lows)
                unit(u0 + 1, a0 + 1)
                with pe.Fori(0, KT // 2 - 1) as i:
                    for s in range(2):
                        unit(u0 + 2 + s, a0 + 2 + s, i, 2, 2)

            def norm_sum(a, r):
                pe.wait_ge(sum_done, KT * (r + 1))
                wait_room(pe, a)
                for c in range(NCH):
                    last = pe.matmul(PS[:, 3 * (a % 2) + c, 0:CH], ONES[:, :],
                                     Z[2][:, c * CH:(c + 1) * CH], start=True, stop=True)
                last.then_inc(acc_done, 1)

            pe.wait_ge(pool_const, 4)
            pe.wait_ge(tab_in, 32)
            pe.wait_ge(dve_const, 1)
            lw = LINE // NCH
            for c in range(NCH):
                last = pe.matmul(PS[0:NH, 3 + c, 0:lw], TAB[:, :], HOT[:, c * lw:(c + 1) * lw],
                                 start=True, stop=True)
            last.then_inc(line_mm, 1)

            norm_sum(A_N0, 0)
            pe.wait_ge(line_read, 1)

            def rg(j, i=None, lows=None):
                u, a = U_RG + 3 * j, A_RG + 4 * j
                unit(u, a, i, 6, 8, lows)
                unit(u + 1, a + 1, i, 6, 8)
                pe.wait_ge(w_lo, val(u + 3, i, 6))
                pe.wait_ge(xcl_ready, val(j + 1, i, 2))
                for g in range(2):
                    wait_room(pe, a + 2 + g, i, 8)
                    product((u + 2) % 2, g, a + 2 + g, XCH[:, :], XCL[:, :], True, True
                            ).then_inc(acc_done, 1)

            rg(0, lows=0)
            rg(1)
            with pe.Fori(0, KT // 2 - 1) as i:
                rg(2, i)
                rg(3, i)
            plain(U_OUT, A_OUT, KT)

            def ffn(l, u0, a0, lows):
                def up(u, a, i=None, lows=None):
                    for j in range(4):
                        unit(u + j, a + j, i, 12, 24, lows if j == 0 else None)

                def down(u, a, g, i=None):
                    pe.wait_ge(FS[l]["hl_ready"], val(2 * g + 2, i, 4))
                    for o in range(KT):
                        s = (u + o // 4) % 2
                        if o % 4 == 0:
                            pe.wait_ge(w_lo, val(u + o // 4 + 1, i, 12))
                        wait_room(pe, a + o, i, 24)
                        for t in range(2):
                            h = 2 * (g % 2) + t
                            last = product(s, 2 * (o % 4) + t, a + o, HHI[:, h, :], HLO[:, h, :],
                                           t == 0, t == 1)
                        last.then_inc(acc_done, 1)

                up(u0, a0, lows=lows)
                with pe.Fori(0, (GROUPS - 2) // 2) as i:
                    for g in range(2):
                        up(u0 + 4 + 6 * g, up_acc(a0, g + 1, 0), i)
                        down(u0 + 8 + 6 * g, down_acc(a0, g, 0), g, i)
                g = GROUPS - 1
                u = u0 + 4 + 6 * (g - 1)
                up(u, up_acc(a0, g, 0))
                down(u + 4, down_acc(a0, g - 1, 0), g - 1)
                down(u + 6, down_acc(a0, g, 0), g)

            norm_sum(A_NF0, 1)
            ffn(0, U_F0, A_F0, 2 * KT)

            norm_sum(A_NKV, 2)
            plain(U_K, A_K, 3 * KT)

            def v_back(j, i=None):
                wait_read(pe, A_V + j, i, 2)
                for b in range(KT):
                    if b % 4 == 0:
                        pe.wait_ge(vtr_read, val(2 * j + b // 4 + 1, i, 4))
                    last = pe.transpose(PS[:, 6 + b // 4, (b % 4) * P:(b % 4 + 1) * P],
                                        Z[j % 2][:, b * P:(b + 1) * P], IDENT[:, :])
                    if b % 4 == 3:
                        last.then_inc(vtr_done, 1)

            unit(U_V, A_V)
            with pe.Fori(0, KT // 2 - 1) as i:
                for s in range(2):
                    unit(U_V + 1 + s, A_V + 1 + s, i, 2, 2)
                    v_back(s, i)
            unit(U_V + KT - 1, A_V + KT - 1)
            v_back(KT - 2)
            v_back(KT - 1)
            pe.wait_ge(vtr_read, 2 * KT + 2)
            for h in range(NH):
                last = pe.transpose(PS[0:TS, 6 + h // 4, (h % 4) * P:(h % 4 + 1) * P],
                                    VTS[:, h, :], IDENT[:, :])
            last.then_inc(vtr_done, 1)
            plain(U_Q, A_Q, 4 * KT)

            wait_read(pe, A_Q + KT - 2)
            wait_read(pe, A_Q + KT - 1)
            pe.wait_ge(vtr_read, 2 * KT + 3)
            with pe.Fori(0, NH // 2) as hp:
                for t in range(ATT_STEPS):
                    if t < 16:
                        s, i = t // 8, t % 8
                        n = (i + 1) * P
                        if i == 0:
                            pe.wait_ge(head_in[s], hp * 48 + 48)
                        for c in range(2):
                            pe.wait_ge(ttr_done, hp * 32 + (2 * t + c + 1))
                            for b in range(0, n, 512):
                                w = min(512, n - b)
                                last = pe.matmul(PS[:, 2 * c + b // 512, 0:w],
                                                 QS[c * HD:(c + 1) * HD, s, i * P:(i + 1) * P],
                                                 KS[c * HD:(c + 1) * HD, s, b:b + w],
                                                 start=True, stop=True)
                            last.then_inc(s_done, 1)
                    if 1 <= t < 17:
                        v = t - 1
                        pe.wait_ge(wc_done, hp * 16 + (v + 1))
                        pe.wait_ge(wt_read, hp * 16 + (v + 1))
                        for b in range(v % 8 + 1):
                            last = pe.transpose(PS[:, 4 + b // 4, (b % 4) * P:(b % 4 + 1) * P],
                                                WC[:, b * P:(b + 1) * P], IDENT[:, :])
                        last.then_inc(wt_done, 1)
                    if 2 <= t < 18:
                        v = t - 2
                        s, i = v // 8, v % 8
                        pe.wait_ge(wt_read, hp * 16 + (v + 2))
                        pe.wait_ge(o_read, hp * 16 + (v + 1))
                        for b in range(i + 1):
                            last = pe.matmul(PS[:, 6, 0:P], WTS[:, v % 2, b * P:(b + 1) * P],
                                             V[:, bass.ds(hp * 2 + s, 1), b, :
                                               ].rearrange("p a e -> p (a e)"),
                                             start=(b == 0), stop=(b == i))
                        last.then_inc(pv_done, 1)
                    for s in range(2):
                        for half in range(2):
                            if t == 13 + 8 * s + 2 * half:
                                pe.wait_ge(on_done, hp * 2 + (s + 1))
                                pe.wait_ge(ot_read, hp * 4 + (2 * s + half + 1))
                                for b in range(4):
                                    last = pe.transpose(PS[:, 7, b * P:(b + 1) * P],
                                                        OQ[:, s, 4 * half + b, :], IDENT[:, :])
                                last.then_inc(ot_done, 1)

            with pe.Fori(0, NB // 2) as pr:
                pe.wait_ge(pg_in, pr * 128 + 128)
                pe.wait_ge(qp_done, pr + 1)
                for b in range(2):
                    rows = slice(b * SROWS, (b + 1) * SROWS)
                    for h in range(NH):
                        pe.matmul(PS[rows, 0, 0:PAST], QP[:, b, h * SROWS:(h + 1) * SROWS],
                                  KC[:, b, :, h, :], start=(h == 0), stop=(h == NH - 1))
                    for h in range(NH):
                        last = pe.matmul(PS[rows, 0, PAST:PAST + TS],
                                         QP[:, b, h * SROWS:(h + 1) * SROWS], KTR[:, h, SEQ:T],
                                         start=(h == 0), stop=(h == NH - 1))
                last.then_inc(ss_done, 1)
                pe.wait_ge(spn_done, pr + 1)
                for g in range(NPG):
                    pe.transpose(PS[:, 1, g * P:(g + 1) * P], SPR[:, g * P:(g + 1) * P], IDENT[:, :])
                pe.transpose(PS[0:TS, 2, 0:P], SPR[:, PAST:PAST + TS], IDENT[:, :]
                             ).then_inc(st_done, 1)
                pe.wait_ge(sw_done, pr + 1)
                for b in range(2):
                    for h in range(NH):
                        q = (b * NH + h) * NS
                        for g in range(NPG):
                            pe.matmul(PS[:, 3, q:q + NS], VC[:, b, g, h, :],
                                      SW[:, g, b, h:NS * NH:NH], start=(g == 0), stop=False)
                        last = pe.matmul(PS[:, 3, q:q + NS], VS[:, h, :], SWN[:, b, h:NS * NH:NH],
                                         start=False, stop=True)
                last.then_inc(so_done, 1)
            pe.wait_ge(sosq_done, 1)
            pe.matmul(PS[:, 1, 0:NH * TS], ONES[:, :], OSQ[:, :, :].rearrange("p h t -> p (h t)"),
                      start=True, stop=True).then_inc(sored_done, 1)
            pe.wait_ge(sostd_done, 1)

            plain(U_O, A_O, 5 * KT)
            norm_sum(A_NF1, 3)
            ffn(1, U_F1, A_F1, 6 * KT)
            norm_sum(A_NY, 4)

        @block.scalar
        def _(act):
            step = Steps(act, act_step)

            def evac_line(a, line, hist, i=None, m=0):
                wait_acc(act, a, i, m)
                b = 3 * (a % 2)
                act.activation(line[:, hist:hist + 2 * CH].rearrange("p (c t) -> p c t", c=2),
                               PS[:, b:b + 2, 0:CH], ACT.Copy)
                act.activation(line[:, hist + 2 * CH:hist + SEQ], PS[:, b + 2, 0:SEQ - 2 * CH],
                               ACT.Copy)
                act.activation(samples(line, hist)[:, :, hist:hist + NS],
                               PS[:, b + 2, SEQ - 2 * CH:CH].rearrange("p (b s) -> p b s", b=NB),
                               ACT.Copy).then_inc(acc_free[a % 2], 1)

            def squares(r):
                for k in range(KT):
                    if k >= 2:
                        act.wait_ge(sum_done, KT * r + k - 1)
                    act.activation(Z[k % 2][:, 0:T], X[:, k, :], ACT.Square).then_inc(sq_done, 1)

            def root(a):
                wait_acc(act, a)
                act.activation(as_acc(Z[3][:, 0:T]), acc(a), ACT.Sqrt, bias=EPSC[:, :],
                               scale=1.0 / D).then_inc(acc_free[a % 2], 1)

            def highs(n):
                for k in range(KT):
                    act.wait_ge(xt_done, KT * n + k + 1)
                    act.activation(XNH[:, k, :], Z[k % 2][:, 0:T], ACT.Copy).then_inc(nhi_done, 1)

            act.dma_start(X[:, :, :], I["x"]).then_inc(x_in, 16)
            act.dma_start(COL[:, :], I["columns"]).then_inc(c_in, 16)
            act.dma_start(TAB[0:BUCKETS, :], I["rel_bias"]).then_inc(tab_in, 16)
            act.dma_start(HOT[:, :], I["one_hot"]).then_inc(tab_in, 16)
            act.dma_start(LAMV[:, :, :], I["lam"]).then_inc(lam_in, 16)
            act.dma_start(RST[:, :, :, :], I["rg_conv_state"]).then_inc(rst_in, 16)
            act.dma_start(H0[:, :, :], I["rg_h_state"]).then_inc(rst_in, 16)
            act.dma_start(FST[:, :, :, :], I["ffn_state"][0]).then_inc(fst_in, 16)

            act.wait_ge(c_in, 16)
            step(act.activation(SPT[:, 0], COL[:, C_LAM:C_LAM + KT], ACT.Abs))
            act.activation(SPT[:, 1], SPT[:, 0], ACT.Exp, scale=-1.0).then_inc(act_const, 1)
            act.wait_ge(dve_const, 4)
            act.activation(NLAM[:, 0:2], NLAM[:, 0:2], ACT.Exp).then_inc(act_const, 1)
            act.wait_ge(pool_const, 4)
            for n, q in enumerate((wt_read, ot_read)):
                act.activation(CARRY[:, 9 + n:10 + n], EPSC[:, :], ACT.Copy).then_inc(q, 1)
            act.wait_ge(line_mm, 1)
            lw = LINE // NCH
            act.activation(BLN[:, :].rearrange("h (c n) -> h c n", c=NCH), PS[0:NH, 3:6, 0:lw],
                           ACT.Copy).then_inc(line_read, 1)
            act.wait_ge(line_read, 1)
            act.dma_start(S["line"].rearrange("h (p i) -> h p i", p=P),
                          BLN[:, :].unsqueeze(1).to_broadcast([NH, P, LINE])
                          ).then_inc(line_out, 16)

            act.wait_ge(x_in, 16)
            squares(0)
            root(A_N0)
            highs(0)
            act.wait_ge(rst_in, 32)
            act.wait_ge(scal_done, 1)
            with act.Fori(0, KT) as n:
                act.wait_ge(rec_used, n + 1)
                evac_line(A_RG, Z[4], RW - 1, n, 4)
                act.activation(samples(Z[4], RW - 1)[:, :, 0:RW - 1],
                               RST[:, bass.ds(n, 1)].rearrange("p a b s -> p (a b) s"), ACT.Copy
                               ).then_inc(rec_ready, 1)
                act.wait_ge(xc_ready, n + 1)
                act.activation(XCH[:, :], Z[0][:, 0:T], ACT.Copy).then_inc(xch_ready, 1)
                act.wait_ge(y_done, n + 1)
                wait_acc(act, A_RG + 1, n, 4)
                act.activation(as_acc(Z[5][:, 0:T]), acc(A_RG + 1), ACT.Gelu_apprx_tanh
                               ).then_inc(acc_free[(A_RG + 1) % 2], 1)
                wait_acc(act, A_RG + 2, n, 4)
                act.activation(as_acc(Z[6][:, 0:T]), acc(A_RG + 2), ACT.Tanh, scale=0.5,
                               bias=HBA[:, bass.ds(n, 1)]).then_inc(acc_free[(A_RG + 2) % 2], 1)
                wait_acc(act, A_RG + 3, n, 4)
                act.activation(as_acc(Z[1][:, 0:T]), acc(A_RG + 3), ACT.Tanh, scale=0.5,
                               bias=HBX[:, bass.ds(n, 1)]).then_inc(acc_free[(A_RG + 3) % 2], 1)
                wait_read(act, A_RG + 2, n, 4)
                act.activation(Z[6][:, 0:T], Z[6][:, 0:T], ACT.Tanh, scale=SP2[:, bass.ds(n, 1)],
                               bias=SP2[:, bass.ds(n, 1)]).then_inc(s_ready, 1)
                act.wait_ge(s_ready, n + 1)
                act.activation(Z[2][:, 0:T], Z[6][:, 0:T], ACT.Sqrt).then_inc(sqrt_ready, 1)
            act.wait_ge(y_done, KT + 1)
            act.dma_start(O["rg_conv"], RTAIL[:, :, :, :]).then_inc(rg_out, 16)
            act.dma_start(O["rg_h"], HTAIL[:, :, :]).then_inc(rg_out, 16)
            wait_acc(act, A_OUT - 1)
            for k in range(KT):
                act.activation(XNH[:, k, :], Y[:, k, :], ACT.Copy).then_inc(nhi_done, 1)

            def ffn(l, a0):
                q = FS[l]

                def up(a, g, i=None):
                    for t in range(2):
                        f = 2 * g + t
                        for v in range(2):
                            n = 2 * f + v
                            if n >= 2:
                                act.wait_ge(q["u_used"], val(n - 1, i, 8))
                            evac_line(a + 2 * t + v, Z[4 + v], FW - 1, i, 24)
                            src = (FST[:, v * FT + f] if i is None else
                                   FST[:, bass.ds(i * 4 + (v * FT + f), 1)].rearrange(
                                       "p a b s -> p (a b) s"))
                            act.activation(samples(Z[4 + v], FW - 1)[:, :, 0:FW - 1], src, ACT.Copy
                                           ).then_inc(q["u_ready"], 1)
                        act.wait_ge(q["gc_ready"], val(f + 1, i, 4))
                        act.activation(Z[1][:, 0:T], Z[1][:, 0:T], ACT.Gelu_apprx_tanh
                                       ).then_inc(q["gg_ready"], 1)
                        act.wait_ge(q["hf_ready"], val(f + 1, i, 4))
                        if g >= 2:
                            wait_acc(act, down_acc(a0, g - 2, KT - 1), i, 24)
                        act.activation(HHI[:, f % 4, :], Z[2][:, 0:T], ACT.Copy
                                       ).then_inc(q["hh_ready"], 1)

                for g in range(3):
                    up(up_acc(a0, g, 0), g)
                with act.Fori(0, (GROUPS - 4) // 2) as i:
                    for g in (3, 4):
                        up(up_acc(a0, g, 0), g, i)
                up(up_acc(a0, GROUPS - 1, 0), GROUPS - 1)
                act.wait_ge(q["u_used"], 4 * GROUPS)
                act.dma_start(O["ffn_conv"][l], FTAIL[:, :, :, :]).then_inc(q["tail_out"], 16)
                wait_read(act, down_acc(a0, GROUPS - 1, KT - 2))
                wait_read(act, down_acc(a0, GROUPS - 1, KT - 1))

            wait_read(act, A_OUT + KT - 2)
            wait_read(act, A_OUT + KT - 1)
            squares(1)
            root(A_NF0)
            highs(1)
            act.wait_ge(fst_in, 16)
            ffn(0, A_F0)

            act.dma_start(S["x"], X[:, :, :]).then_inc(x_out, 16)
            squares(2)
            root(A_NKV)
            highs(2)
            with act.Fori(0, KT // 2) as i:
                for s in range(2):
                    wait_acc(act, A_K + s, i, 2)
                    act.activation(as_acc(tile(KTR, s, i, 2)), acc(A_K + s), ACT.Copy
                                   ).then_inc(acc_free[(A_K + s) % 2], 1)
            wait_read(act, A_K + KT - 2)
            wait_read(act, A_K + KT - 1)
            act.dma_start(O["k"], KTR[:, :, :]).then_inc(k_out, 16)

            def v_evac(j, i=None):
                if j >= 2:
                    act.wait_ge(vtr_done, val(2 * j - 2, i, 4))
                    act.wait_ge(vt_out[j % 2], val(16 * (j // 2), i, 16))
                wait_acc(act, A_V + j, i, 2)
                act.activation(VTS[:, j, :] if i is None else
                               VTS[:, bass.ds(i * 2 + j, 1), :].rearrange("p a t -> p (a t)"),
                               PS[:, 3 * ((A_V + j) % 2) + 2, SEQ - 2 * CH:CH], ACT.Copy)
                act.activation(as_acc(Z[j % 2][:, 0:T]), acc(A_V + j), ACT.Copy
                               ).then_inc(acc_free[(A_V + j) % 2], 1)
                wait_read(act, A_V + j, i, 2)
                dst = (O["v"][:, j, :] if i is None else
                       O["v"][:, bass.ds(i * 2 + j, 1), :].rearrange("p a t -> p (a t)"))
                act.dma_start(dst, Z[j % 2][:, 0:T]).then_inc(vt_out[j % 2], 16)

            act.wait_ge(FS[0]["tail_out"], 16)
            v_evac(0)
            v_evac(1)
            with act.Fori(0, KT // 2 - 1) as i:
                v_evac(2, i)
                v_evac(3, i)
            highs(3)
            act.wait_ge(x_out, 16)
            with act.Fori(0, KT // 2) as i:
                for s in range(2):
                    wait_acc(act, A_Q + s, i, 2)
                    act.activation(as_acc(tile(QT, s, i, 2)), acc(A_Q + s), ACT.Copy,
                                   scale=HD ** -0.5).then_inc(acc_free[(A_Q + s) % 2], 1)

            act.wait_ge(k_out, 16)
            with act.Fori(0, NH // 2) as hp:
                for t in range(ATT_STEPS):
                    if t < 16:
                        s, i = t // 8, t % 8
                        for c in range(2):
                            act.wait_ge(nm_ready, hp * 32 + (2 * t + c + 1))
                            pr = PR[:, t % 2, c, 0:(i + 1) * P]
                            act.activation(pr, pr, ACT.Exp, bias=MX[:, t % 2, 2 + c:3 + c],
                                           accum_out=SSUM[:, s, c, i:i + 1]).then_inc(e_done, 1)
                    if 1 <= t < 17:
                        v = t - 1
                        n = v % 8 + 1
                        act.wait_ge(wt_done, hp * 16 + (v + 1))
                        if v >= 2:
                            act.wait_ge(pv_done, hp * 16 + (v - 1))
                        if n <= 4:
                            act.activation(WTS[:, v % 2, 0:n * P], PS[:, 4, 0:n * P], ACT.Copy
                                           ).then_inc(wt_read, 1)
                        else:
                            act.activation(WTS[:, v % 2, 0:512], PS[:, 4, :], ACT.Copy)
                            act.activation(WTS[:, v % 2, 512:n * P], PS[:, 5, 0:n * P - 512],
                                           ACT.Copy).then_inc(wt_read, 1)
                    for s in range(2):
                        if t == 10 + 8 * s:
                            act.wait_ge(o_read, hp * 16 + (8 * (s + 1) + 1))
                            act.activation(OQS[:, :, :], OQ[:, s, :, :], ACT.Square
                                           ).then_inc(osq_done, 1)
                        if t == 11 + 8 * s:
                            act.wait_ge(var_done, hp * 2 + (s + 1))
                            act.activation(SM[:, 2], SM[:, 1], ACT.Sqrt, scale=1.0 / P
                                           ).then_inc(std_done, 1)
                        for half in range(2):
                            if t == 13 + 8 * s + 2 * half:
                                act.wait_ge(ot_done, hp * 4 + (2 * s + half + 1))
                                act.activation(
                                    OT[:, bass.ds(hp * 2 + s, 1), half * 512:(half + 1) * 512
                                       ].rearrange("p a t -> p (a t)"),
                                    PS[:, 7, :], ACT.Copy, scale=SUBG[:, :]).then_inc(ot_read, 1)

            with act.Fori(0, NB // 2) as pr:
                act.wait_ge(snm_done, pr + 1)
                act.activation(SPR[:, :], SPR[:, :], ACT.Exp, bias=SST[:, 1:2],
                               accum_out=SST[:, 2:3]).then_inc(sexp_done, 1)
                act.wait_ge(st_done, pr + 1)
                act.activation(SC1[:, :, :, :],
                               PS[:, 1, 0:NPG * P].rearrange("p (g b c r) -> p g b c r", g=NPG, b=2,
                                                             c=2)[:, :, :, 1, :], ACT.Copy)
                act.activation(SCN[:, :, :],
                               PS[0:TS, 2, 0:P].rearrange("p (b c r) -> p b c r", b=2, c=2)[:, :, 1, :],
                               ACT.Copy).then_inc(sc1_done, 1)
            act.wait_ge(so_read, NB // 2 + 1)
            act.activation(OSQ[:, :, :], OSM[:, :, :], ACT.Square).then_inc(sosq_done, 1)
            act.wait_ge(sored_done, 1)
            act.activation(OSQ[:, :, :].rearrange("p h t -> p (h t)"), PS[:, 1, 0:NH * TS], ACT.Sqrt,
                           scale=1.0 / P, bias=EPSC[:, :]).then_inc(sostd_done, 1)
            act.wait_ge(son_done, 1)
            act.activation(OT[:, :, SEQ:T], OSM[:, :, :], ACT.Copy, scale=SUBG[:, :]
                           ).then_inc(ot_full, 1)
            act.wait_ge(ot_full, 1)
            act.dma_start(X[:, :, :], S["x"]).then_inc(x_back, 16)
            act.dma_start(FST[:, :, :, :], I["ffn_state"][1]).then_inc(fst_in, 16)
            for k in range(KT):
                act.activation(XNH[:, k, :], OT[:, k, :], ACT.Copy).then_inc(nhi_done, 1)

            wait_read(act, A_O + KT - 2)
            wait_read(act, A_O + KT - 1)
            squares(3)
            root(A_NF1)
            highs(4)
            act.wait_ge(fst_in, 32)
            ffn(1, A_F1)
            squares(4)
            root(A_NY)

        @block.vector
        def _(dve):
            step = Steps(dve, dve_step)
            MUL, ADD, SUB = ALU.mult, ALU.add, ALU.subtract

            def conv(src, tmp, dst, taps, bias, hist, signal):
                n = SEQ + NB * (hist + NS)
                step(dve.tensor_scalar(tmp[:, 0:n], src[:, 0:n], taps[0], bias, MUL, ADD))
                for j in range(1, hist):
                    step(dve.scalar_tensor_tensor(tmp[:, 0:n], src[:, j:j + n], taps[j],
                                                  tmp[:, 0:n], MUL, ADD))
                dve.scalar_tensor_tensor(dst[:, 0:SEQ], src[:, hist:hist + SEQ], taps[hist],
                                         tmp[:, 0:SEQ], MUL, ADD)
                dve.scalar_tensor_tensor(dst[:, SEQ:T].rearrange("p (b s) -> p b s", b=NB),
                                         samples(src, hist)[:, :, hist:hist + NS], taps[hist],
                                         samples(tmp, hist)[:, :, 0:NS], MUL, ADD
                                         ).then_inc(signal, 1)

            def sums(r):
                for k in range(KT):
                    dve.wait_ge(sq_done, KT * r + k + 1)
                    if k == 0:
                        dve.tensor_copy(Z[2][:, 0:T], Z[0][:, 0:T]).then_inc(sum_done, 1)
                    else:
                        dve.wait_ge(sum_done, KT * r + k)
                        dve.tensor_tensor(Z[2][:, 0:T], Z[2][:, 0:T], Z[k % 2][:, 0:T], ADD
                                          ).then_inc(sum_done, 1)

            def inverse(a):
                wait_read(dve, a)
                step(dve.reciprocal(Z[3][:, 0:T], Z[3][:, 0:T]))

            def scaled(n, gain, k):
                dve.scalar_tensor_tensor(Z[k % 2][:, 0:T], X[:, k, :], col(gain + k), Z[3][:, 0:T],
                                         MUL, MUL).then_inc(xt_done, 1)

            def normed(n, m, gain):
                scaled(n, gain, 0)
                for k in range(KT):
                    if k + 1 < KT:
                        if k >= 1:
                            dve.wait_ge(nlo_done, KT * m + k)
                        scaled(n, gain, k + 1)
                    dve.wait_ge(nhi_done, KT * m + k + 1)
                    dve.wait_ge(xt_done, KT * n + k + 1)
                    dve.tensor_tensor(XNL[:, k, :], Z[k % 2][:, 0:T], XNH[:, k, :].bitcast(F32), SUB
                                      ).then_inc(nlo_done, 1)

            def lows(m, region):
                for k in range(KT):
                    dve.wait_ge(nhi_done, KT * m + k + 1)
                    dve.tensor_tensor(XNL[:, k, :], region[:, k, :], XNH[:, k, :].bitcast(F32), SUB
                                      ).then_inc(nlo_done, 1)

            def add_to_x(a, k, i=None, m=0, tm=0):
                wait_acc(dve, a, i, m)
                x = X[:, k, :] if not tm else tile(X, k, i, tm)
                dve.tensor_tensor(as_acc(x), acc(a), as_acc(x), ADD).then_inc(acc_free[a % 2], 1)

            dve.memset(TAB[BUCKETS:BUCKETS + 1, :], NEG).then_inc(dve_const, 1)
            dve.memset(Z[4][:, 0:RW - 1], 0.0).then_inc(rec_used, 1)
            dve.memset(Z[5][:, 0:FW - 1], 0.0).then_inc(y_done, 1)
            dve.memset(CROW[:, :], 1.0).then_inc(dve_const, 1)
            for j, q in enumerate((ttr_done, ttr_done, o_read, so_read, vtr_read, vtr_read)):
                dve.memset(CARRY[:, 3 + j:4 + j], 0.0).then_inc(q, 1)
            dve.wait_ge(lam_in, 16)
            for j in range(2):
                dve.tensor_tensor_reduce(LAMP[:, j], LAMV[:, 2 * j, :], LAMV[:, 2 * j + 1, :], 1.0,
                                         0.0, MUL, ADD, NLAM[:, j:j + 1]).then_inc(dve_const, 1)
            dve.wait_ge(c_in, 16)
            dve.tensor_scalar(HBA[:, :], COL[:, C_BA:C_BA + KT], 0.5, None, MUL)
            dve.tensor_scalar(HBX[:, :], COL[:, C_BX:C_BX + KT], 0.5, None, MUL)
            dve.tensor_scalar(SUBG[:, :], col(C_SUB), 1.0 - LAM_INIT, None, MUL)
            dve.wait_ge(act_const, 1)
            E, TT, W2, PP = SPT[:, 1], SPT[:, 2], SPT[:, 3], SPT[:, 0]
            step(dve.tensor_scalar(TT, E, 2.0, None, ADD))
            step(dve.reciprocal(TT, TT))
            step(dve.tensor_tensor(TT, TT, E, MUL))
            step(dve.tensor_tensor(W2, TT, TT, MUL))
            step(dve.tensor_scalar(PP, W2, 1.0 / 17, None, MUL))
            for d in (15, 13, 11, 9, 7, 5, 3):
                step(dve.scalar_tensor_tensor(PP, PP, 1.0 / d, W2, ADD, MUL))
            step(dve.scalar_tensor_tensor(PP, PP, 1.0, TT, ADD, MUL))
            step(dve.tensor_scalar(W2, COL[:, C_LAM:C_LAM + KT], -2.0, 0.0, MUL, ALU.max))
            dve.scalar_tensor_tensor(SP2[:, :], PP, 4.0, W2, MUL, ADD).then_inc(scal_done, 1)
            dve.wait_ge(act_const, 2)
            step(dve.tensor_tensor(NLAM[:, 2:3], NLAM[:, 1:2], NLAM[:, 0:1], SUB))
            step(dve.tensor_scalar(NLAM[:, 3:4], NLAM[:, 2:3], LAM_INIT, None, SUB))
            for b in range(2):
                q = slice(b * SROWS + NS * NH, (b + 1) * SROWS)
                step(dve.tensor_copy(CROW[q, :], NLAM[q, 3:4]))

            sums(0)
            inverse(A_N0)
            normed(0, 0, C_GMIX0)
            dve.wait_ge(line_out, 16)
            dve.wait_ge(rst_in, 32)
            dve.wait_ge(nlo_done, KT)
            with dve.Fori(0, KT) as n:
                step.enter(n, 13)
                dve.wait_ge(y_done, n + 1)
                REC, XC, S_, TI, SQ, RC = Z[4], Z[0], Z[6], Z[1], Z[2], Z[3]
                dve.wait_ge(rec_ready, n + 1)
                conv(REC, S_, XC, [col(C_RGW + j * KT, n) for j in range(RW)], col(C_RGB, n), RW - 1,
                     xc_ready)
                dve.tensor_copy(RTAIL[:, bass.ds(n, 1), 0, :].rearrange("p a s -> p (a s)"),
                                REC[:, SEQ:SEQ + RW - 1])
                dve.tensor_copy(RTAIL[:, bass.ds(n, 1), 1:NB + 1, :].rearrange("p a b s -> p (a b) s"),
                                samples(REC, RW - 1)[:, :, NS:NS + RW - 1]).then_inc(rec_used, 1)
                dve.wait_ge(xch_ready, n + 1)
                dve.wait_ge(xc_ready, n + 1)
                dve.tensor_tensor(XCL[:, :], XC[:, 0:T], XCH[:, :].bitcast(F32), SUB
                                  ).then_inc(xcl_ready, 1)
                wait_read(dve, A_RG + 3, n, 4)
                step(dve.scalar_tensor_tensor(TI[:, 0:T], TI[:, 0:T], 1.0, XC[:, 0:T], ADD, MUL))
                dve.wait_ge(s_ready, n + 1)
                step(dve.tensor_scalar(RC[:, 0:T], S_[:, 0:T], 1.0, None, ADD))
                step(dve.reciprocal(RC[:, 0:T], RC[:, 0:T]))
                dve.wait_ge(sqrt_ready, n + 1)
                step(dve.tensor_tensor(SQ[:, 0:T], SQ[:, 0:T], RC[:, 0:T], MUL))
                step(dve.tensor_tensor(SQ[:, 0:T], SQ[:, 0:T], TI[:, 0:T], MUL))
                dve.tensor_scalar(SQ[:, 0:1], TI[:, 0:1], 0.5, None, MUL)
                step(dve.tensor_scalar(RC[:, 0:T], RC[:, 0:T], 2.0, -1.0, MUL, ADD))
                first = RC[:, SEQ:T:NS]
                step(dve.tensor_tensor(T8[:, :], first,
                                       H0[:, bass.ds(n, 1), :].rearrange("p a b -> p (a b)"), MUL))
                step(dve.tensor_tensor(SQ[:, SEQ:T:NS], SQ[:, SEQ:T:NS], T8[:, :], ADD))
                dve.memset(RC[:, 0:1], 0.0)
                step(dve.memset(first, 0.0))
                step(dve.tensor_tensor_scan(S_[:, 0:T], RC[:, 0:T], SQ[:, 0:T], 0.0, MUL, ADD))
                dve.tensor_copy(HTAIL[:, bass.ds(n, 1), 0:1].rearrange("p a b -> p (a b)"),
                                S_[:, SEQ - 1:SEQ])
                dve.tensor_copy(HTAIL[:, bass.ds(n, 1), 1:NB + 1].rearrange("p a b -> p (a b)"),
                                S_[:, SEQ + NS - 1:T:NS])
                wait_read(dve, A_RG + 1, n, 4)
                dve.tensor_tensor(tile(Y, 0, n), S_[:, 0:T], Z[5][:, 0:T], MUL).then_inc(y_done, 1)
                step.leave(KT)
            lows(1, Y)

            def outputs(a0):
                with dve.Fori(0, KT // 2) as i:
                    for s in range(2):
                        add_to_x(a0 + s, s, i, 2, 2)

            outputs(A_OUT)

            def ffn(l, a0):
                q = FS[l]

                def convolved(g, t, v, i):
                    f = 2 * g + t
                    n = 2 * f + v
                    dve.wait_ge(q["u_ready"], val(n + 1, i, 8))
                    c = C_FW + l * NFC + v * FT + f
                    r = None if i is None else i * 4
                    src = Z[4 + v]
                    if v:
                        dve.wait_ge(q["vc_ready"], val(f + 1, i, 4))
                    elif f:
                        dve.wait_ge(q["hf_ready"], val(f, i, 4))
                    if v:
                        conv(src, Z[6], Z[1], [col(c + j * 2 * FT, r) for j in range(FW)],
                             col(c + FW * 2 * FT, r), FW - 1, q["gc_ready"])
                    else:
                        conv(src, Z[6], Z[0], [col(c + j * 2 * FT, r) for j in range(FW)],
                             col(c + FW * 2 * FT, r), FW - 1, q["vc_ready"])
                    at_ = slice(v * FT + f, v * FT + f + 1) if i is None else bass.ds(r + (v * FT + f), 1)
                    dve.tensor_copy(FTAIL[:, at_, 0, :].rearrange("p a s -> p (a s)"),
                                    src[:, SEQ:SEQ + FW - 1])
                    dve.tensor_copy(FTAIL[:, at_, 1:NB + 1, :].rearrange("p a b s -> p (a b) s"),
                                    samples(src, FW - 1)[:, :, NS:NS + FW - 1]
                                    ).then_inc(q["u_used"], 1)

                def gated(f, i):
                    dve.wait_ge(q["vc_ready"], val(f + 1, i, 4))
                    if f:
                        dve.wait_ge(q["hl_ready"], val(f, i, 4))
                    dve.wait_ge(q["gg_ready"], val(f + 1, i, 4))
                    dve.tensor_tensor(Z[2][:, 0:T], Z[0][:, 0:T], Z[1][:, 0:T], MUL
                                      ).then_inc(q["hf_ready"], 1)

                def low(f, i):
                    dve.wait_ge(q["hh_ready"], val(f + 1, i, 4))
                    dve.wait_ge(q["hf_ready"], val(f + 1, i, 4))
                    dve.tensor_tensor(HLO[:, f % 4, :], Z[2][:, 0:T], HHI[:, f % 4, :].bitcast(F32),
                                      SUB).then_inc(q["hl_ready"], 1)

                def group(g, i=None):
                    f = 2 * g
                    convolved(g, 0, 0, i)
                    convolved(g, 0, 1, i)
                    gated(f, i)
                    low(f, i)
                    convolved(g, 1, 0, i)
                    convolved(g, 1, 1, i)
                    b = down_acc(a0, g - 1, 0) if g else None

                    def outs(lo, hi):
                        if g:
                            for o in range(lo, hi):
                                add_to_x(b + o, o, i, 24)

                    outs(0, 2)
                    gated(f + 1, i)
                    outs(2, 4)
                    low(f + 1, i)
                    outs(4, KT)

                step(dve.memset(Z[4][:, 0:FW - 1], 0.0))
                step(dve.memset(Z[5][:, 0:FW - 1], 0.0))
                group(0)
                with dve.Fori(0, (GROUPS - 2) // 2) as i:
                    step.enter(i, 16)
                    group(1, i)
                    group(2, i)
                    step.leave((GROUPS - 2) // 2)
                group(GROUPS - 1)
                for o in range(KT):
                    add_to_x(down_acc(a0, GROUPS - 1, o), o)

            sums(1)
            inverse(A_NF0)
            normed(1, 2, C_GFFN0)
            ffn(0, A_F0)

            sums(2)
            inverse(A_NKV)
            normed(2, 3, C_GKV)
            dve.wait_ge(FS[0]["tail_out"], 16)

            with dve.Fori(0, KT) as j:
                for b in range(2):
                    dve.wait_ge(vtr_done, j * 2 + (b + 1))
                    dve.tensor_copy(V[:, bass.ds(j, 1), 4 * b:4 * b + 4, :].rearrange(
                        "p a t e -> p (a t) e"),
                        PS[:, 6 + b, :].rearrange("p (t e) -> p t e", t=4)).then_inc(vtr_read, 1)
            dve.wait_ge(vtr_done, 2 * KT + 1)
            dve.tensor_copy(VS[:, :, :].rearrange("p (b h) e -> p b h e", b=2),
                            PS[0:TS, 6:8, :].rearrange("p b (h e) -> p b h e", h=4)
                            ).then_inc(vtr_read, 1)
            for s in range(2):
                dve.wait_ge(vt_out[s], 16 * (KT // 2))
            normed(3, 4, C_GMIX1)

            wait_acc(dve, A_Q + KT - 1)
            with dve.Fori(0, NH // 2) as hp:
                step.enter(hp, 16 * 2 + 2 * 3)
                for t in range(ATT_STEPS):
                    if t < 16:
                        s, i = t // 8, t % 8
                        n = (i + 1) * P
                        if i == 0:
                            dve.wait_ge(head_in[s], hp * 48 + 48)
                        for c in range(2):
                            dve.wait_ge(s_done, hp * 32 + (2 * t + c + 1))
                            dve.memset(CARRY[:, 1 + c:2 + c], 0.0)
                            dve.tensor_tensor_reduce(
                                PR[:, t % 2, c, 0:n],
                                PS[:, 2 * c:2 * c + 2, :].rearrange("p b n -> p (b n)")[:, 0:n],
                                BIAS[:, s, SEQ - n:SEQ], 1.0, -3e38, ADD, ALU.max,
                                MX[:, t % 2, c:c + 1]).then_inc(ttr_done, 1)
                        for c in range(2):
                            dve.wait_ge(ttr_done, hp * 32 + (2 + 2 * t + c + 1))
                            dve.tensor_scalar(MX[:, t % 2, 2 + c:3 + c], MX[:, t % 2, c:c + 1], -1.0,
                                              None, MUL).then_inc(nm_ready, 1)
                    if 1 <= t < 17:
                        v = t - 1
                        s, i = v // 8, v % 8
                        n = (i + 1) * P
                        dve.wait_ge(e_done, hp * 32 + (2 * v + 2))
                        dve.wait_ge(wt_read, hp * 16 + (v + 1))
                        step(dve.reciprocal(SM[:, 3, 0:1], SSUM[:, s, 1, i:i + 1]))
                        step(dve.scalar_tensor_tensor(SM[:, 3, 1:2], SM[:, 3, 0:1],
                                                      NLAM[:, 3:4], SSUM[:, s, 0, i:i + 1], MUL, MUL))
                        dve.scalar_tensor_tensor(WC[:, 0:n], PR[:, v % 2, 1, 0:n], SM[:, 3, 1:2],
                                                 PR[:, v % 2, 0, 0:n], MUL, ADD).then_inc(wc_done, 1)
                    if 3 <= t < 19:
                        v = t - 3
                        s, i = v // 8, v % 8
                        dve.wait_ge(pv_done, hp * 16 + (v + 1))
                        if i == 0:
                            dve.wait_ge(ot_read, hp * 4 + 1)
                        dve.tensor_copy(OQ[:, s, i, :], PS[:, 6, 0:P]).then_inc(o_read, 1)
                    for s in range(2):
                        if t == 11 + 8 * s:
                            dve.wait_ge(osq_done, hp * 2 + (s + 1))
                            step(dve.tensor_reduce(SM[:, 0], OQS[:, :, :], X_AXIS, ADD))
                            step(dve.tensor_tensor(SM[:, 1], SSUM[:, s, 0, :], SSUM[:, s, 0, :], MUL))
                            dve.scalar_tensor_tensor(SM[:, 1], SM[:, 1], P * EPS, SM[:, 0], MUL, ADD
                                                     ).then_inc(var_done, 1)
                        if t == 12 + 8 * s:
                            dve.wait_ge(std_done, hp * 2 + (s + 1))
                            step(dve.reciprocal(SM[:, 2], SM[:, 2]))
                            dve.tensor_tensor(OQ[:, s, :, :], OQ[:, s, :, :],
                                              SM[:, 2].unsqueeze(2).to_broadcast([P, 8, P]), MUL
                                              ).then_inc(on_done, 1)
                step.leave(NH // 2)

            dve.wait_ge(ot_read, 1 + 2 * NH)
            step(dve.memset(SMK[:, :, :], NEG))
            step(dve.memset(QP[:, :, :], 0.0))
            dve.wait_ge(sb_in, 16 * 4 * NS)
            for pr in range(NB // 2):
                for b in range(2):
                    q = slice(b * SROWS, (b + 1) * SROWS)
                    j = (2 * pr + b) * NS
                    last = dve.tensor_copy(SMK[q, pr, j:j + NS], SBI[q, PAST:NKEY])
            step(last)
            with dve.Fori(0, NB // 2) as pr:
                step.enter(pr, 4)
                for c in range(2):
                    q = slice(c * HD, (c + 1) * HD)
                    last = dve.tensor_copy(
                        QP[q].rearrange("p b (h x) -> p b h x", x=SROWS + 1)[
                            :, :, :, c * NS * NH:(c + 1) * NS * NH:NH],
                        QT[q, :, bass.ds(pr * 8 + SEQ, 2 * NS)].rearrange(
                            "p h (b s) -> p b h s", b=2))
                last.then_inc(qp_done, 1)
                dve.wait_ge(ss_done, pr + 1)
                dve.tensor_tensor(SPR[:, 0:PAST], PS[:, 0, 0:PAST], SBI[:, 0:PAST], ADD)
                step(dve.tensor_tensor(SPR[:, PAST:PAST + TS], PS[:, 0, PAST:PAST + TS],
                                       SMK[:, bass.ds(pr, 1), :].rearrange("p a t -> p (a t)"), ADD))
                step(dve.reduce_max(SST[:, 0:1], SPR[:, :], X_AXIS))
                dve.tensor_scalar(SST[:, 1:2], SST[:, 0:1], -1.0, None, MUL).then_inc(snm_done, 1)
                dve.wait_ge(sexp_done, pr + 1)
                step(dve.reciprocal(SST[:, 3:4], SST[:, 2:3]))
                dve.tensor_scalar(SPR[:, :], SPR[:, :], SST[:, 3:4], CROW[:, :], MUL, MUL
                                  ).then_inc(spn_done, 1)
                dve.wait_ge(sc1_done, pr + 1)
                dve.tensor_tensor(SW[:, :, :, :],
                                  PS[:, 1, 0:NPG * P].rearrange("p (g b c r) -> p g b c r", g=NPG,
                                                                b=2, c=2)[:, :, :, 0, :],
                                  SC1[:, :, :, :], ADD)
                dve.tensor_tensor(SWN[:, :, :],
                                  PS[0:TS, 2, 0:P].rearrange("p (b c r) -> p b c r", b=2, c=2
                                                             )[:, :, 0, :],
                                  SCN[:, :, :], ADD).then_inc(sw_done, 1)
                dve.wait_ge(so_done, pr + 1)
                step(dve.tensor_copy(
                    OSM[:, :, bass.ds(pr * 8, 2 * NS)].rearrange("p h (b s) -> p b h s", b=2),
                    PS[:, 3, 0:2 * NH * NS].rearrange("p (b h s) -> p b h s", b=2, h=NH)))
                dve.memset(T8[:, 4:5], 0.0).then_inc(so_read, 1)
                step.leave(NB // 2)
            dve.wait_ge(sostd_done, 1)
            step(dve.reciprocal(OSQ[:, :, :], OSQ[:, :, :]))
            dve.tensor_tensor(OSM[:, :, :], OSM[:, :, :], OSQ[:, :, :], MUL).then_inc(son_done, 1)
            dve.wait_ge(ot_full, 1)
            lows(5, OT)
            dve.wait_ge(x_back, 16)
            outputs(A_O)
            sums(3)
            inverse(A_NF1)
            normed(4, 6, C_GFFN1)
            ffn(1, A_F1)
            sums(4)
            inverse(A_NY)
            for k in range(KT):
                if k >= 2:
                    dve.wait_ge(y_out[k % 2], 16 * (k // 2))
                scaled(5, C_GOUT, k)


_OUTPUTS = {
    "y": (P, KT, T), "rg_h": (P, KT, NB + 1), "rg_conv": (P, KT, NB + 1, RW - 1),
    "ffn_conv": (2, P, 2 * FT, NB + 1, FW - 1), "k": (P, KT, T), "v": (P, KT, T),
}


def _tiles(a, rest=()):
    a = np.asarray(a)
    return a.reshape(a.shape[0] // P, P, *a.shape[1:]).swapaxes(0, 1)


def _weight_units(w):
    k, n = w.shape
    return w.reshape(k // P, P, n // P, P).transpose(2, 1, 0, 3)


def _ffn_units(up, down):
    u = _weight_units(up)
    d = down.reshape(GROUPS, 2, P, 2, 4, P).transpose(0, 3, 2, 4, 1, 5).reshape(GROUPS, 2, P, KT, P)
    ups = [np.stack([u[f], u[FT + f]]) for f in range(FT)]
    parts = [ups[0], ups[1]]
    for g in range(GROUPS):
        if g + 1 < GROUPS:
            parts += [ups[2 * g + 2], ups[2 * g + 3]]
        parts.append(d[g])
    return np.concatenate(parts)


def _one_hot():
    rel = REL0 - np.arange(LINE)
    n = np.maximum(rel, 0)
    exact = BUCKETS // 2
    nf = np.maximum(n, 1).astype(np.float32)
    large = exact + (np.log(nf / np.float32(exact)) / np.float32(np.log(MAXDIST / exact))
                     * np.float32(BUCKETS - exact)).astype(np.int32)
    bucket = np.where(n < exact, n, np.minimum(large, BUCKETS - 1))
    hot = np.zeros((BUCKETS + 1, LINE), np.float32)
    hot[np.where(rel >= 0, bucket, BUCKETS), np.arange(LINE)] = 1.0
    return hot


def kernel(x_prompt, x_sample, state_rglru_h, state_rglru_conv, state_ffn_conv, cache_k, cache_v,
           page_table, rel_bias, norm_mix, norm_ffn, final_norm, rg_w_in, rg_conv_w, rg_conv_b,
           rg_w_a, rg_b_a, rg_w_x, rg_b_x, rg_lambda, rg_w_out, kv_norm, w_kv, attn_w_q, lam_q1,
           lam_k1, lam_q2, lam_k2, attn_subln, attn_w_o, ffn_w_up, ffn_conv_w, ffn_conv_b,
           ffn_w_down):
    import concourse.bacc as bacc
    from concourse.bass_utils import run_bass_kernel_spmd

    f = {k: np.asarray(v) for k, v in locals().items() if k not in ("bacc", "run_bass_kernel_spmd")}
    x = np.concatenate([f["x_prompt"].reshape(SEQ, D), f["x_sample"].reshape(TS, D)])

    w_in = _weight_units(f["rg_w_in"][0])
    gates = np.zeros((KT, P, KT, P), np.float32)
    gates[:, :, 0] = f["rg_w_a"][0]
    gates[:, :, 1] = f["rg_w_x"][0]
    rg = np.stack([w_in[KT:], w_in[:KT], gates], 1).reshape(3 * KT, P, KT, P)
    w = np.concatenate([
        rg, _weight_units(f["rg_w_out"][0]), _ffn_units(f["ffn_w_up"][0], f["ffn_w_down"][0]),
        _weight_units(f["w_kv"]), _weight_units(f["attn_w_q"][0]), _weight_units(f["attn_w_o"][0]),
        _ffn_units(f["ffn_w_up"][1], f["ffn_w_down"][1])])

    def cols(*vectors):
        return np.concatenate([_tiles(v) for v in vectors], 1)

    columns = cols(
        f["norm_mix"][0], f["norm_ffn"][0], f["kv_norm"], f["norm_mix"][1], f["norm_ffn"][1],
        f["final_norm"], *f["rg_conv_w"][0], f["rg_conv_b"][0], f["rg_b_a"][0], f["rg_b_x"][0],
        f["rg_lambda"][0], f["attn_subln"][0], *f["ffn_conv_w"][0], f["ffn_conv_b"][0],
        *f["ffn_conv_w"][1], f["ffn_conv_b"][1])
    lam = np.stack([f["lam_q1"][0], f["lam_k1"][0], f["lam_q2"][0], f["lam_k2"][0]])

    inputs = {
        "x": _tiles(x.T),
        "w": w,
        "columns": columns,
        "lam": np.broadcast_to(lam, (P, 4, HD)),
        "rel_bias": f["rel_bias"],
        "one_hot": _one_hot(),
        "rg_conv_state": _tiles(f["state_rglru_conv"][0].transpose(2, 0, 1)),
        "rg_h_state": _tiles(f["state_rglru_h"][0].T),
        "ffn_state": np.stack([_tiles(s.transpose(2, 0, 1)) for s in f["state_ffn_conv"]]),
        "cache_k": f["cache_k"].reshape(NPOOL, PAGE, NH, P).transpose(0, 3, 2, 1),
        "cache_v": f["cache_v"],
        "page_table": f["page_table"].reshape(1, NB * NPG),
    }
    inputs = {k: np.ascontiguousarray(v) for k, v in inputs.items()}

    nc = bacc.Bacc("TRN2", target_bir_lowering=False, num_devices=1, dynamic_dma_scratch_size=1024)
    dt = mybir.dt
    I = {k: nc.dram_tensor(f"in_{k}", v.shape, dt.from_np(v.dtype), kind="ExternalInput").ap()
         for k, v in inputs.items()}
    O = {k: nc.dram_tensor(f"out_{k}", s, dt.float32, kind="ExternalOutput").ap()
         for k, s in _OUTPUTS.items()}
    S = {k: nc.dram_tensor(f"scratch_{k}", s, dt.float32, kind="Internal").ap()
         for k, s in {"x": (P, KT, T), "line": (NH, P * LINE)}.items()}
    program(nc, I, O, S)
    r = run_bass_kernel_spmd(nc, [{f"in_{k}": v for k, v in inputs.items()}], core_ids=[0])
    out = {k: r.results[0][f"out_{k}"] for k in _OUTPUTS}

    def rows(a):
        return a.transpose(2, 1, 0).reshape(a.shape[2], -1)

    y, k, v = rows(out["y"]), rows(out["k"]), rows(out["v"])
    h = out["rg_h"].transpose(2, 1, 0).reshape(NB + 1, D)
    rc = out["rg_conv"].transpose(2, 3, 1, 0).reshape(NB + 1, RW - 1, D)
    fc = out["ffn_conv"].transpose(0, 3, 4, 2, 1).reshape(2, NB + 1, FW - 1, 2 * DFF)
    c = np.ascontiguousarray
    return (c(y[:SEQ].reshape(1, SEQ, D)), c(y[SEQ:].reshape(NB, NS, D)),
            c(h[None, :1]), c(rc[None, :1]), c(fc[:, :1]),
            c(k[:SEQ].reshape(1, SEQ, NH, 2, HD)), c(v[:SEQ].reshape(1, SEQ, NH, 2 * HD)),
            c(h[None, 1:]), c(rc[None, 1:]), c(fc[:, 1:]),
            c(k[SEQ:].reshape(NB, NS, NH, 2, HD)), c(v[SEQ:].reshape(NB, NS, NH, 2 * HD)))
```

```python
from contextlib import ExitStack

import numpy as np

import concourse.bass as bass
from concourse import mybir

P = 128
D = 1024
KT = D // P
SEQ = 1024
NB, NS = 8, 4
TS = NB * NS
T = SEQ + TS
NCH = 3
CH = T // NCH
PAST = 256
PAGE = 128
NPG = PAST // PAGE
NPOOL = 20
NH = 8
HD = 64
DFF = 3072
FT = DFF // P
GROUPS = FT // 2
RW = 4
FW = 3
EPS = 1e-6
NEG = -1e30
BUCKETS, MAXDIST = 32, 128
LAM_INIT = 0.8 - 0.6 * float(np.exp(-0.3))

U_RG = 0
U_OUT = U_RG + 3 * KT
U_F0 = U_OUT + KT
F_UNITS = 6 * GROUPS
U_K = U_F0 + F_UNITS
U_V = U_K + KT
U_Q = U_V + KT
U_O = U_Q + KT
U_F1 = U_O + KT
NU = U_F1 + F_UNITS

A_RG = 0
A_OUT = A_RG + 4 * KT
A_F0 = A_OUT + KT
F_ACCS = 12 * GROUPS
A_K = A_F0 + F_ACCS
A_V = A_K + KT
A_Q = A_V + KT
A_O = A_Q + KT
A_F1 = A_O + KT


def up_acc(a, g, j):
    return a + j if g == 0 else a + 4 + (g - 1) * 12 + j


def down_acc(a, g, o):
    return a + 4 + g * 12 + (4 if g < GROUPS - 1 else 0) + o


def accs_after():
    out = []
    for n in range(KT):
        b = A_RG + 4 * n
        out += [b + 1, b + 2, b + 4]
    out += [A_OUT + o + 1 for o in range(KT)]

    def ffn(a):
        r = [up_acc(a, 0, j) + 1 for j in range(4)]
        for g in range(GROUPS):
            if g + 1 < GROUPS:
                r += [up_acc(a, g + 1, j) + 1 for j in range(4)]
            r += [down_acc(a, g, 3) + 1, down_acc(a, g, 7) + 1]
        return r

    out += ffn(A_F0)
    for a in (A_K, A_V, A_Q, A_O):
        out += [a + o + 1 for o in range(KT)]
    return out + ffn(A_F1)


AFTER = accs_after()
assert len(AFTER) == NU

C_GMIX0, C_GFFN0, C_GKV, C_GMIX1, C_GFFN1, C_GOUT = (8 * i for i in range(6))
C_RGW = 48
C_RGB = C_RGW + RW * KT
C_BA = C_RGB + KT
C_BX = C_BA + KT
C_LAM = C_BX + KT
C_SUB = C_LAM + KT
C_FW = C_SUB + 1
NFC = (FW + 1) * 2 * FT
NCOL = C_FW + 2 * NFC

REL0 = SEQ - 1
LINE = SEQ + P
SROWS = 2 * NS * NH
NKEY = PAST + NS


def program(nc, I, O, S):
    F32, F32R, I32 = mybir.dt.float32, mybir.dt.float32r, mybir.dt.int32
    ALU, ACT = mybir.AluOpType, mybir.ActivationFunctionType
    X_AXIS = mybir.AxisListType.X

    with ExitStack() as ctx:
        top = [(nc.sbuf_base + 63) // 64 * 64]

        def at(name, shape, dt, offset):
            assert offset + 4 * int(np.prod(shape[1:])) <= nc.sbuf_usable_end, name
            return nc.alloc_sbuf_tensor_at(name, shape, dt, offset=offset)

        def sb(name, shape, dt=F32):
            t = at(name, shape, dt, top[0])
            top[0] += (4 * int(np.prod(shape[1:])) + 31) // 32 * 32
            return t

        b0 = top[0]
        X = sb("x", [P, KT, T])
        a0 = top[0]
        Y = sb("y", [P, KT, T])
        n0 = top[0]
        XNH = sb("xn_hi", [P, KT, T], F32R)
        XNL = sb("xn_lo", [P, KT, T], F32R)
        n1 = top[0]
        w0 = top[0]
        WRAW = sb("w_raw", [P, 2, KT, P])
        WHI = sb("w_hi", [P, 2, KT, P], F32R)
        WLO = sb("w_lo", [P, 2, KT, P], F32R)
        w1 = top[0]
        COL = sb("columns", [P, NCOL])
        ONES = sb("ones", [P, P])
        IDENT = sb("ident", [P, P])
        EPSC = sb("eps", [P, 1])
        CARRY = sb("carriers", [P, 11])
        HBA = sb("half_b_a", [P, KT])
        HBX = sb("half_b_x", [P, KT])
        SP2 = sb("softplus_twice", [P, KT])
        SPM = sb("softplus_minus_4", [P, KT])
        SPT = sb("softplus_tmp", [P, 4, KT])
        NLAM = sb("neg_lambda", [P, 4])
        SUBG = sb("subln_scaled", [P, 1])
        CROW = sb("sample_row_factor", [P, 1])
        T8 = sb("tmp8", [P, NB])
        RST = sb("rg_conv_state", [P, KT, NB, RW - 1])
        H0 = sb("rg_h_state", [P, KT, NB])
        RTAIL = sb("rg_conv_tails", [P, KT, NB + 1, RW - 1])
        HTAIL = sb("rg_h_tails", [P, KT, NB + 1])
        r0 = top[0]
        RINV = sb("inverse_rms", [P, T])
        l0 = top[0]
        LINEW = 1088
        Z = [sb(f"line{i}", [P, LINEW]) for i in range(7)]
        XCH = sb("xc_hi", [P, T], F32R)
        XCL = sb("xc_lo", [P, T], F32R)
        FST = sb("ffn_state", [P, 2 * FT, NB, FW - 1])
        FTAIL = sb("ffn_tails", [P, 2 * FT, NB + 1, FW - 1])

        LAMV = at("lam_vectors", [P, 4, HD], F32, a0)
        LAMP = at("lam_products", [P, 2, HD], F32, a0 + 1024)
        TAB = at("bias_table", [BUCKETS + 1, NH], F32, a0 + 2048)
        HOT = at("one_hot", [BUCKETS + 1, LINE], F32, a0 + 4096)
        BLN = at("bias_line", [NH, LINE], F32, a0 + 4096 + 4 * LINE)
        HHI = at("h_hi", [P, 4, T], F32R, a0)
        HLO = at("h_lo", [P, 4, T], F32R, a0 + 16 * T)
        KTR = at("k_t", [P, KT, T], F32, a0)
        OT = at("o_t", [P, KT, T], F32, a0)
        QT = at("q_t", [P, KT, T], F32, b0)
        v0 = l0 + 4 * 4 * LINEW
        V = at("v", [P, NH, KT, P], F32, v0)
        VS = at("v_sample", [TS, NH, P], F32, v0 + 4 * SEQ * KT)
        VTS = at("v_sample_t", [P, NH, TS], F32, v0 + 4 * SEQ * (KT + 1))

        def region(lo, hi):
            o = [lo]

            def place(name, shape, dt=F32):
                t = at(name, shape, dt, o[0])
                o[0] += (4 * int(np.prod(shape[1:])) + 31) // 32 * 32
                assert o[0] <= hi, name
                return t

            def same(name, like, dt):
                size = (4 * int(np.prod(like.shape[1:])) + 31) // 32 * 32
                return at(name, like.shape, dt, o[0] - size)

            return place, same

        xa, xsame = region(n0, n1)
        QRAW, QLO, QHI, KRAW, KLO, KHI = ([] for _ in range(6))
        for s, (place, same) in enumerate((region(l0, v0), (xa, xsame))):
            for raw, low, high, n in ((QRAW, QLO, QHI, "q"), (KRAW, KLO, KHI, "k")):
                raw.append(place(f"{n}_raw{s}", [P, SEQ]))
                low.append(same(f"{n}_low{s}", raw[-1], F32R))
                high.append(place(f"{n}_high{s}", [P, SEQ], F32R))
        PR = xa("probs", [P, 3, 2, SEQ])
        WTS = xa("w_t", [P, 2, SEQ])
        OQ = xa("o_q", [P, 2, 8, P])
        BIAS = xa("bias_strip", [P, 2, SEQ])
        MX = xa("maxima", [P, 3, 4])
        SSUM = xa("sums", [P, 2, 2, 8])
        SM = xa("small", [P, 4, 8])
        OSM = xa("o_sample", [P, NH, TS])
        OQS = at("o_sq", [P, 8, P], F32, r0)
        OSQ = at("o_sample_sq", [P, NH, TS], F32, r0)
        wa, _ = region(w0, w1)
        KC = wa("k_pages", [P, NPG, NH, PAGE])
        VC = wa("v_pages", [P, NPG, NH, P])
        QP = wa("q_padded", [P, NH * (SROWS + 1)])
        SPR = wa("sample_probs", [P, PAST + TS])
        SC1 = wa("sample_c1", [P, NPG, NS * NH])
        SCN = wa("sample_c1_new", [TS, NS * NH])
        SW = wa("sample_w_t", [P, NPG, NS * NH])
        SWN = wa("sample_w_new_t", [TS, NS * NH])
        SBI = wa("sample_bias", [SROWS, NKEY])
        SMK = wa("sample_new_bias", [SROWS, NB * (TS + NS)])
        SST = wa("sample_stats", [SROWS, 8])
        PT = wa("pages", [1, NB * NPG], I32)

        PS = ctx.enter_context(nc.psum_tensor("psum", [P, 8, 512], F32))

        def sem(name):
            return ctx.enter_context(nc.semaphore(name))

        w_in = [sem("w_in0"), sem("w_in1")]
        w_hi, w_lo = sem("w_hi"), sem("w_lo")
        acc_done = sem("acc_done")
        acc_free = [sem("acc_free0"), sem("acc_free1")]
        sq_done, sum_done, sum_mm, root_done = (
            sem(n) for n in ("sq_done", "sum_done", "sum_mm", "root_done"))
        nhi_done, nlo_done, xn_free, yt_done = (
            sem(n) for n in ("nhi_done", "nlo_done", "xn_free", "yt_done"))
        x_in = [sem(f"x_in{k}") for k in range(KT)]
        c_in, lam_in, tab_in, rst_in, fst_in = (
            sem(n) for n in ("c_in", "lam_in", "tab_in", "rst_in", "fst_in"))
        pool_const, act_const, dve_const, scal_done = (
            sem(n) for n in ("pool_const", "act_const", "dve_const", "scal_done"))
        line_mm, line_read, line_out = (
            sem(n) for n in ("line_mm", "line_read", "line_out"))
        rec_state, rec_used, xc_ready, xch_ready, xcl_ready, gel_ready, s_ready, sqrt_ready, y_done = (
            sem(n) for n in ("rec_state", "rec_used", "xc_ready", "xch_ready", "xcl_ready",
                             "gel_ready", "s_ready", "sqrt_ready", "y_done"))
        FS = [{n: sem(f"{n}{i}") for n in ("u_state", "u_used", "vc_ready", "gc_ready", "gg_ready",
                                           "hf_ready", "hh_ready", "hl_ready", "tail_out")}
              for i in range(2)]
        k_out, x_out, x_back = sem("k_out"), sem("x_out"), sem("x_back")
        vt_out = [sem("vt_out0"), sem("vt_out1")]
        vtr_done, vtr_read = sem("vtr_done"), sem("vtr_read")
        vts_done = sem("vts_done")
        head_in = [sem("head_in0"), sem("head_in1")]
        bias_in = [sem("bias_in0"), sem("bias_in1")]
        split_done = sem("split_done")
        s_done, ttr_done, nm_ready, e_done, wc_done, wt_done, wt_read, pv_done, o_read = (
            sem(n) for n in ("s_done", "ttr_done", "nm_ready", "e_done", "wc_done", "wt_done",
                             "wt_read", "pv_done", "o_read"))
        osq_done, var_done, std_done, on_done, ot_done, ot_read = (
            sem(n) for n in ("osq_done", "var_done", "std_done", "on_done", "ot_done", "ot_read"))
        pages_in, pg_in, sb_in = sem("pages_in"), sem("pg_in"), sem("sb_in")
        qp_done, ss_done, snm_done, sexp_done, spn_done, st_done, sc1_done, sw_done, so_done, so_read = (
            sem(n) for n in ("qp_done", "ss_done", "snm_done", "sexp_done", "spn_done", "st_done",
                             "sc1_done", "sw_done", "so_done", "so_read"))
        sosq_done, sored_done, sostd_done, son_done, ot_full = (
            sem(n) for n in ("sosq_done", "sored_done", "sostd_done", "son_done", "ot_full"))
        rg_out = sem("rg_out")
        y_out = [sem("y_out0"), sem("y_out1")]
        dve_step, act_step = sem("dve_step"), sem("act_step")

        ATT_STEPS = 25
        SAMPLE_STEP = (5, 17)

        block = ctx.enter_context(nc.Block())

        def col(c, n=None):
            return COL[:, c:c + 1] if n is None else COL[:, bass.ds(n + c, 1)]

        def as_acc(line):
            return line.rearrange("p (c t) -> p c t", c=NCH)

        def acc(a):
            s = a % 2
            return PS[:, 3 * s:3 * s + 3, 0:CH]

        def tile(region, k, i=None, m=1):
            if i is None:
                return region[:, k, :]
            return region[:, bass.ds(i * m + k, 1), :].rearrange("p a t -> p (a t)")

        def samples(line, hist):
            return line[:, hist + SEQ:hist + SEQ + NB * (hist + NS)].rearrange(
                "p (b s) -> p b s", b=NB)

        def val(base, i=None, m=0):
            return base if i is None else i * m + base

        def wait_acc(eng, a, i=None, m=0):
            eng.wait_ge(acc_done, val(a + 1, i, m))

        def wait_read(eng, a, i=None, m=0):
            eng.wait_ge(acc_free[a % 2], val(a // 2 + 1, i, m // 2))

        def wait_room(eng, a, i=None, m=0):
            if a >= 2:
                wait_read(eng, a - 2, i, m)

        class Steps:

            def __init__(self, eng, s):
                self.eng, self.s, self.n, self.i, self.per = eng, s, 0, None, 0

            def __call__(self, ins):
                ins.then_inc(self.s, 1)
                self.n += 1
                self.eng.wait_ge(self.s, val(self.n, self.i, self.per))

            def enter(self, i, per):
                self.start, self.i, self.per = self.n, i, per

            def leave(self, turns):
                assert self.n == self.start + self.per, (self.n - self.start, self.per)
                self.n = self.start + self.per * turns
                self.i = None

        @block.sync
        def _(sp):
            def load_weights(s, u):
                sp.dma_start(WRAW[:, s], I["w"][bass.ds(u, 1)].rearrange("u p k f -> p (u k) f")
                             ).then_inc(w_in[s], 16)

            def pairs(lo, hi):
                with sp.Fori(lo // 2, hi // 2) as i:
                    for s in range(2):
                        sp.wait_ge(w_lo, i * 2 + s - 1)
                        load_weights(s, i * 2 + s)

            sp.dma_start(COL[:, :], I["columns"]).then_inc(c_in, 16)
            load_weights(0, 0)
            load_weights(1, 1)
            pairs(2, U_O)

            def head(s, h):
                for dst, src in ((QRAW, QT), (KRAW, KTR)):
                    sp.dma_start(dst[s][:, :], src[:, bass.ds(h, 1), 0:SEQ].rearrange(
                        "p a t -> p (a t)")).then_inc(head_in[s], 16)

            def strip(s, h):
                line = S["line"][bass.ds(h, 1), P - 1:P - 1 + P * (LINE - 1)]
                sp.dma_start(BIAS[:, s], line.rearrange("h (p m) -> p (h m)", m=LINE - 1)[:, 0:SEQ]
                             ).then_inc(bias_in[s], 16)

            def pages(j, i=None):
                for g in range(NPG):
                    c = j * NPG + g
                    at_ = slice(c, c + 1) if i is None else bass.ds(i * (2 * NPG) + c, 1)
                    page = sp.value_load(PT[0:1, at_], min_val=0, max_val=NPOOL - 1)
                    sp.dma_start(KC[:, g], I["cache_k"][bass.ds(page, 1)].rearrange(
                        "n d h s -> d (n h) s")).then_inc(pg_in, 16)
                    sp.dma_start(VC[:, g], I["cache_v"][bass.ds(page, 1)].rearrange(
                        "n s h e -> s (n h) e")).then_inc(pg_in, 16)

            for s in range(2):
                sp.wait_ge(vt_out[s], 16 * (KT // 2))
            sp.wait_ge(vts_done, KT)
            wait_read(sp, A_Q)
            head(0, 0)
            wait_read(sp, A_Q + KT - 2)
            wait_read(sp, A_Q + KT - 1)
            sp.wait_ge(line_out, 16)
            strip(0, 0)
            sp.dma_start(PT[:, :], I["page_table"]).then_inc(pages_in, 16)
            head(1, 1)
            strip(1, 1)
            for r in range(2 * NS):
                off = REL0 - PAST - r % NS
                sp.dma_start(SBI[r * NH:(r + 1) * NH, :], S["line"][:, off:off + NKEY]
                             ).then_inc(sb_in, 16)
            sp.wait_ge(pages_in, 16)
            pages(0)
            with sp.Fori(0, NH // 2 - 1) as i:
                sp.wait_ge(so_done, i * 2 + 1)
                pages(1, i)
                for s in range(2):
                    sp.wait_ge(ttr_done, i * 32 + (2 + (s + 1) * 16))
                    head(s, i * 2 + (2 + s))
                    strip(s, i * 2 + (2 + s))
                sp.wait_ge(so_done, i * 2 + 2)
                pages(2, i)
            sp.wait_ge(so_done, NB - 1)
            pages(NB - 1)
            sp.wait_ge(so_read, NB)

            pairs(U_O, NU)
            for k in range(KT):
                sp.wait_ge(yt_done, k + 1)
                sp.dma_start(O["y"][:, k, :], Z[k % 2][:, 0:T]).then_inc(y_out[k % 2], 16)
            for s in range(2):
                sp.wait_ge(y_out[s], 16 * (KT // 2))
            sp.wait_ge(rg_out, 32)
            sp.wait_ge(k_out, 16)
            for s in range(2):
                sp.wait_ge(vt_out[s], 16 * (KT // 2))
                sp.wait_ge(FS[s]["tail_out"], 16)

        @block.gpsimd
        def _(pool):
            pool.memset(ONES[:, :], 1.0).then_inc(pool_const, 1)
            pool.memset(EPSC[:, :], EPS).then_inc(pool_const, 1)
            pool.memset(IDENT[:, :], 0.0).then_inc(pool_const, 1)
            pool.wait_ge(pool_const, 3)
            pool.affine_select(out=IDENT[:, :], in_=IDENT[:, :], compare_op=ALU.not_equal, fill=1.0,
                               base=0, pattern=[[-1, P]], channel_multiplier=1).then_inc(pool_const, 1)

            def split(u, used, i=None, m=0, stride=0):
                s = u % 2
                if used:
                    pool.wait_ge(acc_done, val(used, i, stride))
                pool.wait_ge(w_in[s], val(16 * (u // 2 + 1), i, 8 * m))
                pool.tensor_tensor(CARRY[:, 0:1], EPSC[:, :], EPSC[:, :], ALU.add)
                pool.tensor_scalar(WHI[:, s], WRAW[:, s], 1.0, 0.0, ALU.mult, ALU.add
                                   ).then_inc(w_hi, 1)
                pool.wait_ge(w_hi, val(u + 1, i, m))
                pool.tensor_tensor(WLO[:, s], WRAW[:, s], WHI[:, s].bitcast(F32), ALU.subtract
                                   ).then_inc(w_lo, 1)

            def straight(lo, hi):
                for u in range(lo, hi):
                    split(u, AFTER[u - 2] if u >= 2 else 0)

            def turns(u0, m, n):
                stride = AFTER[u0 + m] - AFTER[u0]
                used = [AFTER[u0 + j - 2] for j in range(m)]
                assert m % 2 == 0 and all(AFTER[u0 + j + i * m - 2] == used[j] + i * stride
                                          for i in range(n) for j in range(m))
                with pool.Fori(0, n) as i:
                    for j in range(m):
                        split(u0 + j, used[j], i, m, stride)

            def ffn(u0):
                n = (GROUPS - 2) // 2
                straight(u0, u0 + 6)
                turns(u0 + 6, 12, n - 1)
                straight(u0 + 6 + 12 * (n - 1), u0 + F_UNITS)

            straight(0, 6)
            turns(6, 6, KT // 2 - 1)
            straight(U_OUT, U_OUT + 2)
            turns(U_OUT + 2, 2, KT // 2 - 1)
            ffn(U_F0)
            straight(U_K, U_K + 2)
            turns(U_K + 2, 2, KT * 3 // 2 - 1)
            with pool.Fori(0, NH // 2) as hp:
                for s in range(2):
                    pool.wait_ge(head_in[s], hp * 32 + 32)
                    pool.tensor_tensor(CARRY[:, 0:1], EPSC[:, :], EPSC[:, :], ALU.add)
                    for raw, high in ((QRAW, QHI), (KRAW, KHI)):
                        pool.tensor_scalar(high[s][:, :], raw[s][:, :], 1.0, 0.0, ALU.mult, ALU.add
                                           ).then_inc(split_done, 1)
                    pool.wait_ge(split_done, hp * 8 + (4 * s + 2))
                    for raw, high, low in ((QRAW, QHI, QLO), (KRAW, KHI, KLO)):
                        pool.tensor_tensor(low[s][:, :], raw[s][:, :], high[s][:, :].bitcast(F32),
                                           ALU.subtract).then_inc(split_done, 1)
            straight(U_O, U_O + 2)
            turns(U_O + 2, 2, KT // 2 - 1)
            ffn(U_F1)

        @block.tensor
        def _(pe):
            def product(s, k, a, hi, lo, start, stop):
                for w, r, first, final in ((WHI, hi, True, False), (WLO, hi, False, False),
                                           (WHI, lo, False, True)):
                    for c in range(NCH):
                        last = pe.matmul(PS[:, 3 * (a % 2) + c, 0:CH], w[:, s, k, :],
                                         r[:, c * CH:(c + 1) * CH],
                                         start=start and first, stop=stop and final)
                return last

            def unit(u, a, i=None, m=0, stride=0, lows=None, release=False):
                pe.wait_ge(w_lo, val(u + 1, i, m))
                wait_room(pe, a, i, stride)
                for k in range(KT):
                    if lows is not None:
                        pe.wait_ge(nlo_done, lows + k + 1)
                    last = product(u % 2, k, a, XNH[:, k, :], XNL[:, k, :], k == 0, k == KT - 1)
                    if release and k < KT - 1:
                        last.then_inc(xn_free, 1)
                last.then_inc(acc_done, 1)

            def norm_sum(r, a):
                pe.wait_ge(sum_done, KT * (r + 1))
                if a is not None:
                    wait_room(pe, a)
                pe.matmul(PS[:, 3, 0:TS], ONES[:, :], Z[2][:, SEQ:T], start=True, stop=True
                          ).then_inc(sum_mm, 1)
                pe.matmul(PS[:, 6, :], ONES[:, :], Z[2][:, 0:512], start=True, stop=True)
                pe.matmul(PS[:, 7, :], ONES[:, :], Z[2][:, 512:SEQ], start=True, stop=True
                          ).then_inc(sum_mm, 1)
                pe.wait_ge(root_done, 2 * r + 1)

            def plain(u0, a0, lows, norm=None, release=False):
                unit(u0, a0, lows=lows)
                if norm is not None:
                    norm_sum(norm, a0 + 1)
                unit(u0 + 1, a0 + 1)
                with pe.Fori(0, KT // 2 - 2) as i:
                    for s in range(2):
                        unit(u0 + 2 + s, a0 + 2 + s, i, 2, 2)
                unit(u0 + KT - 2, a0 + KT - 2)
                unit(u0 + KT - 1, a0 + KT - 1, release=release)

            def bias_line():
                pe.wait_ge(tab_in, 32)
                pe.wait_ge(dve_const, 1)
                lw = LINE // NCH
                for c in range(NCH):
                    last = pe.matmul(PS[0:NH, 3 + c, 0:lw], TAB[:, :], HOT[:, c * lw:(c + 1) * lw],
                                     start=True, stop=True)
                last.then_inc(line_mm, 1)
                pe.wait_ge(line_read, 1)

            def rg(j, i=None, lows=None):
                u, a = U_RG + 3 * j, A_RG + 4 * j
                unit(u, a, i, 6, 8, lows)
                if lows is not None:
                    norm_sum(0, None)
                    bias_line()
                unit(u + 1, a + 1, i, 6, 8)
                pe.wait_ge(w_lo, val(u + 3, i, 6))
                pe.wait_ge(xcl_ready, val(j + 1, i, 2))
                for g in range(2):
                    wait_room(pe, a + 2 + g, i, 8)
                    product((u + 2) % 2, g, a + 2 + g, XCH[:, :], XCL[:, :], True, True
                            ).then_inc(acc_done, 1)

            pe.wait_ge(pool_const, 4)
            rg(0, lows=0)
            rg(1)
            with pe.Fori(0, KT // 2 - 1) as i:
                rg(2, i)
                rg(3, i)
            for j in range(2):
                pe.wait_ge(w_lo, U_OUT + j + 1)
                wait_room(pe, A_OUT + j)
                for k in range(KT - 1):
                    if j == 0:
                        pe.wait_ge(nlo_done, KT + k + 1)
                    product(j, k, A_OUT + j, XNH[:, k, :], XNL[:, k, :], k == 0, False)
            pe.wait_ge(nlo_done, 2 * KT)
            for j in range(2):
                k = KT - 1
                product(j, k, A_OUT + j, XNH[:, k, :], XNL[:, k, :], False, True).then_inc(acc_done, 1)
            with pe.Fori(0, KT // 2 - 2) as i:
                for s in range(2):
                    unit(U_OUT + 2 + s, A_OUT + 2 + s, i, 2, 2)
            unit(U_OUT + KT - 2, A_OUT + KT - 2)
            unit(U_OUT + KT - 1, A_OUT + KT - 1, release=True)

            def ffn(l, u0, a0, lows, norm):
                def up(u, a, i=None, lows=None):
                    for j in range(4):
                        unit(u + j, a + j, i, 12, 24, lows if j == 0 else None)
                        if lows is not None and j == 0:
                            norm_sum(norm, a + 1)

                def down(u, a, g, i=None):
                    pe.wait_ge(FS[l]["hl_ready"], val(2 * g + 2, i, 4))
                    for o in range(KT):
                        s = (u + o // 4) % 2
                        if o % 4 == 0:
                            pe.wait_ge(w_lo, val(u + o // 4 + 1, i, 12))
                        wait_room(pe, a + o, i, 24)
                        for t in range(2):
                            h = 2 * (g % 2) + t
                            last = product(s, 2 * (o % 4) + t, a + o, HHI[:, h, :], HLO[:, h, :],
                                           t == 0, t == 1)
                        last.then_inc(acc_done, 1)

                up(u0, a0, lows=lows)
                with pe.Fori(0, (GROUPS - 2) // 2) as i:
                    for g in range(2):
                        up(u0 + 4 + 6 * g, up_acc(a0, g + 1, 0), i)
                        down(u0 + 8 + 6 * g, down_acc(a0, g, 0), g, i)
                g = GROUPS - 1
                u = u0 + 4 + 6 * (g - 1)
                up(u, up_acc(a0, g, 0))
                down(u + 4, down_acc(a0, g - 1, 0), g - 1)
                down(u + 6, down_acc(a0, g, 0), g)

            ffn(0, U_F0, A_F0, 2 * KT, 1)

            plain(U_K, A_K, 3 * KT, norm=2)

            def v_back(j, i=None):
                wait_read(pe, A_V + j, i, 2)
                for b in range(KT):
                    if b % 4 == 0:
                        pe.wait_ge(vtr_read, val(2 * j + b // 4 + 1, i, 4))
                    last = pe.transpose(PS[:, 6 + b // 4, (b % 4) * P:(b % 4 + 1) * P],
                                        Z[j % 2][:, b * P:(b + 1) * P], IDENT[:, :])
                    if b % 4 == 3:
                        last.then_inc(vtr_done, 1)

            unit(U_V, A_V)
            with pe.Fori(0, KT // 2 - 1) as i:
                for s in range(2):
                    unit(U_V + 1 + s, A_V + 1 + s, i, 2, 2)
                    v_back(s, i)
            unit(U_V + KT - 1, A_V + KT - 1, release=True)
            v_back(KT - 2)
            v_back(KT - 1)
            pe.wait_ge(vts_done, KT)
            pe.wait_ge(vtr_read, 2 * KT + 2)
            for h in range(NH):
                last = pe.transpose(PS[0:TS, 6 + h // 4, (h % 4) * P:(h % 4 + 1) * P],
                                    VTS[:, h, :], IDENT[:, :])
            last.then_inc(vtr_done, 1)
            plain(U_Q, A_Q, 4 * KT)

            wait_read(pe, A_Q + KT - 2)
            wait_read(pe, A_Q + KT - 1)
            pe.wait_ge(vtr_read, 2 * KT + 3)

            def sample_scores(j, hp):
                pe.wait_ge(pg_in, hp * 128 + 64 * (j + 1))
                pe.wait_ge(qp_done, hp * 2 + (j + 1))
                pe.wait_ge(ot_read, hp * 4 + (1 + 2 * j))
                for h in range(NH):
                    pe.matmul(PS[0:SROWS, 7, 0:PAST], QP[:, h * SROWS:(h + 1) * SROWS],
                              KC[:, :, h, :], start=(h == 0), stop=(h == NH - 1))
                for h in range(NH):
                    last = pe.matmul(PS[0:SROWS, 7, PAST:PAST + TS],
                                     QP[:, h * SROWS:(h + 1) * SROWS], KTR[:, h, SEQ:T],
                                     start=(h == 0), stop=(h == NH - 1))
                last.then_inc(ss_done, 1)

            def sample_transposes(j, hp):
                pe.wait_ge(spn_done, hp * 2 + (j + 1))
                for g in range(NPG):
                    pe.transpose(PS[:, 7, g * P:(g + 1) * P], SPR[:, g * P:(g + 1) * P],
                                 IDENT[:, :])
                pe.transpose(PS[0:TS, 7, NPG * P:(NPG + 1) * P], SPR[:, PAST:PAST + TS],
                             IDENT[:, :]).then_inc(st_done, 1)

            def sample_outputs(j, hp):
                pe.wait_ge(sw_done, hp * 2 + (j + 1))
                for h in range(NH):
                    q = h * NS
                    for g in range(NPG):
                        pe.matmul(PS[:, 7, q:q + NS], VC[:, g, h, :], SW[:, g, h:NS * NH:NH],
                                  start=(g == 0), stop=False)
                    last = pe.matmul(PS[:, 7, q:q + NS], VS[:, h, :], SWN[:, h:NS * NH:NH],
                                     start=False, stop=True)
                last.then_inc(so_done, 1)

            with pe.Fori(0, NH // 2) as hp:
                for t in range(ATT_STEPS):
                    if t < 16:
                        s, i = t // 8, t % 8
                        n = (i + 1) * P
                        if i == 0:
                            pe.wait_ge(split_done, hp * 8 + 4 * (s + 1))
                        for c in range(2):
                            pe.wait_ge(ttr_done, hp * 32 + (2 * t + c + 1))
                            rows = slice(c * HD, (c + 1) * HD)
                            for b in range(0, n, 512):
                                w = min(512, n - b)
                                for p, (q, k) in enumerate(((QHI, KHI), (QLO, KHI), (QHI, KLO))):
                                    last = pe.matmul(PS[:, 2 * c + b // 512, 0:w],
                                                     q[s][rows, i * P:(i + 1) * P],
                                                     k[s][rows, b:b + w],
                                                     start=(p == 0), stop=(p == 2))
                            last.then_inc(s_done, 1)
                    if 2 <= t < 18:
                        v = t - 2
                        pe.wait_ge(wc_done, hp * 16 + (v + 1))
                        pe.wait_ge(wt_read, hp * 16 + (v + 1))
                        for b in range(v % 8 + 1):
                            last = pe.transpose(PS[:, 4 + b // 4, (b % 4) * P:(b % 4 + 1) * P],
                                                PR[:, v % 3, 0, b * P:(b + 1) * P], IDENT[:, :])
                        last.then_inc(wt_done, 1)
                    if 3 <= t < 19:
                        v = t - 3
                        s, i = v // 8, v % 8
                        pe.wait_ge(wt_read, hp * 16 + (v + 2))
                        pe.wait_ge(o_read, hp * 16 + (v + 1))
                        for b in range(i + 1):
                            last = pe.matmul(PS[:, 6, 0:P], WTS[:, v % 2, b * P:(b + 1) * P],
                                             V[:, bass.ds(hp * 2 + s, 1), b, :
                                               ].rearrange("p a e -> p (a e)"),
                                             start=(b == 0), stop=(b == i))
                        last.then_inc(pv_done, 1)
                    for s in range(2):
                        if t == SAMPLE_STEP[s]:
                            sample_scores(s, hp)
                        if t == SAMPLE_STEP[s] + 2:
                            sample_transposes(s, hp)
                        if t == SAMPLE_STEP[s] + 4:
                            sample_outputs(s, hp)
                        for half in range(2):
                            if t == 14 + 8 * s + 2 * half:
                                pe.wait_ge(on_done, hp * 2 + (s + 1))
                                pe.wait_ge(ot_read, hp * 4 + (2 * s + half + 1))
                                if half == 0:
                                    pe.wait_ge(so_read, hp * 2 + (s + 1))
                                for b in range(4):
                                    last = pe.transpose(PS[:, 7, b * P:(b + 1) * P],
                                                        OQ[:, s, 4 * half + b, :], IDENT[:, :])
                                last.then_inc(ot_done, 1)

            pe.wait_ge(sosq_done, 1)
            pe.matmul(PS[:, 1, 0:NH * TS], ONES[:, :], OSQ[:, :, :].rearrange("p h t -> p (h t)"),
                      start=True, stop=True).then_inc(sored_done, 1)
            pe.wait_ge(sostd_done, 1)

            plain(U_O, A_O, 5 * KT, release=True)
            ffn(1, U_F1, A_F1, 6 * KT, 3)
            wait_read(pe, A_F1 + F_ACCS - 1)
            norm_sum(4, None)

        @block.scalar
        def _(act):
            step = Steps(act, act_step)

            def square(r, k):
                if k >= 2:
                    act.wait_ge(sum_done, KT * r + k - 1)
                act.activation(Z[k % 2][:, 0:T], X[:, k, :], ACT.Square).then_inc(sq_done, 1)

            def high(gain, k):
                act.activation(XNH[:, k, :], X[:, k, :], ACT.Copy, scale=col(gain + k)
                               ).then_inc(nhi_done, 1)

            def root(r):
                act.wait_ge(sum_mm, 2 * r + 1)
                act.activation(RINV[:, SEQ:T], PS[:, 3, 0:TS], ACT.Sqrt, bias=EPSC[:, :],
                               scale=1.0 / D).then_inc(root_done, 1)
                act.wait_ge(sum_mm, 2 * r + 2)
                act.activation(RINV[:, 0:SEQ].rearrange("p (b t) -> p b t", b=2), PS[:, 6:8, :],
                               ACT.Sqrt, bias=EPSC[:, :], scale=1.0 / D).then_inc(root_done, 1)

            def norm_after_units(r, a0, gain, released):
                for k in range(KT - 1):
                    wait_read(act, a0 + k)
                    square(r, k)
                for k in range(KT - 1):
                    act.wait_ge(xn_free, released + k + 1)
                    high(gain, k)
                wait_read(act, a0 + KT - 1)
                high(gain, KT - 1)
                square(r, KT - 1)
                root(r)

            for k in range(KT):
                act.dma_start(X[:, k, :], I["x"][:, k, :]).then_inc(x_in[k], 16)
            act.dma_start(TAB[0:BUCKETS, :], I["rel_bias"]).then_inc(tab_in, 16)
            act.dma_start(HOT[:, :], I["one_hot"]).then_inc(tab_in, 16)
            act.dma_start(LAMV[:, :, :], I["lam"]).then_inc(lam_in, 16)
            act.dma_start(RST[:, :, :, :], I["rg_conv_state"]).then_inc(rst_in, 16)
            act.dma_start(H0[:, :, :], I["rg_h_state"]).then_inc(rst_in, 16)
            act.dma_start(FST[:, :, :, :], I["ffn_state"][0]).then_inc(fst_in, 16)

            act.wait_ge(c_in, 16)
            step(act.activation(SPT[:, 0], COL[:, C_LAM:C_LAM + KT], ACT.Abs))
            act.activation(SPT[:, 1], SPT[:, 0], ACT.Exp, scale=-1.0).then_inc(act_const, 1)
            act.wait_ge(dve_const, 4)
            act.activation(NLAM[:, 0:2], NLAM[:, 0:2], ACT.Exp).then_inc(act_const, 1)
            act.wait_ge(pool_const, 4)
            for n, q in enumerate((wt_read, ot_read)):
                act.activation(CARRY[:, 9 + n:10 + n], EPSC[:, :], ACT.Copy).then_inc(q, 1)

            def bias_line():
                act.wait_ge(line_mm, 1)
                lw = LINE // NCH
                act.activation(BLN[:, :].rearrange("h (c n) -> h c n", c=NCH), PS[0:NH, 3:6, 0:lw],
                               ACT.Copy).then_inc(line_read, 1)
                act.wait_ge(line_read, 1)
                act.dma_start(S["line"].rearrange("h (p i) -> h p i", p=P),
                              BLN[:, :].unsqueeze(1).to_broadcast([NH, P, LINE])
                              ).then_inc(line_out, 16)

            for k in range(KT):
                act.wait_ge(x_in[k], 16)
                high(C_GMIX0, k)
                square(0, k)
            root(0)
            bias_line()
            act.wait_ge(rst_in, 32)
            act.wait_ge(scal_done, 1)
            with act.Fori(0, KT) as n:
                act.wait_ge(rec_used, n + 1)
                act.activation(samples(Z[4], RW - 1)[:, :, 0:RW - 1],
                               RST[:, bass.ds(n, 1)].rearrange("p a b s -> p (a b) s"), ACT.Copy
                               ).then_inc(rec_state, 1)
                act.wait_ge(xc_ready, n + 1)
                act.activation(XCH[:, :], Z[0][:, 0:T], ACT.Copy).then_inc(xch_ready, 1)
                wait_read(act, A_RG + 1, n, 4)
                act.activation(Z[5][:, 0:T], Z[5][:, 0:T], ACT.Gelu_apprx_tanh
                               ).then_inc(gel_ready, 1)
                wait_acc(act, A_RG + 2, n, 4)
                act.activation(as_acc(Z[6][:, 0:T]), acc(A_RG + 2), ACT.Tanh, scale=0.5,
                               bias=HBA[:, bass.ds(n, 1)]).then_inc(acc_free[(A_RG + 2) % 2], 1)
                act.wait_ge(y_done, n + 1)
                wait_read(act, A_RG + 2, n, 4)
                act.activation(Z[2][:, 0:T], Z[6][:, 0:T], ACT.Tanh, scale=SP2[:, bass.ds(n, 1)],
                               bias=SP2[:, bass.ds(n, 1)]).then_inc(s_ready, 1)
                wait_acc(act, A_RG + 3, n, 4)
                act.activation(as_acc(Z[1][:, 0:T]), acc(A_RG + 3), ACT.Tanh, scale=0.5,
                               bias=HBX[:, bass.ds(n, 1)]).then_inc(acc_free[(A_RG + 3) % 2], 1)
                act.activation(Z[3][:, 0:T], Z[6][:, 0:T], ACT.Exp, scale=SPM[:, bass.ds(n, 1)],
                               bias=SPM[:, bass.ds(n, 1)])
                act.wait_ge(s_ready, n + 1)
                act.activation(Z[2][:, 0:T], Z[2][:, 0:T], ACT.Sqrt).then_inc(sqrt_ready, 1)
            wait_acc(act, A_OUT - 3)
            for k in range(KT):
                act.wait_ge(y_done, k + 2)
                act.activation(XNH[:, k, :], Y[:, k, :], ACT.Copy).then_inc(nhi_done, 1)
            act.dma_start(O["rg_conv"], RTAIL[:, :, :, :]).then_inc(rg_out, 16)
            act.dma_start(O["rg_h"], HTAIL[:, :, :]).then_inc(rg_out, 16)

            def ffn(l, a0):
                q = FS[l]

                def up(g, i=None):
                    for t in range(2):
                        f = 2 * g + t
                        for v in range(2):
                            n = 2 * f + v
                            if n >= 2:
                                act.wait_ge(q["u_used"], val(n - 1, i, 8))
                            src = (FST[:, v * FT + f] if i is None else
                                   FST[:, bass.ds(i * 4 + (v * FT + f), 1)].rearrange(
                                       "p a b s -> p (a b) s"))
                            act.activation(samples(Z[4 + v], FW - 1)[:, :, 0:FW - 1], src, ACT.Copy
                                           ).then_inc(q["u_state"], 1)
                        act.wait_ge(q["gc_ready"], val(f + 1, i, 4))
                        act.activation(Z[1][:, 0:T], Z[1][:, 0:T], ACT.Gelu_apprx_tanh
                                       ).then_inc(q["gg_ready"], 1)
                        act.wait_ge(q["hf_ready"], val(f + 1, i, 4))
                        if g >= 2:
                            wait_acc(act, down_acc(a0, g - 2, KT - 1), i, 24)
                        act.activation(HHI[:, f % 4, :], Z[2][:, 0:T], ACT.Copy
                                       ).then_inc(q["hh_ready"], 1)

                for g in range(3):
                    up(g)
                with act.Fori(0, (GROUPS - 4) // 2) as i:
                    for g in (3, 4):
                        up(g, i)
                up(GROUPS - 1)
                act.wait_ge(q["u_used"], 4 * GROUPS)
                act.dma_start(O["ffn_conv"][l], FTAIL[:, :, :, :]).then_inc(q["tail_out"], 16)

            norm_after_units(1, A_OUT, C_GFFN0, 0)
            act.wait_ge(fst_in, 16)
            ffn(0, A_F0)

            for k in range(KT):
                wait_read(act, down_acc(A_F0, GROUPS - 1, k))
                high(C_GKV, k)
            for k in range(KT):
                square(2, k)
            root(2)
            act.dma_start(S["x"], X[:, :, :]).then_inc(x_out, 16)
            wait_read(act, A_K + KT - 2)
            wait_read(act, A_K + KT - 1)
            act.dma_start(O["k"], KTR[:, :, :]).then_inc(k_out, 16)

            def v_out(j, i=None):
                wait_read(act, A_V + j, i, 2)
                act.activation(VTS[:, j, :] if i is None else
                               VTS[:, bass.ds(i * 2 + j, 1), :].rearrange("p a t -> p (a t)"),
                               Z[j % 2][:, SEQ:T], ACT.Copy).then_inc(vts_done, 1)
                dst = (O["v"][:, j, :] if i is None else
                       O["v"][:, bass.ds(i * 2 + j, 1), :].rearrange("p a t -> p (a t)"))
                act.dma_start(dst, Z[j % 2][:, 0:T]).then_inc(vt_out[j % 2], 16)

            act.wait_ge(FS[0]["tail_out"], 16)
            with act.Fori(0, KT // 2 - 1) as i:
                for j in range(2):
                    v_out(j, i)
            v_out(KT - 2)
            for k in range(KT):
                if k < KT - 1:
                    act.wait_ge(xn_free, KT - 1 + k + 1)
                else:
                    wait_acc(act, A_V + KT - 1)
                high(C_GMIX1, k)
            v_out(KT - 1)

            act.wait_ge(k_out, 16)
            with act.Fori(0, NH // 2) as hp:
                for t in range(ATT_STEPS):
                    if t < 16:
                        s, i = t // 8, t % 8
                        for c in range(2):
                            act.wait_ge(nm_ready, hp * 32 + (2 * t + c + 1))
                            pr = PR[:, t % 3, c, 0:(i + 1) * P]
                            act.activation(pr, pr, ACT.Exp, bias=MX[:, t % 3, 2 + c:3 + c],
                                           accum_out=SSUM[:, s, c, i:i + 1]).then_inc(e_done, 1)
                    if 2 <= t < 18:
                        v = t - 2
                        n = v % 8 + 1
                        act.wait_ge(wt_done, hp * 16 + (v + 1))
                        if v >= 2:
                            act.wait_ge(pv_done, hp * 16 + (v - 1))
                        if n <= 4:
                            act.activation(WTS[:, v % 2, 0:n * P], PS[:, 4, 0:n * P], ACT.Copy
                                           ).then_inc(wt_read, 1)
                        else:
                            act.activation(WTS[:, v % 2, 0:512], PS[:, 4, :], ACT.Copy)
                            act.activation(WTS[:, v % 2, 512:n * P], PS[:, 5, 0:n * P - 512],
                                           ACT.Copy).then_inc(wt_read, 1)
                    for s in range(2):
                        if t == SAMPLE_STEP[s] + 1:
                            act.wait_ge(snm_done, hp * 2 + (s + 1))
                            act.activation(SPR[0:SROWS, :], SPR[0:SROWS, :], ACT.Exp, bias=SST[:, 1:2],
                                           accum_out=SST[:, 2:3]).then_inc(sexp_done, 1)
                        if t == SAMPLE_STEP[s] + 3:
                            act.wait_ge(st_done, hp * 2 + (s + 1))
                            act.activation(SC1[:, :, :], PS[:, 7, 0:NPG * P].rearrange(
                                "p (g r) -> p g r", g=NPG)[:, :, NS * NH:SROWS], ACT.Copy)
                            act.activation(SCN[:, :], PS[0:TS, 7, NPG * P + NS * NH:
                                                         NPG * P + SROWS], ACT.Copy
                                           ).then_inc(sc1_done, 1)
                        if t == 11 + 8 * s:
                            act.wait_ge(o_read, hp * 16 + (8 * (s + 1) + 1))
                            act.activation(OQS[:, :, :], OQ[:, s, :, :], ACT.Square
                                           ).then_inc(osq_done, 1)
                        if t == 12 + 8 * s:
                            act.wait_ge(var_done, hp * 2 + (s + 1))
                            act.activation(SM[:, 2], SM[:, 1], ACT.Sqrt, scale=1.0 / P
                                           ).then_inc(std_done, 1)
                        for half in range(2):
                            if t == 14 + 8 * s + 2 * half:
                                act.wait_ge(ot_done, hp * 4 + (2 * s + half + 1))
                                act.activation(
                                    OT[:, bass.ds(hp * 2 + s, 1), half * 512:(half + 1) * 512
                                       ].rearrange("p a t -> p (a t)"),
                                    PS[:, 7, :], ACT.Copy, scale=SUBG[:, :]).then_inc(ot_read, 1)

            act.wait_ge(so_read, NB)
            act.activation(OSQ[:, :, :], OSM[:, :, :], ACT.Square).then_inc(sosq_done, 1)
            act.wait_ge(sored_done, 1)
            act.activation(OSQ[:, :, :].rearrange("p h t -> p (h t)"), PS[:, 1, 0:NH * TS], ACT.Sqrt,
                           scale=1.0 / P, bias=EPSC[:, :]).then_inc(sostd_done, 1)
            act.wait_ge(son_done, 1)
            act.activation(OT[:, :, SEQ:T], OSM[:, :, :], ACT.Copy, scale=SUBG[:, :]
                           ).then_inc(ot_full, 1)
            act.wait_ge(ot_full, 1)
            act.dma_start(X[:, :, :], S["x"]).then_inc(x_back, 16)
            act.dma_start(FST[:, :, :, :], I["ffn_state"][1]).then_inc(fst_in, 16)
            for k in range(KT):
                act.activation(XNH[:, k, :], OT[:, k, :], ACT.Copy).then_inc(nhi_done, 1)

            norm_after_units(3, A_O, C_GFFN1, 2 * (KT - 1))
            act.wait_ge(fst_in, 32)
            ffn(1, A_F1)
            for k in range(KT):
                wait_read(act, down_acc(A_F1, GROUPS - 1, k))
                square(4, k)
            root(4)

        @block.vector
        def _(dve):
            step = Steps(dve, dve_step)
            MUL, ADD, SUB = ALU.mult, ALU.add, ALU.subtract

            def conv_first(src, tmp, taps, bias, hist):
                n = SEQ + NB * (hist + NS)
                step(dve.tensor_scalar(tmp[:, 0:n], src[:, 0:n], taps[0], bias, MUL, ADD))
                for j in range(1, hist):
                    step(dve.scalar_tensor_tensor(tmp[:, 0:n], src[:, j:j + n], taps[j],
                                                  tmp[:, 0:n], MUL, ADD))

            def conv_last(src, tmp, dst, taps, hist, signal):
                dve.scalar_tensor_tensor(dst[:, 0:SEQ], src[:, hist:hist + SEQ], taps[hist],
                                         tmp[:, 0:SEQ], MUL, ADD)
                dve.scalar_tensor_tensor(dst[:, SEQ:T].rearrange("p (b s) -> p b s", b=NB),
                                         samples(src, hist)[:, :, hist:hist + NS], taps[hist],
                                         samples(tmp, hist)[:, :, 0:NS], MUL, ADD
                                         ).then_inc(signal, 1)

            def evac_line(a, line, hist, i=None, m=0):
                wait_acc(dve, a, i, m)
                b = 3 * (a % 2)
                c2, left = 2 * CH, SEQ - 2 * CH
                dve.tensor_tensor(line[:, hist:hist + c2].rearrange("p (c t) -> p c t", c=2),
                                  PS[:, b:b + 2, 0:CH],
                                  RINV[:, 0:c2].rearrange("p (c t) -> p c t", c=2), MUL)
                dve.tensor_tensor(line[:, hist + c2:hist + SEQ], PS[:, b + 2, 0:left],
                                  RINV[:, c2:SEQ], MUL)
                dve.tensor_tensor(samples(line, hist)[:, :, hist:hist + NS],
                                  PS[:, b + 2, left:CH].rearrange("p (b s) -> p b s", b=NB),
                                  RINV[:, SEQ:T].rearrange("p (b s) -> p b s", b=NB), MUL
                                  ).then_inc(acc_free[a % 2], 1)

            def evac(a, line, i=None, m=0):
                wait_acc(dve, a, i, m)
                dve.tensor_tensor(as_acc(line), acc(a), as_acc(RINV[:, :]), MUL
                                  ).then_inc(acc_free[a % 2], 1)

            def add_square(r, k):
                dve.wait_ge(sq_done, KT * r + k + 1)
                if k == 0:
                    dve.tensor_copy(Z[2][:, 0:T], Z[0][:, 0:T]).then_inc(sum_done, 1)
                else:
                    dve.wait_ge(sum_done, KT * r + k)
                    dve.tensor_tensor(Z[2][:, 0:T], Z[2][:, 0:T], Z[k % 2][:, 0:T], ADD
                                      ).then_inc(sum_done, 1)

            def low(m, gain, k):
                dve.wait_ge(nhi_done, KT * m + k + 1)
                dve.scalar_tensor_tensor(XNL[:, k, :], X[:, k, :], col(gain + k),
                                         XNH[:, k, :].bitcast(F32), MUL, SUB).then_inc(nlo_done, 1)

            def inverse(r):
                dve.wait_ge(root_done, 2 * r + 2)
                step(dve.reciprocal(RINV[:, :], RINV[:, :]))

            def lows(m, region):
                for k in range(KT):
                    dve.wait_ge(nhi_done, KT * m + k + 1)
                    dve.tensor_tensor(XNL[:, k, :], region[:, k, :], XNH[:, k, :].bitcast(F32), SUB
                                      ).then_inc(nlo_done, 1)

            def add_to_x(a, k, i=None, m=0, tm=0):
                wait_acc(dve, a, i, m)
                x = X[:, k, :] if not tm else tile(X, k, i, tm)
                dve.tensor_tensor(as_acc(x), acc(a), as_acc(x), ADD).then_inc(acc_free[a % 2], 1)

            dve.memset(TAB[BUCKETS:BUCKETS + 1, :], NEG).then_inc(dve_const, 1)
            dve.memset(Z[4][:, 0:RW - 1], 0.0).then_inc(rec_used, 1)
            dve.memset(Z[5][:, 0:FW - 1], 0.0).then_inc(y_done, 1)
            dve.memset(CROW[:, :], 1.0).then_inc(dve_const, 1)
            for j, q in enumerate((ttr_done, ttr_done, o_read, vtr_read, vtr_read)):
                dve.memset(CARRY[:, 3 + j:4 + j], 0.0).then_inc(q, 1)
            dve.wait_ge(lam_in, 16)
            for j in range(2):
                dve.tensor_tensor_reduce(LAMP[:, j], LAMV[:, 2 * j, :], LAMV[:, 2 * j + 1, :], 1.0,
                                         0.0, MUL, ADD, NLAM[:, j:j + 1]).then_inc(dve_const, 1)
            dve.wait_ge(c_in, 16)
            dve.tensor_scalar(HBA[:, :], COL[:, C_BA:C_BA + KT], 0.5, None, MUL)
            dve.tensor_scalar(HBX[:, :], COL[:, C_BX:C_BX + KT], 0.5, None, MUL)
            dve.tensor_scalar(SUBG[:, :], col(C_SUB), 1.0 - LAM_INIT, None, MUL)
            dve.wait_ge(act_const, 1)
            E, TT, W2, PP = SPT[:, 1], SPT[:, 2], SPT[:, 3], SPT[:, 0]
            step(dve.tensor_scalar(TT, E, 2.0, None, ADD))
            step(dve.reciprocal(TT, TT))
            step(dve.tensor_tensor(TT, TT, E, MUL))
            step(dve.tensor_tensor(W2, TT, TT, MUL))
            step(dve.tensor_scalar(PP, W2, 1.0 / 17, None, MUL))
            for d in (15, 13, 11, 9, 7, 5, 3):
                step(dve.scalar_tensor_tensor(PP, PP, 1.0 / d, W2, ADD, MUL))
            step(dve.scalar_tensor_tensor(PP, PP, 1.0, TT, ADD, MUL))
            step(dve.tensor_scalar(W2, COL[:, C_LAM:C_LAM + KT], -2.0, 0.0, MUL, ALU.max))
            step(dve.scalar_tensor_tensor(SP2[:, :], PP, 4.0, W2, MUL, ADD))
            dve.tensor_scalar(SPM[:, :], SP2[:, :], -2.0, None, MUL).then_inc(scal_done, 1)
            dve.wait_ge(act_const, 2)
            step(dve.tensor_tensor(NLAM[:, 2:3], NLAM[:, 1:2], NLAM[:, 0:1], SUB))
            step(dve.tensor_scalar(NLAM[:, 3:4], NLAM[:, 2:3], LAM_INIT, None, SUB))
            step(dve.tensor_copy(CROW[NS * NH:SROWS, :], NLAM[NS * NH:SROWS, 3:4]))

            for k in range(KT):
                low(0, C_GMIX0, k)
                add_square(0, k)
            inverse(0)
            dve.wait_ge(line_out, 16)
            dve.wait_ge(rst_in, 32)
            with dve.Fori(0, KT) as n:
                step.enter(n, 10)
                dve.wait_ge(y_done, n + 1)
                REC, XC, TI, SQ, A_, S_, G_ = Z[4], Z[0], Z[1], Z[2], Z[3], Z[6], Z[5]
                evac_line(A_RG, REC, RW - 1, n, 4)
                dve.wait_ge(rec_state, n + 1)
                wait_read(dve, A_RG, n, 4)
                taps = [col(C_RGW + j * KT, n) for j in range(RW)]
                conv_first(REC, S_, taps, col(C_RGB, n), RW - 1)
                conv_last(REC, S_, XC, taps, RW - 1, xc_ready)
                dve.tensor_copy(RTAIL[:, bass.ds(n, 1), 0, :].rearrange("p a s -> p (a s)"),
                                REC[:, SEQ:SEQ + RW - 1])
                dve.tensor_copy(RTAIL[:, bass.ds(n, 1), 1:NB + 1, :].rearrange("p a b s -> p (a b) s"),
                                samples(REC, RW - 1)[:, :, NS:NS + RW - 1]).then_inc(rec_used, 1)
                dve.wait_ge(xch_ready, n + 1)
                dve.wait_ge(xc_ready, n + 1)
                dve.tensor_tensor(XCL[:, :], XC[:, 0:T], XCH[:, :].bitcast(F32), SUB
                                  ).then_inc(xcl_ready, 1)
                evac(A_RG + 1, G_[:, 0:T], n, 4)
                wait_read(dve, A_RG + 3, n, 4)
                step(dve.scalar_tensor_tensor(TI[:, 0:T], TI[:, 0:T], 1.0, XC[:, 0:T], ADD, MUL))
                dve.wait_ge(sqrt_ready, n + 1)
                step(dve.scalar_tensor_tensor(SQ[:, 0:T], A_[:, 0:T], 1.0, SQ[:, 0:T], ADD, MUL))
                step(dve.scalar_tensor_tensor(SQ[:, 0:T], SQ[:, 0:T], 0.5, TI[:, 0:T], MUL, MUL))
                dve.tensor_scalar(SQ[:, 0:1], TI[:, 0:1], 0.5, None, MUL)
                first = A_[:, SEQ:T:NS]
                step(dve.tensor_tensor(T8[:, :], first,
                                       H0[:, bass.ds(n, 1), :].rearrange("p a b -> p (a b)"), MUL))
                step(dve.tensor_tensor(SQ[:, SEQ:T:NS], SQ[:, SEQ:T:NS], T8[:, :], ADD))
                dve.memset(A_[:, 0:1], 0.0)
                step(dve.memset(first, 0.0))
                step(dve.tensor_tensor_scan(S_[:, 0:T], A_[:, 0:T], SQ[:, 0:T], 0.0, MUL, ADD))
                dve.tensor_copy(HTAIL[:, bass.ds(n, 1), 0:1].rearrange("p a b -> p (a b)"),
                                S_[:, SEQ - 1:SEQ])
                dve.tensor_copy(HTAIL[:, bass.ds(n, 1), 1:NB + 1].rearrange("p a b -> p (a b)"),
                                S_[:, SEQ + NS - 1:T:NS])
                dve.wait_ge(gel_ready, n + 1)
                dve.tensor_tensor(tile(Y, 0, n), S_[:, 0:T], Z[5][:, 0:T], MUL).then_inc(y_done, 1)
                step.leave(KT)
            lows(1, Y)

            def norm_after_units(r, a0, m, gain):
                for k in range(KT - 1):
                    add_to_x(a0 + k, k)
                    add_square(r, k)
                for k in range(KT - 1):
                    low(m, gain, k)
                add_to_x(a0 + KT - 1, KT - 1)
                low(m, gain, KT - 1)
                add_square(r, KT - 1)
                inverse(r)

            norm_after_units(1, A_OUT, 2, C_GFFN0)

            def ffn(l, a0):
                q = FS[l]

                def taps(g, t, v, i):
                    c = C_FW + l * NFC + v * FT + 2 * g + t
                    return [col(c + j * 2 * FT, None if i is None else i * 4) for j in range(FW + 1)]

                def arrived(g, t, v, i):
                    n = 2 * (2 * g + t) + v
                    if n >= 2:
                        dve.wait_ge(q["u_used"], val(n - 1, i, 8))
                    a = up_acc(a0, g, 2 * t + v)
                    evac_line(a, Z[4 + v], FW - 1, i, 24)
                    dve.wait_ge(q["u_state"], val(n + 1, i, 8))
                    wait_read(dve, a, i, 24)
                    f = 2 * g + t
                    if v:
                        dve.wait_ge(q["vc_ready"], val(f + 1, i, 4))
                    elif f:
                        dve.wait_ge(q["hf_ready"], val(f, i, 4))

                def tails(g, t, v, i):
                    c = v * FT + 2 * g + t
                    at_ = slice(c, c + 1) if i is None else bass.ds(i * 4 + c, 1)
                    src = Z[4 + v]
                    dve.tensor_copy(FTAIL[:, at_, 0, :].rearrange("p a s -> p (a s)"),
                                    src[:, SEQ:SEQ + FW - 1])
                    dve.tensor_copy(FTAIL[:, at_, 1:NB + 1, :].rearrange("p a b s -> p (a b) s"),
                                    samples(src, FW - 1)[:, :, NS:NS + FW - 1]
                                    ).then_inc(q["u_used"], 1)

                def convolved(g, t, v, i):
                    arrived(g, t, v, i)
                    w = taps(g, t, v, i)
                    conv_first(Z[4 + v], Z[6], w, w[FW], FW - 1)
                    conv_last(Z[4 + v], Z[6], Z[v], w, FW - 1, q["gc_ready" if v else "vc_ready"])
                    tails(g, t, v, i)

                def gated(f, i):
                    dve.wait_ge(q["vc_ready"], val(f + 1, i, 4))
                    if f:
                        dve.wait_ge(q["hl_ready"], val(f, i, 4))
                    dve.wait_ge(q["gg_ready"], val(f + 1, i, 4))
                    dve.tensor_tensor(Z[2][:, 0:T], Z[0][:, 0:T], Z[1][:, 0:T], MUL
                                      ).then_inc(q["hf_ready"], 1)

                def low_h(f, i):
                    dve.wait_ge(q["hh_ready"], val(f + 1, i, 4))
                    dve.wait_ge(q["hf_ready"], val(f + 1, i, 4))
                    dve.tensor_tensor(HLO[:, f % 4, :], Z[2][:, 0:T], HHI[:, f % 4, :].bitcast(F32),
                                      SUB).then_inc(q["hl_ready"], 1)

                def group(g, i=None):
                    f = 2 * g

                    def outs(lo, hi):
                        if g:
                            for o in range(lo, hi):
                                add_to_x(down_acc(a0, g - 1, o), o, i, 24)

                    convolved(g, 0, 0, i)
                    convolved(g, 0, 1, i)
                    gated(f, i)
                    low_h(f, i)
                    convolved(g, 1, 0, i)
                    arrived(g, 1, 1, i)
                    w = taps(g, 1, 1, i)
                    conv_first(Z[5], Z[6], w, w[FW], FW - 1)
                    outs(0, 1)
                    conv_last(Z[5], Z[6], Z[1], w, FW - 1, q["gc_ready"])
                    tails(g, 1, 1, i)
                    outs(1, 3)
                    gated(f + 1, i)
                    outs(3, 4)
                    low_h(f + 1, i)
                    outs(4, KT)

                step(dve.memset(Z[4][:, 0:FW - 1], 0.0))
                step(dve.memset(Z[5][:, 0:FW - 1], 0.0))
                group(0)
                with dve.Fori(0, (GROUPS - 2) // 2) as i:
                    step.enter(i, 16)
                    group(1, i)
                    group(2, i)
                    step.leave((GROUPS - 2) // 2)
                group(GROUPS - 1)

            ffn(0, A_F0)

            for k in range(KT):
                add_to_x(down_acc(A_F0, GROUPS - 1, k), k)
                if k:
                    low(3, C_GKV, k - 1)
            low(3, C_GKV, KT - 1)
            for k in range(KT):
                add_square(2, k)
            inverse(2)
            with dve.Fori(0, KT // 2) as i:
                for s in range(2):
                    evac(A_K + s, tile(KTR, s, i, 2), i, 2)
            dve.wait_ge(FS[0]["tail_out"], 16)

            def v_line(j, i=None):
                if j >= 2:
                    dve.wait_ge(vtr_done, val(2 * j - 2, i, 4))
                    dve.wait_ge(vts_done, val(j - 1, i, 2))
                    dve.wait_ge(vt_out[j % 2], val(16 * (j // 2), i, 16))
                evac(A_V + j, Z[j % 2][:, 0:T], i, 2)

            def v_rows(j, i=None):
                at_ = slice(j, j + 1) if i is None else bass.ds(i * 2 + j, 1)
                for b in range(2):
                    dve.wait_ge(vtr_done, val(2 * j + b + 1, i, 4))
                    dve.tensor_copy(V[:, at_, 4 * b:4 * b + 4, :].rearrange("p a t e -> p (a t) e"),
                                    PS[:, 6 + b, :].rearrange("p (t e) -> p t e", t=4)
                                    ).then_inc(vtr_read, 1)

            v_line(0)
            v_line(1)
            with dve.Fori(0, KT // 2 - 1) as i:
                for j in range(2):
                    v_rows(j, i)
                    v_line(j + 2, i)
            for k in range(KT - 1):
                low(4, C_GMIX1, k)
            v_rows(KT - 2)
            low(4, C_GMIX1, KT - 1)
            v_rows(KT - 1)
            dve.wait_ge(vtr_done, 2 * KT + 1)
            dve.tensor_copy(VS[:, :, :].rearrange("p (b h) e -> p b h e", b=2),
                            PS[0:TS, 6:8, :].rearrange("p b (h e) -> p b h e", h=4)
                            ).then_inc(vtr_read, 1)
            dve.wait_ge(x_out, 16)
            with dve.Fori(0, KT // 2) as i:
                for s in range(2):
                    wait_acc(dve, A_Q + s, i, 2)
                    dve.scalar_tensor_tensor(as_acc(tile(QT, s, i, 2)), acc(A_Q + s), HD ** -0.5,
                                             as_acc(RINV[:, :]), MUL, MUL
                                             ).then_inc(acc_free[(A_Q + s) % 2], 1)

            wait_acc(dve, A_Q + KT - 1)
            step(dve.memset(SMK[:, :], NEG))
            step(dve.memset(QP[:, :], 0.0))
            step(dve.memset(SPR[:, :], 0.0))
            dve.wait_ge(sb_in, 16 * 2 * NS)
            step(dve.tensor_copy(SMK[:, :].rearrange("p (q x) -> p q x", q=NB)[:, :, 0:NS],
                                 SBI[:, PAST:NKEY].unsqueeze(1).to_broadcast([SROWS, NB, NS])))

            def sample_queries(j, hp):
                for c in range(2):
                    q = slice(c * HD, (c + 1) * HD)
                    last = dve.tensor_copy(
                        QP[q, :].rearrange("p (h x) -> p h x", x=SROWS + 1)[
                            :, :, c * NS * NH:(c + 1) * NS * NH:NH],
                        QT[q, :, bass.ds(hp * (2 * NS) + (SEQ + NS * j), NS)])
                last.then_inc(qp_done, 1)

            def sample_maxima(j, hp):
                dve.wait_ge(ss_done, hp * 2 + (j + 1))
                dve.tensor_tensor(SPR[0:SROWS, 0:PAST], PS[0:SROWS, 7, 0:PAST], SBI[:, 0:PAST], ADD)
                step(dve.tensor_tensor(SPR[0:SROWS, PAST:PAST + TS], PS[0:SROWS, 7, PAST:PAST + TS],
                                       SMK[:, bass.ds(hp * (2 * TS) + j * TS, TS)], ADD))
                step(dve.reduce_max(SST[:, 0:1], SPR[0:SROWS, :], X_AXIS))
                dve.tensor_scalar(SST[:, 1:2], SST[:, 0:1], -1.0, None, MUL).then_inc(snm_done, 1)

            def sample_weights(j, hp):
                dve.wait_ge(sexp_done, hp * 2 + (j + 1))
                step(dve.reciprocal(SST[:, 3:4], SST[:, 2:3]))
                dve.tensor_scalar(SPR[0:SROWS, :], SPR[0:SROWS, :], SST[:, 3:4], CROW[0:SROWS, :], MUL, MUL
                                  ).then_inc(spn_done, 1)

            def sample_combine(j, hp):
                dve.wait_ge(sc1_done, hp * 2 + (j + 1))
                dve.tensor_tensor(SW[:, :, :], PS[:, 7, 0:NPG * P].rearrange(
                    "p (g r) -> p g r", g=NPG)[:, :, 0:NS * NH], SC1[:, :, :], ADD)
                dve.tensor_tensor(SWN[:, :], PS[0:TS, 7, NPG * P:NPG * P + NS * NH],
                                  SCN[:, :], ADD).then_inc(sw_done, 1)

            def sample_output(j, hp):
                dve.wait_ge(so_done, hp * 2 + (j + 1))
                dve.tensor_copy(OSM[:, :, bass.ds(hp * (2 * NS) + NS * j, NS)],
                                PS[:, 7, 0:NH * NS].rearrange("p (h s) -> p h s", h=NH)
                                ).then_inc(so_read, 1)

            with dve.Fori(0, NH // 2) as hp:
                step.enter(hp, 16 * 2 + 2 * 3 + 2 * 3)
                for t in range(ATT_STEPS):
                    if 4 <= t < 20:
                        v = t - 4
                        s, i = v // 8, v % 8
                        dve.wait_ge(pv_done, hp * 16 + (v + 1))
                        if i == 0:
                            dve.wait_ge(ot_read, hp * 4 + 1)
                        dve.tensor_copy(OQ[:, s, i, :], PS[:, 6, 0:P]).then_inc(o_read, 1)
                    if t < 16:
                        s, i = t // 8, t % 8
                        n = (i + 1) * P
                        if i == 0:
                            dve.wait_ge(bias_in[s], hp * 16 + 16)
                        for c in range(2):
                            dve.wait_ge(s_done, hp * 32 + (2 * t + c + 1))
                            dve.memset(CARRY[:, 1 + c:2 + c], 0.0)
                            dve.tensor_tensor_reduce(
                                PR[:, t % 3, c, 0:n],
                                PS[:, 2 * c:2 * c + 2, :].rearrange("p b n -> p (b n)")[:, 0:n],
                                BIAS[:, s, SEQ - n:SEQ], 1.0, -3e38, ADD, ALU.max,
                                MX[:, t % 3, c:c + 1]).then_inc(ttr_done, 1)
                            if c == 1:
                                for b in range(2):
                                    dve.wait_ge(ttr_done, hp * 32 + (2 + 2 * t + b + 1))
                                    dve.tensor_scalar(MX[:, t % 3, 2 + b:3 + b],
                                                      MX[:, t % 3, b:b + 1], -1.0, None, MUL
                                                      ).then_inc(nm_ready, 1)
                    if 1 <= t < 17:
                        v = t - 1
                        s, i = v // 8, v % 8
                        n = (i + 1) * P
                        dve.wait_ge(e_done, hp * 32 + (2 * v + 2))
                        if v:
                            dve.wait_ge(wc_done, hp * 16 + v)
                        step(dve.reciprocal(SM[:, 3, 0:1], SSUM[:, s, 1, i:i + 1]))
                        step(dve.scalar_tensor_tensor(SM[:, 3, 1:2], SM[:, 3, 0:1],
                                                      NLAM[:, 3:4], SSUM[:, s, 0, i:i + 1], MUL, MUL))
                        dve.scalar_tensor_tensor(PR[:, v % 3, 0, 0:n], PR[:, v % 3, 1, 0:n],
                                                 SM[:, 3, 1:2], PR[:, v % 3, 0, 0:n], MUL, ADD
                                                 ).then_inc(wc_done, 1)
                    for s in range(2):
                        if t == SAMPLE_STEP[s] - 1:
                            sample_queries(s, hp)
                        if t == SAMPLE_STEP[s]:
                            sample_maxima(s, hp)
                        if t == SAMPLE_STEP[s] + 1:
                            sample_weights(s, hp)
                        if t == SAMPLE_STEP[s] + 3:
                            sample_combine(s, hp)
                        if t == SAMPLE_STEP[s] + 4:
                            sample_output(s, hp)
                        if t == 12 + 8 * s:
                            dve.wait_ge(osq_done, hp * 2 + (s + 1))
                            step(dve.tensor_reduce(SM[:, 0], OQS[:, :, :], X_AXIS, ADD))
                            step(dve.tensor_tensor(SM[:, 1], SSUM[:, s, 0, :], SSUM[:, s, 0, :], MUL))
                            dve.scalar_tensor_tensor(SM[:, 1], SM[:, 1], P * EPS, SM[:, 0], MUL, ADD
                                                     ).then_inc(var_done, 1)
                        if t == 13 + 8 * s:
                            dve.wait_ge(std_done, hp * 2 + (s + 1))
                            step(dve.reciprocal(SM[:, 2], SM[:, 2]))
                            dve.tensor_tensor(OQ[:, s, :, :], OQ[:, s, :, :],
                                              SM[:, 2].unsqueeze(2).to_broadcast([P, 8, P]), MUL
                                              ).then_inc(on_done, 1)
                step.leave(NH // 2)

            dve.wait_ge(sostd_done, 1)
            step(dve.reciprocal(OSQ[:, :, :], OSQ[:, :, :]))
            dve.tensor_tensor(OSM[:, :, :], OSM[:, :, :], OSQ[:, :, :], MUL).then_inc(son_done, 1)
            dve.wait_ge(ot_full, 1)
            lows(5, OT)
            dve.wait_ge(x_back, 16)
            norm_after_units(3, A_O, 6, C_GFFN1)
            ffn(1, A_F1)
            for k in range(KT):
                add_to_x(down_acc(A_F1, GROUPS - 1, k), k)
                add_square(4, k)
            inverse(4)
            for k in range(KT):
                if k >= 2:
                    dve.wait_ge(y_out[k % 2], 16 * (k // 2))
                dve.scalar_tensor_tensor(Z[k % 2][:, 0:T], X[:, k, :], col(C_GOUT + k), RINV[:, :],
                                         MUL, MUL).then_inc(yt_done, 1)


_OUTPUTS = {
    "y": (P, KT, T), "rg_h": (P, KT, NB + 1), "rg_conv": (P, KT, NB + 1, RW - 1),
    "ffn_conv": (2, P, 2 * FT, NB + 1, FW - 1), "k": (P, KT, T), "v": (P, KT, T),
}


def _tiles(a, rest=()):
    a = np.asarray(a)
    return a.reshape(a.shape[0] // P, P, *a.shape[1:]).swapaxes(0, 1)


def _weight_units(w):
    k, n = w.shape
    return w.reshape(k // P, P, n // P, P).transpose(2, 1, 0, 3)


def _ffn_units(up, down):
    u = _weight_units(up)
    d = down.reshape(GROUPS, 2, P, 2, 4, P).transpose(0, 3, 2, 4, 1, 5).reshape(GROUPS, 2, P, KT, P)
    ups = [np.stack([u[f], u[FT + f]]) for f in range(FT)]
    parts = [ups[0], ups[1]]
    for g in range(GROUPS):
        if g + 1 < GROUPS:
            parts += [ups[2 * g + 2], ups[2 * g + 3]]
        parts.append(d[g])
    return np.concatenate(parts)


def _one_hot():
    rel = REL0 - np.arange(LINE)
    n = np.maximum(rel, 0)
    exact = BUCKETS // 2
    nf = np.maximum(n, 1).astype(np.float32)
    large = exact + (np.log(nf / np.float32(exact)) / np.float32(np.log(MAXDIST / exact))
                     * np.float32(BUCKETS - exact)).astype(np.int32)
    bucket = np.where(n < exact, n, np.minimum(large, BUCKETS - 1))
    hot = np.zeros((BUCKETS + 1, LINE), np.float32)
    hot[np.where(rel >= 0, bucket, BUCKETS), np.arange(LINE)] = 1.0
    return hot


def kernel(x_prompt, x_sample, state_rglru_h, state_rglru_conv, state_ffn_conv, cache_k, cache_v,
           page_table, rel_bias, norm_mix, norm_ffn, final_norm, rg_w_in, rg_conv_w, rg_conv_b,
           rg_w_a, rg_b_a, rg_w_x, rg_b_x, rg_lambda, rg_w_out, kv_norm, w_kv, attn_w_q, lam_q1,
           lam_k1, lam_q2, lam_k2, attn_subln, attn_w_o, ffn_w_up, ffn_conv_w, ffn_conv_b,
           ffn_w_down):
    import concourse.bacc as bacc
    from concourse.bass_utils import run_bass_kernel_spmd

    f = {k: np.asarray(v) for k, v in locals().items() if k not in ("bacc", "run_bass_kernel_spmd")}
    x = np.concatenate([f["x_prompt"].reshape(SEQ, D), f["x_sample"].reshape(TS, D)])

    w_in = _weight_units(f["rg_w_in"][0])
    gates = np.zeros((KT, P, KT, P), np.float32)
    gates[:, :, 0] = f["rg_w_a"][0]
    gates[:, :, 1] = f["rg_w_x"][0]
    rg = np.stack([w_in[KT:], w_in[:KT], gates], 1).reshape(3 * KT, P, KT, P)
    w = np.concatenate([
        rg, _weight_units(f["rg_w_out"][0]), _ffn_units(f["ffn_w_up"][0], f["ffn_w_down"][0]),
        _weight_units(f["w_kv"]), _weight_units(f["attn_w_q"][0]), _weight_units(f["attn_w_o"][0]),
        _ffn_units(f["ffn_w_up"][1], f["ffn_w_down"][1])])

    def cols(*vectors):
        return np.concatenate([_tiles(v) for v in vectors], 1)

    columns = cols(
        f["norm_mix"][0], f["norm_ffn"][0], f["kv_norm"], f["norm_mix"][1], f["norm_ffn"][1],
        f["final_norm"], *f["rg_conv_w"][0], f["rg_conv_b"][0], f["rg_b_a"][0], f["rg_b_x"][0],
        f["rg_lambda"][0], f["attn_subln"][0], *f["ffn_conv_w"][0], f["ffn_conv_b"][0],
        *f["ffn_conv_w"][1], f["ffn_conv_b"][1])
    lam = np.stack([f["lam_q1"][0], f["lam_k1"][0], f["lam_q2"][0], f["lam_k2"][0]])

    inputs = {
        "x": _tiles(x.T),
        "w": w,
        "columns": columns,
        "lam": np.broadcast_to(lam, (P, 4, HD)),
        "rel_bias": f["rel_bias"],
        "one_hot": _one_hot(),
        "rg_conv_state": _tiles(f["state_rglru_conv"][0].transpose(2, 0, 1)),
        "rg_h_state": _tiles(f["state_rglru_h"][0].T),
        "ffn_state": np.stack([_tiles(s.transpose(2, 0, 1)) for s in f["state_ffn_conv"]]),
        "cache_k": f["cache_k"].reshape(NPOOL, PAGE, NH, P).transpose(0, 3, 2, 1),
        "cache_v": f["cache_v"],
        "page_table": f["page_table"].reshape(1, NB * NPG),
    }
    inputs = {k: np.ascontiguousarray(v) for k, v in inputs.items()}

    nc = bacc.Bacc("TRN2", target_bir_lowering=False, num_devices=1, dynamic_dma_scratch_size=1024)
    dt = mybir.dt
    I = {k: nc.dram_tensor(f"in_{k}", v.shape, dt.from_np(v.dtype), kind="ExternalInput").ap()
         for k, v in inputs.items()}
    O = {k: nc.dram_tensor(f"out_{k}", s, dt.float32, kind="ExternalOutput").ap()
         for k, s in _OUTPUTS.items()}
    S = {k: nc.dram_tensor(f"scratch_{k}", s, dt.float32, kind="Internal").ap()
         for k, s in {"x": (P, KT, T), "line": (NH, P * LINE)}.items()}
    program(nc, I, O, S)
    r = run_bass_kernel_spmd(nc, [{f"in_{k}": v for k, v in inputs.items()}], core_ids=[0])
    out = {k: r.results[0][f"out_{k}"] for k in _OUTPUTS}

    def rows(a):
        return a.transpose(2, 1, 0).reshape(a.shape[2], -1)

    y, k, v = rows(out["y"]), rows(out["k"]), rows(out["v"])
    h = out["rg_h"].transpose(2, 1, 0).reshape(NB + 1, D)
    rc = out["rg_conv"].transpose(2, 3, 1, 0).reshape(NB + 1, RW - 1, D)
    fc = out["ffn_conv"].transpose(0, 3, 4, 2, 1).reshape(2, NB + 1, FW - 1, 2 * DFF)
    c = np.ascontiguousarray
    return (c(y[:SEQ].reshape(1, SEQ, D)), c(y[SEQ:].reshape(NB, NS, D)),
            c(h[None, :1]), c(rc[None, :1]), c(fc[:, :1]),
            c(k[:SEQ].reshape(1, SEQ, NH, 2, HD)), c(v[:SEQ].reshape(1, SEQ, NH, 2 * HD)),
            c(h[None, 1:]), c(rc[None, 1:]), c(fc[:, 1:]),
            c(k[SEQ:].reshape(NB, NS, NH, 2, HD)), c(v[SEQ:].reshape(NB, NS, NH, 2 * HD)))
```

```python
from contextlib import ExitStack

import numpy as np

import concourse.bass as bass
from concourse import mybir

P = 128
D = 1024
KT = D // P
SEQ = 1024
NB, NS = 8, 4
TS = NB * NS
T = SEQ + TS
NCH = 3
CH = T // NCH
PAST = 256
PAGE = 128
NPG = PAST // PAGE
NPOOL = 20
NH = 8
HD = 64
DFF = 3072
FT = DFF // P
GROUPS = FT // 2
RW = 4
FW = 3
EPS = 1e-6
NEG = -1e30
BUCKETS, MAXDIST = 32, 128
LAM_INIT = 0.8 - 0.6 * float(np.exp(-0.3))

U_RG = 0
U_OUT = U_RG + 3 * KT
U_F0 = U_OUT + KT
F_UNITS = 6 * GROUPS
U_K = U_F0 + F_UNITS
U_V = U_K + KT
U_Q = U_V + KT
U_O = U_Q + KT
U_F1 = U_O + KT
NU = U_F1 + F_UNITS

A_RG = 0
A_OUT = A_RG + 4 * KT
A_F0 = A_OUT + KT
F_ACCS = 12 * GROUPS
A_K = A_F0 + F_ACCS
A_V = A_K + KT
A_Q = A_V + KT
A_O = A_Q + KT
A_F1 = A_O + KT


def up_acc(a, g, j):
    return a + j if g == 0 else a + 4 + (g - 1) * 12 + j


def down_acc(a, g, o):
    return a + 4 + g * 12 + (4 if g < GROUPS - 1 else 0) + o


def accs_after():
    out = []
    for n in range(KT):
        b = A_RG + 4 * n
        out += [b + 1, b + 2, b + 4]
    out += [A_OUT + o + 1 for o in range(KT)]

    def ffn(a):
        r = [up_acc(a, 0, j) + 1 for j in range(4)]
        for g in range(GROUPS):
            if g + 1 < GROUPS:
                r += [up_acc(a, g + 1, j) + 1 for j in range(4)]
            r += [down_acc(a, g, 3) + 1, down_acc(a, g, 7) + 1]
        return r

    out += ffn(A_F0)
    for a in (A_K, A_V, A_Q, A_O):
        out += [a + o + 1 for o in range(KT)]
    return out + ffn(A_F1)


AFTER = accs_after()
assert len(AFTER) == NU

C_GMIX0, C_GFFN0, C_GKV, C_GMIX1, C_GFFN1, C_GOUT = (8 * i for i in range(6))
C_RGW = 48
C_RGB = C_RGW + RW * KT
C_BA = C_RGB + KT
C_BX = C_BA + KT
C_LAM = C_BX + KT
C_SUB = C_LAM + KT
C_FW = C_SUB + 1
NFC = (FW + 1) * 2 * FT
NCOL = C_FW + 2 * NFC

REL0 = SEQ - 1
LINE = SEQ + P
SROWS = 2 * NS * NH
NKEY = PAST + NS


def program(nc, I, O, S):
    F32, F32R, I32 = mybir.dt.float32, mybir.dt.float32r, mybir.dt.int32
    ALU, ACT = mybir.AluOpType, mybir.ActivationFunctionType
    X_AXIS = mybir.AxisListType.X

    with ExitStack() as ctx:
        top = [(nc.sbuf_base + 63) // 64 * 64]

        def at(name, shape, dt, offset):
            assert offset + 4 * int(np.prod(shape[1:])) <= nc.sbuf_usable_end, name
            return nc.alloc_sbuf_tensor_at(name, shape, dt, offset=offset)

        def sb(name, shape, dt=F32):
            t = at(name, shape, dt, top[0])
            top[0] += (4 * int(np.prod(shape[1:])) + 31) // 32 * 32
            return t

        b0 = top[0]
        X = sb("x", [P, KT, T])
        a0 = top[0]
        Y = sb("y", [P, KT, T])
        n0 = top[0]
        XNH = sb("xn_hi", [P, KT, T], F32R)
        XNL = sb("xn_lo", [P, KT, T], F32R)
        n1 = top[0]
        w0 = top[0]
        WRAW = sb("w_raw", [P, 2, KT, P])
        WHI = sb("w_hi", [P, 2, KT, P], F32R)
        WLO = sb("w_lo", [P, 2, KT, P], F32R)
        w1 = top[0]
        COL = sb("columns", [P, NCOL])
        ONES = sb("ones", [P, P])
        IDENT = sb("ident", [P, P])
        EPSC = sb("eps", [P, 1])
        CARRY = sb("carriers", [P, 11])
        HBA = sb("half_b_a", [P, KT])
        HBX = sb("half_b_x", [P, KT])
        SP2 = sb("softplus_twice", [P, KT])
        SPM = sb("softplus_minus_4", [P, KT])
        SPT = sb("softplus_tmp", [P, 4, KT])
        NLAM = sb("neg_lambda", [P, 4])
        SUBG = sb("subln_scaled", [P, 1])
        CROW = sb("sample_row_factor", [P, 1])
        T8 = sb("tmp8", [P, NB])
        RST = sb("rg_conv_state", [P, KT, NB, RW - 1])
        H0 = sb("rg_h_state", [P, KT, NB])
        RTAIL = sb("rg_conv_tails", [P, KT, NB + 1, RW - 1])
        HTAIL = sb("rg_h_tails", [P, KT, NB + 1])
        r0 = top[0]
        RINV = sb("inverse_rms", [P, T])
        l0 = top[0]
        LINEW = 1088
        Z = [sb(f"line{i}", [P, LINEW]) for i in range(7)]
        XCH = sb("xc_hi", [P, T], F32R)
        XCL = sb("xc_lo", [P, T], F32R)
        FST = sb("ffn_state", [P, 2 * FT, NB, FW - 1])
        FTAIL = sb("ffn_tails", [P, 2 * FT, NB + 1, FW - 1])

        LAMV = at("lam_vectors", [P, 4, HD], F32, a0)
        LAMP = at("lam_products", [P, 2, HD], F32, a0 + 1024)
        TAB = at("bias_table", [BUCKETS + 1, NH], F32, a0 + 2048)
        HOT = at("one_hot", [BUCKETS + 1, LINE], F32, a0 + 4096)
        BLN = at("bias_line", [NH, LINE], F32, a0 + 4096 + 4 * LINE)
        HHI = at("h_hi", [P, 4, T], F32R, a0)
        HLO = at("h_lo", [P, 4, T], F32R, a0 + 16 * T)
        KTR = at("k_t", [P, KT, T], F32, a0)
        OT = at("o_t", [P, KT, T], F32, a0)
        QT = at("q_t", [P, KT, T], F32, b0)
        v0 = l0 + 4 * 4 * LINEW
        V = at("v", [P, NH, KT, P], F32, v0)
        VS = at("v_sample", [TS, NH, P], F32, v0 + 4 * SEQ * KT)
        VTS = at("v_sample_t", [P, NH, TS], F32, v0 + 4 * SEQ * (KT + 1))

        def region(lo, hi):
            o = [lo]

            def place(name, shape, dt=F32):
                t = at(name, shape, dt, o[0])
                o[0] += (4 * int(np.prod(shape[1:])) + 31) // 32 * 32
                assert o[0] <= hi, name
                return t

            def same(name, like, dt):
                size = (4 * int(np.prod(like.shape[1:])) + 31) // 32 * 32
                return at(name, like.shape, dt, o[0] - size)

            return place, same

        xa, xsame = region(n0, n1)
        QRAW, QLO, QHI, KRAW, KLO, KHI = ([] for _ in range(6))
        for s, (place, same) in enumerate((region(l0, v0), (xa, xsame))):
            for raw, low, high, n in ((QRAW, QLO, QHI, "q"), (KRAW, KLO, KHI, "k")):
                raw.append(place(f"{n}_raw{s}", [P, SEQ]))
                low.append(same(f"{n}_low{s}", raw[-1], F32R))
                high.append(place(f"{n}_high{s}", [P, SEQ], F32R))
        PR = [xa("probs0", [P, 4, SEQ]), xa("probs1", [P, 2, SEQ])]
        WTS = xa("w_t", [P, 2, SEQ])
        OQ = xa("o_q", [P, 2, 8, P])
        BIAS = xa("bias_strip", [P, 2, SEQ])
        MX = xa("maxima", [P, 4, 4])
        SSUM = xa("sums", [P, 2, 2, 8])
        SM = xa("small", [P, 4, 8])
        OSM = xa("o_sample", [P, NH, TS])
        OQS = at("o_sq", [P, 8, P], F32, r0)
        OSQ = at("o_sample_sq", [P, NH, TS], F32, r0)
        wa, _ = region(w0, w1)
        KC = wa("k_pages", [P, NPG, NH, PAGE])
        VC = wa("v_pages", [P, NPG, NH, P])
        QP = wa("q_padded", [P, NH * (SROWS + 1)])
        SPR = wa("sample_probs", [P, PAST + TS])
        SC1 = wa("sample_c1", [P, NPG, NS * NH])
        SCN = wa("sample_c1_new", [TS, NS * NH])
        SW = wa("sample_w_t", [P, NPG, NS * NH])
        SWN = wa("sample_w_new_t", [TS, NS * NH])
        SBI = wa("sample_bias", [SROWS, NKEY])
        SMK = wa("sample_new_bias", [SROWS, NB * (TS + NS)])
        SST = wa("sample_stats", [SROWS, 8])
        PT = wa("pages", [1, NB * NPG], I32)

        PS = ctx.enter_context(nc.psum_tensor("psum", [P, 8, 512], F32))

        def sem(name):
            return ctx.enter_context(nc.semaphore(name))

        w_in = [sem("w_in0"), sem("w_in1")]
        w_hi, w_lo = sem("w_hi"), sem("w_lo")
        acc_done = sem("acc_done")
        acc_free = [sem("acc_free0"), sem("acc_free1")]
        sq_done, sum_done, sum_mm, root_done = (
            sem(n) for n in ("sq_done", "sum_done", "sum_mm", "root_done"))
        nhi_done, nlo_done, xn_free, yt_done = (
            sem(n) for n in ("nhi_done", "nlo_done", "xn_free", "yt_done"))
        x_in = [sem(f"x_in{k}") for k in range(KT)]
        c_in, lam_in, tab_in, rst_in, fst_in = (
            sem(n) for n in ("c_in", "lam_in", "tab_in", "rst_in", "fst_in"))
        pool_const, act_const, dve_const, scal_done = (
            sem(n) for n in ("pool_const", "act_const", "dve_const", "scal_done"))
        line_mm, line_read, line_out = (
            sem(n) for n in ("line_mm", "line_read", "line_out"))
        rec_state, rec_used, xc_ready, xch_ready, xcl_ready, gel_ready, s_ready, sqrt_ready, y_done = (
            sem(n) for n in ("rec_state", "rec_used", "xc_ready", "xch_ready", "xcl_ready",
                             "gel_ready", "s_ready", "sqrt_ready", "y_done"))
        FS = [{n: sem(f"{n}{i}") for n in ("u_state", "u_used", "vc_ready", "gc_ready", "gg_ready",
                                           "hf_ready", "hh_ready", "hl_ready", "tail_out")}
              for i in range(2)]
        k_out, x_out, x_back = sem("k_out"), sem("x_out"), sem("x_back")
        vt_out = [sem("vt_out0"), sem("vt_out1")]
        vtr_done, vtr_read = sem("vtr_done"), sem("vtr_read")
        vts_done = sem("vts_done")
        head_in = [sem("head_in0"), sem("head_in1")]
        bias_in = [sem("bias_in0"), sem("bias_in1")]
        split_done = sem("split_done")
        s_done, ttr_done, nm_ready, e_done, wc_done, wt_done, wt_read, pv_done, o_read = (
            sem(n) for n in ("s_done", "ttr_done", "nm_ready", "e_done", "wc_done", "wt_done",
                             "wt_read", "pv_done", "o_read"))
        osq_done, var_done, std_done, on_done, ot_done, ot_read = (
            sem(n) for n in ("osq_done", "var_done", "std_done", "on_done", "ot_done", "ot_read"))
        pages_in, pg_in, sb_in = sem("pages_in"), sem("pg_in"), sem("sb_in")
        qp_done, ss_done, snm_done, sexp_done, spn_done, st_done, sc1_done, sw_done, so_done, so_read = (
            sem(n) for n in ("qp_done", "ss_done", "snm_done", "sexp_done", "spn_done", "st_done",
                             "sc1_done", "sw_done", "so_done", "so_read"))
        sosq_done, sored_done, sostd_done, son_done, ot_full = (
            sem(n) for n in ("sosq_done", "sored_done", "sostd_done", "son_done", "ot_full"))
        rg_out = sem("rg_out")
        y_out = sem("y_out")
        dve_step, act_step = sem("dve_step"), sem("act_step")

        TILES = (0, 1, 2, 3, 4, 5, 6, 7)
        SAMPLE_STEP = (1, 9)
        SQUARE_STEP = {11: 0, 3: -1}
        VAR_STEP = {12: 0, 4: -1}
        SCALE_STEP = {13: 0, 5: -1}
        OUT_STEP = {15: (0, 0), 0: (-2, 1), 7: (-1, 0), 8: (-1, 1)}

        def turns_of(eng, turn, enter=None, leave=None):
            turn(0, first=True)
            with eng.Fori(1, NH // 2) as hp:
                if enter:
                    enter(hp)
                turn(hp)
                if leave:
                    leave()
            turn(NH // 2, tail=True)

        def live(v, first, tail):
            return not tail if v >= 0 else not first

        def one(e):
            return slice(e, e + 1) if isinstance(e, int) else bass.ds(e, 1)

        def some(e, n):
            return slice(e, e + n) if isinstance(e, int) else bass.ds(e, n)

        block = ctx.enter_context(nc.Block())

        def col(c, n=None):
            return COL[:, c:c + 1] if n is None else COL[:, bass.ds(n + c, 1)]

        def as_acc(line):
            return line.rearrange("p (c t) -> p c t", c=NCH)

        def acc(a):
            s = a % 2
            return PS[:, 3 * s:3 * s + 3, 0:CH]

        def tile(region, k, i=None, m=1):
            if i is None:
                return region[:, k, :]
            return region[:, bass.ds(i * m + k, 1), :].rearrange("p a t -> p (a t)")

        def samples(line, hist):
            return line[:, hist + SEQ:hist + SEQ + NB * (hist + NS)].rearrange(
                "p (b s) -> p b s", b=NB)

        def val(base, i=None, m=0):
            return base if i is None else i * m + base

        def wait_acc(eng, a, i=None, m=0):
            eng.wait_ge(acc_done, val(a + 1, i, m))

        def wait_read(eng, a, i=None, m=0):
            eng.wait_ge(acc_free[a % 2], val(a // 2 + 1, i, m // 2))

        def wait_room(eng, a, i=None, m=0):
            if a >= 2:
                wait_read(eng, a - 2, i, m)

        class Steps:

            def __init__(self, eng, s):
                self.eng, self.s, self.n, self.i, self.per = eng, s, 0, None, 0

            def __call__(self, ins):
                ins.then_inc(self.s, 1)
                self.n += 1
                self.eng.wait_ge(self.s, val(self.n, self.i, self.per))

            def enter(self, i, per, first=0):
                self.n -= per * first
                self.start, self.i, self.per, self.first = self.n, i, per, first

            def leave(self, end):
                assert self.n == self.start + self.per, (self.n - self.start, self.per)
                self.n = self.start + self.per * end
                self.i = None

        @block.sync
        def _(sp):
            def load_weights(s, u):
                sp.dma_start(WRAW[:, s], I["w"][bass.ds(u, 1)].rearrange("u p k f -> p (u k) f")
                             ).then_inc(w_in[s], 16)

            def pairs(lo, hi):
                with sp.Fori(lo // 2, hi // 2) as i:
                    for s in range(2):
                        sp.wait_ge(w_lo, i * 2 + s - 1)
                        load_weights(s, i * 2 + s)

            sp.dma_start(COL[:, :], I["columns"]).then_inc(c_in, 16)
            load_weights(0, 0)
            load_weights(1, 1)
            pairs(2, U_O)

            def head(s, h):
                for dst, src in ((QRAW, QT), (KRAW, KTR)):
                    sp.dma_start(dst[s][:, :], src[:, bass.ds(h, 1), 0:SEQ].rearrange(
                        "p a t -> p (a t)")).then_inc(head_in[s], 16)

            def strip(s, h):
                line = S["line"][bass.ds(h, 1), P - 1:P - 1 + P * (LINE - 1)]
                sp.dma_start(BIAS[:, s], line.rearrange("h (p m) -> p (h m)", m=LINE - 1)[:, 0:SEQ]
                             ).then_inc(bias_in[s], 16)

            def pages(j, i=None):
                for g in range(NPG):
                    c = j * NPG + g
                    at_ = slice(c, c + 1) if i is None else bass.ds(i * (2 * NPG) + c, 1)
                    page = sp.value_load(PT[0:1, at_], min_val=0, max_val=NPOOL - 1)
                    sp.dma_start(KC[:, g], I["cache_k"][bass.ds(page, 1)].rearrange(
                        "n d h s -> d (n h) s")).then_inc(pg_in, 16)
                    sp.dma_start(VC[:, g], I["cache_v"][bass.ds(page, 1)].rearrange(
                        "n s h e -> s (n h) e")).then_inc(pg_in, 16)

            for s in range(2):
                sp.wait_ge(vt_out[s], 16 * (KT // 2))
            sp.wait_ge(vts_done, KT)
            wait_read(sp, A_Q)
            head(0, 0)
            wait_read(sp, A_Q + KT - 2)
            wait_read(sp, A_Q + KT - 1)
            sp.wait_ge(line_out, 16)
            strip(0, 0)
            sp.dma_start(PT[:, :], I["page_table"]).then_inc(pages_in, 16)
            head(1, 1)
            strip(1, 1)
            for r in range(2 * NS):
                off = REL0 - PAST - r % NS
                sp.dma_start(SBI[r * NH:(r + 1) * NH, :], S["line"][:, off:off + NKEY]
                             ).then_inc(sb_in, 16)
            sp.wait_ge(pages_in, 16)
            pages(0)
            with sp.Fori(0, NH // 2 - 1) as i:
                for s in range(2):
                    sp.wait_ge(so_done, i * 2 + (1 + s))
                    pages(1 + s, i)
                    sp.wait_ge(ttr_done, i * 32 + (2 + (s + 1) * 16))
                    head(s, i * 2 + (2 + s))
                    strip(s, i * 2 + (2 + s))
            sp.wait_ge(so_done, NB - 1)
            pages(NB - 1)
            sp.wait_ge(so_read, NB)

            pairs(U_O, NU)
            for k in range(KT):
                sp.wait_ge(yt_done, k + 1)
                sp.dma_start(O["y"][:, k, :], Y[:, k, :]).then_inc(y_out, 16)
            sp.wait_ge(y_out, 16 * KT)
            sp.wait_ge(rg_out, 32)
            sp.wait_ge(k_out, 16)
            for s in range(2):
                sp.wait_ge(vt_out[s], 16 * (KT // 2))
                sp.wait_ge(FS[s]["tail_out"], 16)

        @block.gpsimd
        def _(pool):
            pool.memset(ONES[:, :], 1.0).then_inc(pool_const, 1)
            pool.memset(EPSC[:, :], EPS).then_inc(pool_const, 1)
            pool.memset(IDENT[:, :], 0.0).then_inc(pool_const, 1)
            pool.wait_ge(pool_const, 3)
            pool.affine_select(out=IDENT[:, :], in_=IDENT[:, :], compare_op=ALU.not_equal, fill=1.0,
                               base=0, pattern=[[-1, P]], channel_multiplier=1).then_inc(pool_const, 1)

            def split(u, used, i=None, m=0, stride=0):
                s = u % 2
                if used:
                    pool.wait_ge(acc_done, val(used, i, stride))
                pool.wait_ge(w_in[s], val(16 * (u // 2 + 1), i, 8 * m))
                pool.tensor_tensor(CARRY[:, 0:1], EPSC[:, :], EPSC[:, :], ALU.add)
                pool.tensor_scalar(WHI[:, s], WRAW[:, s], 1.0, 0.0, ALU.mult, ALU.add
                                   ).then_inc(w_hi, 1)
                pool.wait_ge(w_hi, val(u + 1, i, m))
                pool.tensor_tensor(WLO[:, s], WRAW[:, s], WHI[:, s].bitcast(F32), ALU.subtract
                                   ).then_inc(w_lo, 1)

            def straight(lo, hi):
                for u in range(lo, hi):
                    split(u, AFTER[u - 2] if u >= 2 else 0)

            def turns(u0, m, n):
                stride = AFTER[u0 + m] - AFTER[u0]
                used = [AFTER[u0 + j - 2] for j in range(m)]
                assert m % 2 == 0 and all(AFTER[u0 + j + i * m - 2] == used[j] + i * stride
                                          for i in range(n) for j in range(m))
                with pool.Fori(0, n) as i:
                    for j in range(m):
                        split(u0 + j, used[j], i, m, stride)

            def ffn(u0):
                n = (GROUPS - 2) // 2
                straight(u0, u0 + 6)
                turns(u0 + 6, 12, n - 1)
                straight(u0 + 6 + 12 * (n - 1), u0 + F_UNITS)

            straight(0, 6)
            turns(6, 6, KT // 2 - 1)
            straight(U_OUT, U_OUT + 2)
            turns(U_OUT + 2, 2, KT // 2 - 1)
            ffn(U_F0)
            straight(U_K, U_K + 2)
            turns(U_K + 2, 2, KT * 3 // 2 - 1)
            with pool.Fori(0, NH // 2) as hp:
                for s in range(2):
                    pool.wait_ge(head_in[s], hp * 32 + 32)
                    pool.tensor_tensor(CARRY[:, 0:1], EPSC[:, :], EPSC[:, :], ALU.add)
                    for raw, high in ((QRAW, QHI), (KRAW, KHI)):
                        pool.tensor_scalar(high[s][:, :], raw[s][:, :], 1.0, 0.0, ALU.mult, ALU.add
                                           ).then_inc(split_done, 1)
                    pool.wait_ge(split_done, hp * 8 + (4 * s + 2))
                    for raw, high, low in ((QRAW, QHI, QLO), (KRAW, KHI, KLO)):
                        pool.tensor_tensor(low[s][:, :], raw[s][:, :], high[s][:, :].bitcast(F32),
                                           ALU.subtract).then_inc(split_done, 1)
            straight(U_O, U_O + 2)
            turns(U_O + 2, 2, KT // 2 - 1)
            ffn(U_F1)

        @block.tensor
        def _(pe):
            def product(s, k, a, hi, lo, start, stop):
                for w, r, first, final in ((WHI, hi, True, False), (WLO, hi, False, False),
                                           (WHI, lo, False, True)):
                    for c in range(NCH):
                        last = pe.matmul(PS[:, 3 * (a % 2) + c, 0:CH], w[:, s, k, :],
                                         r[:, c * CH:(c + 1) * CH],
                                         start=start and first, stop=stop and final)
                return last

            def unit(u, a, i=None, m=0, stride=0, lows=None, release=False):
                pe.wait_ge(w_lo, val(u + 1, i, m))
                wait_room(pe, a, i, stride)
                for k in range(KT):
                    if lows is not None:
                        pe.wait_ge(nlo_done, lows + k + 1)
                    last = product(u % 2, k, a, XNH[:, k, :], XNL[:, k, :], k == 0, k == KT - 1)
                    if release and k < KT - 1:
                        last.then_inc(xn_free, 1)
                last.then_inc(acc_done, 1)

            def norm_sum(r, a):
                pe.wait_ge(sum_done, KT * (r + 1))
                if a is not None:
                    wait_room(pe, a)
                pe.matmul(PS[:, 3, 0:TS], ONES[:, :], Z[2][:, SEQ:T], start=True, stop=True
                          ).then_inc(sum_mm, 1)
                pe.matmul(PS[:, 6, :], ONES[:, :], Z[2][:, 0:512], start=True, stop=True)
                pe.matmul(PS[:, 7, :], ONES[:, :], Z[2][:, 512:SEQ], start=True, stop=True
                          ).then_inc(sum_mm, 1)
                pe.wait_ge(root_done, 2 * r + 1)

            def plain(u0, a0, lows, norm=None, release=False):
                unit(u0, a0, lows=lows)
                if norm is not None:
                    norm_sum(norm, a0 + 1)
                unit(u0 + 1, a0 + 1)
                with pe.Fori(0, KT // 2 - 2) as i:
                    for s in range(2):
                        unit(u0 + 2 + s, a0 + 2 + s, i, 2, 2)
                unit(u0 + KT - 2, a0 + KT - 2)
                unit(u0 + KT - 1, a0 + KT - 1, release=release)

            def bias_line():
                pe.wait_ge(tab_in, 32)
                pe.wait_ge(dve_const, 1)
                lw = LINE // NCH
                for c in range(NCH):
                    last = pe.matmul(PS[0:NH, 3 + c, 0:lw], TAB[:, :], HOT[:, c * lw:(c + 1) * lw],
                                     start=True, stop=True)
                last.then_inc(line_mm, 1)
                pe.wait_ge(line_read, 1)

            def rg(j, i=None, lows=None):
                u, a = U_RG + 3 * j, A_RG + 4 * j
                unit(u, a, i, 6, 8, lows)
                if lows is not None:
                    norm_sum(0, None)
                    bias_line()
                unit(u + 1, a + 1, i, 6, 8)
                pe.wait_ge(w_lo, val(u + 3, i, 6))
                pe.wait_ge(xcl_ready, val(j + 1, i, 2))
                for g in range(2):
                    wait_room(pe, a + 2 + g, i, 8)
                    product((u + 2) % 2, g, a + 2 + g, XCH[:, :], XCL[:, :], True, True
                            ).then_inc(acc_done, 1)

            pe.wait_ge(pool_const, 4)
            rg(0, lows=0)
            rg(1)
            with pe.Fori(0, KT // 2 - 1) as i:
                rg(2, i)
                rg(3, i)
            for j in range(2):
                pe.wait_ge(w_lo, U_OUT + j + 1)
                wait_room(pe, A_OUT + j)
                for k in range(KT - 1):
                    if j == 0:
                        pe.wait_ge(nlo_done, KT + k + 1)
                    product(j, k, A_OUT + j, XNH[:, k, :], XNL[:, k, :], k == 0, False)
            pe.wait_ge(nlo_done, 2 * KT)
            for j in range(2):
                k = KT - 1
                product(j, k, A_OUT + j, XNH[:, k, :], XNL[:, k, :], False, True).then_inc(acc_done, 1)
            with pe.Fori(0, KT // 2 - 2) as i:
                for s in range(2):
                    unit(U_OUT + 2 + s, A_OUT + 2 + s, i, 2, 2)
            unit(U_OUT + KT - 2, A_OUT + KT - 2)
            unit(U_OUT + KT - 1, A_OUT + KT - 1, release=True)

            def ffn(l, u0, a0, lows, norm):
                def up(u, a, i=None, lows=None):
                    for j in range(4):
                        unit(u + j, a + j, i, 12, 24, lows if j == 0 else None)
                        if lows is not None and j == 0:
                            norm_sum(norm, a + 1)

                def down(u, a, g, i=None):
                    pe.wait_ge(FS[l]["hl_ready"], val(2 * g + 2, i, 4))
                    for o in range(KT):
                        s = (u + o // 4) % 2
                        if o % 4 == 0:
                            pe.wait_ge(w_lo, val(u + o // 4 + 1, i, 12))
                        wait_room(pe, a + o, i, 24)
                        for t in range(2):
                            h = 2 * (g % 2) + t
                            last = product(s, 2 * (o % 4) + t, a + o, HHI[:, h, :], HLO[:, h, :],
                                           t == 0, t == 1)
                        last.then_inc(acc_done, 1)

                up(u0, a0, lows=lows)
                with pe.Fori(0, (GROUPS - 2) // 2) as i:
                    for g in range(2):
                        up(u0 + 4 + 6 * g, up_acc(a0, g + 1, 0), i)
                        down(u0 + 8 + 6 * g, down_acc(a0, g, 0), g, i)
                g = GROUPS - 1
                u = u0 + 4 + 6 * (g - 1)
                up(u, up_acc(a0, g, 0))
                down(u + 4, down_acc(a0, g - 1, 0), g - 1)
                down(u + 6, down_acc(a0, g, 0), g)

            ffn(0, U_F0, A_F0, 2 * KT, 1)

            plain(U_K, A_K, 3 * KT, norm=2)

            def v_back(j, i=None):
                wait_read(pe, A_V + j, i, 2)
                for b in range(KT):
                    if b % 4 == 0:
                        pe.wait_ge(vtr_read, val(2 * j + b // 4 + 1, i, 4))
                    last = pe.transpose(PS[:, 6 + b // 4, (b % 4) * P:(b % 4 + 1) * P],
                                        Z[j % 2][:, b * P:(b + 1) * P], IDENT[:, :])
                    if b % 4 == 3:
                        last.then_inc(vtr_done, 1)

            unit(U_V, A_V)
            with pe.Fori(0, KT // 2 - 1) as i:
                for s in range(2):
                    unit(U_V + 1 + s, A_V + 1 + s, i, 2, 2)
                    v_back(s, i)
            unit(U_V + KT - 1, A_V + KT - 1, release=True)
            v_back(KT - 2)
            unit(U_Q, A_Q, lows=4 * KT)
            v_back(KT - 1)
            pe.wait_ge(vts_done, KT)
            pe.wait_ge(vtr_read, 2 * KT + 2)
            for h in range(NH):
                last = pe.transpose(PS[0:TS, 6 + h // 4, (h % 4) * P:(h % 4 + 1) * P],
                                    VTS[:, h, :], IDENT[:, :])
            last.then_inc(vtr_done, 1)
            unit(U_Q + 1, A_Q + 1)
            with pe.Fori(0, KT // 2 - 1) as i:
                for s in range(2):
                    unit(U_Q + 2 + s, A_Q + 2 + s, i, 2, 2)

            wait_read(pe, A_Q + KT - 2)
            wait_read(pe, A_Q + KT - 1)
            pe.wait_ge(vtr_read, 2 * KT + 3)

            def sample_scores(j, hp):
                pe.wait_ge(pg_in, hp * 128 + 64 * (j + 1))
                pe.wait_ge(qp_done, hp * 2 + (j + 1))
                if j or not isinstance(hp, int):
                    pe.wait_ge(ot_read, hp * 4 + (1 if j else -1))
                for h in range(NH):
                    pe.matmul(PS[0:SROWS, 7, 0:PAST], QP[:, h * SROWS:(h + 1) * SROWS],
                              KC[:, :, h, :], start=(h == 0), stop=(h == NH - 1))
                for h in range(NH):
                    last = pe.matmul(PS[0:SROWS, 7, PAST:PAST + TS],
                                     QP[:, h * SROWS:(h + 1) * SROWS], KTR[:, h, SEQ:T],
                                     start=(h == 0), stop=(h == NH - 1))
                last.then_inc(ss_done, 1)

            def sample_transposes(j, hp):
                pe.wait_ge(spn_done, hp * 2 + (j + 1))
                for g in range(NPG):
                    pe.transpose(PS[:, 7, g * P:(g + 1) * P], SPR[:, g * P:(g + 1) * P],
                                 IDENT[:, :])
                pe.transpose(PS[0:TS, 7, NPG * P:(NPG + 1) * P], SPR[:, PAST:PAST + TS],
                             IDENT[:, :]).then_inc(st_done, 1)

            def sample_outputs(j, hp, blocks):
                pe.wait_ge(sw_done, hp * 2 + (j + 1))
                for g in blocks:
                    for h in range(NH):
                        v = VC[:, g, h, :] if g < NPG else VS[:, h, :]
                        w = SW[:, g, h:NS * NH:NH] if g < NPG else SWN[:, h:NS * NH:NH]
                        last = pe.matmul(PS[:, 7, h * NS:(h + 1) * NS], v, w,
                                         start=(g == 0 and h == 0),
                                         stop=(g == NPG and h == NH - 1))
                if g == NPG:
                    last.then_inc(so_done, 1)

            def turn(hp, first=False, tail=False):
                for t in range(9 if tail else 16):
                    if not tail:
                        s, i = t // 8, TILES[t % 8]
                        n = (i + 1) * P
                        if t % 8 == 0:
                            pe.wait_ge(split_done, hp * 8 + 4 * (s + 1))
                        for c in range(2):
                            pe.wait_ge(ttr_done, hp * 32 + (2 * t + c + 1))
                            rows = slice(c * HD, (c + 1) * HD)
                            for b in range(0, n, 512):
                                w = min(512, n - b)
                                for p, (q, k) in enumerate(((QHI, KHI), (QLO, KHI), (QHI, KLO))):
                                    last = pe.matmul(PS[:, 2 * c + b // 512, 0:w],
                                                     q[s][rows, i * P:(i + 1) * P],
                                                     k[s][rows, b:b + w],
                                                     start=(p == 0), stop=(p == 2))
                            last.then_inc(s_done, 1)
                    v = t - 2
                    if live(v, first, tail):
                        pe.wait_ge(wc_done, hp * 16 + (v + 1))
                        pe.wait_ge(wt_read, hp * 16 + (v + 1))
                        for b in range(TILES[v % 8] + 1):
                            last = pe.transpose(PS[:, 4 + b // 4, (b % 4) * P:(b % 4 + 1) * P],
                                                PR[0][:, v % 4, b * P:(b + 1) * P], IDENT[:, :])
                        last.then_inc(wt_done, 1)
                    v = t - 3
                    if live(v, first, tail):
                        i = TILES[v % 8]
                        pe.wait_ge(wt_read, hp * 16 + (v + 2))
                        pe.wait_ge(o_read, hp * 16 + (v + 1))
                        for b in range(i + 1):
                            last = pe.matmul(PS[:, 6, 0:P], WTS[:, v % 2, b * P:(b + 1) * P],
                                             V[:, one(hp * 2 + v // 8), b, :
                                               ].rearrange("p a e -> p (a e)"),
                                             start=(b == 0), stop=(b == i))
                        last.then_inc(pv_done, 1)
                    for j in range(2):
                        if not tail:
                            if t == SAMPLE_STEP[j]:
                                sample_scores(j, hp)
                            if t == SAMPLE_STEP[j] + 2:
                                sample_transposes(j, hp)
                            if t == SAMPLE_STEP[j] + 4:
                                sample_outputs(j, hp, (0,))
                            if t == SAMPLE_STEP[j] + 5:
                                sample_outputs(j, hp, (1, 2))
                    if t in OUT_STEP and live(OUT_STEP[t][0], first, tail):
                        h, half = OUT_STEP[t]
                        pe.wait_ge(on_done, hp * 2 + (h + 1))
                        pe.wait_ge(ot_read, hp * 4 + (2 * h + half + 1))
                        if half == 0:
                            pe.wait_ge(so_read, NB if tail else hp * 2 + (h + 2))
                        for b in range(4):
                            last = pe.transpose(PS[:, 7, b * P:(b + 1) * P],
                                                OQ[:, h % 2, 4 * half + b, :], IDENT[:, :])
                        last.then_inc(ot_done, 1)

            turns_of(pe, turn)
            pe.wait_ge(sosq_done, 1)
            pe.matmul(PS[:, 1, 0:NH * TS], ONES[:, :], OSQ[:, :, :].rearrange("p h t -> p (h t)"),
                      start=True, stop=True).then_inc(sored_done, 1)
            pe.wait_ge(sostd_done, 1)

            plain(U_O, A_O, 5 * KT, release=True)
            ffn(1, U_F1, A_F1, 6 * KT, 3)
            wait_read(pe, A_F1 + F_ACCS - 1)
            norm_sum(4, None)

        @block.scalar
        def _(act):
            step = Steps(act, act_step)

            def square(r, k):
                if k >= 2:
                    act.wait_ge(sum_done, KT * r + k - 1)
                act.activation(Z[k % 2][:, 0:T], X[:, k, :], ACT.Square).then_inc(sq_done, 1)

            def high(gain, k):
                act.activation(XNH[:, k, :], X[:, k, :], ACT.Copy, scale=col(gain + k)
                               ).then_inc(nhi_done, 1)

            def root(r):
                act.wait_ge(sum_mm, 2 * r + 1)
                act.activation(RINV[:, SEQ:T], PS[:, 3, 0:TS], ACT.Sqrt, bias=EPSC[:, :],
                               scale=1.0 / D).then_inc(root_done, 1)
                act.wait_ge(sum_mm, 2 * r + 2)
                act.activation(RINV[:, 0:SEQ].rearrange("p (b t) -> p b t", b=2), PS[:, 6:8, :],
                               ACT.Sqrt, bias=EPSC[:, :], scale=1.0 / D).then_inc(root_done, 1)

            def norm_after_units(r, a0, gain, released):
                for k in range(KT - 1):
                    wait_read(act, a0 + k)
                    square(r, k)
                for k in range(KT - 1):
                    act.wait_ge(xn_free, released + k + 1)
                    high(gain, k)
                wait_read(act, a0 + KT - 1)
                high(gain, KT - 1)
                square(r, KT - 1)
                root(r)

            act.dma_start(LAMV[:, :, :], I["lam"]).then_inc(lam_in, 16)
            for k in range(KT):
                act.dma_start(X[:, k, :], I["x"][:, k, :]).then_inc(x_in[k], 16)
            act.dma_start(TAB[0:BUCKETS, :], I["rel_bias"]).then_inc(tab_in, 16)
            act.dma_start(HOT[:, :], I["one_hot"]).then_inc(tab_in, 16)
            act.dma_start(RST[:, :, :, :], I["rg_conv_state"]).then_inc(rst_in, 16)
            act.dma_start(H0[:, :, :], I["rg_h_state"]).then_inc(rst_in, 16)
            act.dma_start(FST[:, :, :, :], I["ffn_state"][0]).then_inc(fst_in, 16)

            act.wait_ge(pool_const, 4)
            for n, q in enumerate((wt_read, ot_read)):
                act.activation(CARRY[:, 9 + n:10 + n], EPSC[:, :], ACT.Copy).then_inc(q, 1)

            def bias_line():
                act.wait_ge(line_mm, 1)
                lw = LINE // NCH
                act.activation(BLN[:, :].rearrange("h (c n) -> h c n", c=NCH), PS[0:NH, 3:6, 0:lw],
                               ACT.Copy).then_inc(line_read, 1)
                act.wait_ge(line_read, 1)
                act.dma_start(S["line"].rearrange("h (p i) -> h p i", p=P),
                              BLN[:, :].unsqueeze(1).to_broadcast([NH, P, LINE])
                              ).then_inc(line_out, 16)

            act.wait_ge(c_in, 16)
            for k in range(KT):
                act.wait_ge(x_in[k], 16)
                high(C_GMIX0, k)
                square(0, k)
            act.wait_ge(c_in, 16)
            step(act.activation(SPT[:, 0], COL[:, C_LAM:C_LAM + KT], ACT.Abs))
            act.activation(SPT[:, 1], SPT[:, 0], ACT.Exp, scale=-1.0).then_inc(act_const, 1)
            act.wait_ge(dve_const, 4)
            act.activation(NLAM[:, 0:2], NLAM[:, 0:2], ACT.Exp).then_inc(act_const, 1)
            root(0)
            bias_line()
            act.wait_ge(rst_in, 32)
            act.wait_ge(scal_done, 1)
            with act.Fori(0, KT) as n:
                act.wait_ge(rec_used, n + 1)
                act.activation(samples(Z[4], RW - 1)[:, :, 0:RW - 1],
                               RST[:, bass.ds(n, 1)].rearrange("p a b s -> p (a b) s"), ACT.Copy
                               ).then_inc(rec_state, 1)
                act.wait_ge(xc_ready, n + 1)
                act.activation(XCH[:, :], Z[0][:, 0:T], ACT.Copy).then_inc(xch_ready, 1)
                wait_read(act, A_RG + 1, n, 4)
                act.activation(Z[5][:, 0:T], Z[5][:, 0:T], ACT.Gelu_apprx_tanh
                               ).then_inc(gel_ready, 1)
                wait_acc(act, A_RG + 2, n, 4)
                act.activation(as_acc(Z[6][:, 0:T]), acc(A_RG + 2), ACT.Tanh, scale=0.5,
                               bias=HBA[:, bass.ds(n, 1)]).then_inc(acc_free[(A_RG + 2) % 2], 1)
                act.wait_ge(y_done, n + 1)
                wait_read(act, A_RG + 2, n, 4)
                act.activation(Z[2][:, 0:T], Z[6][:, 0:T], ACT.Tanh, scale=SP2[:, bass.ds(n, 1)],
                               bias=SP2[:, bass.ds(n, 1)]).then_inc(s_ready, 1)
                wait_acc(act, A_RG + 3, n, 4)
                act.activation(as_acc(Z[1][:, 0:T]), acc(A_RG + 3), ACT.Tanh, scale=0.5,
                               bias=HBX[:, bass.ds(n, 1)]).then_inc(acc_free[(A_RG + 3) % 2], 1)
                act.activation(Z[3][:, 0:T], Z[6][:, 0:T], ACT.Exp, scale=SPM[:, bass.ds(n, 1)],
                               bias=SPM[:, bass.ds(n, 1)])
                act.wait_ge(s_ready, n + 1)
                act.activation(Z[2][:, 0:T], Z[2][:, 0:T], ACT.Sqrt).then_inc(sqrt_ready, 1)
            wait_acc(act, A_OUT - 3)
            for k in range(KT):
                act.wait_ge(y_done, k + 2)
                act.activation(XNH[:, k, :], Y[:, k, :], ACT.Copy).then_inc(nhi_done, 1)
            act.dma_start(O["rg_conv"], RTAIL[:, :, :, :]).then_inc(rg_out, 16)
            act.dma_start(O["rg_h"], HTAIL[:, :, :]).then_inc(rg_out, 16)

            def ffn(l, a0):
                q = FS[l]

                def up(g, i=None):
                    for t in range(2):
                        f = 2 * g + t
                        for v in range(2):
                            n = 2 * f + v
                            if n >= 2:
                                act.wait_ge(q["u_used"], val(n - 1, i, 8))
                            src = (FST[:, v * FT + f] if i is None else
                                   FST[:, bass.ds(i * 4 + (v * FT + f), 1)].rearrange(
                                       "p a b s -> p (a b) s"))
                            act.activation(samples(Z[4 + v], FW - 1)[:, :, 0:FW - 1], src, ACT.Copy
                                           ).then_inc(q["u_state"], 1)
                        act.wait_ge(q["gc_ready"], val(f + 1, i, 4))
                        act.activation(Z[1][:, 0:T], Z[1][:, 0:T], ACT.Gelu_apprx_tanh
                                       ).then_inc(q["gg_ready"], 1)
                        act.wait_ge(q["hf_ready"], val(f + 1, i, 4))
                        if g >= 2:
                            wait_acc(act, down_acc(a0, g - 2, KT - 1), i, 24)
                        act.activation(HHI[:, f % 4, :], Z[2][:, 0:T], ACT.Copy
                                       ).then_inc(q["hh_ready"], 1)

                for g in range(3):
                    up(g)
                with act.Fori(0, (GROUPS - 4) // 2) as i:
                    for g in (3, 4):
                        up(g, i)
                up(GROUPS - 1)
                act.wait_ge(q["u_used"], 4 * GROUPS)
                act.dma_start(O["ffn_conv"][l], FTAIL[:, :, :, :]).then_inc(q["tail_out"], 16)

            norm_after_units(1, A_OUT, C_GFFN0, 0)
            act.wait_ge(fst_in, 16)
            ffn(0, A_F0)

            for k in range(KT):
                wait_read(act, down_acc(A_F0, GROUPS - 1, k))
                high(C_GKV, k)
            for k in range(KT):
                square(2, k)
            root(2)
            act.dma_start(S["x"], X[:, :, :]).then_inc(x_out, 16)
            wait_read(act, A_K + KT - 2)
            wait_read(act, A_K + KT - 1)
            act.dma_start(O["k"], KTR[:, :, :]).then_inc(k_out, 16)

            def v_out(j, i=None):
                wait_read(act, A_V + j, i, 2)
                act.activation(VTS[:, j, :] if i is None else
                               VTS[:, bass.ds(i * 2 + j, 1), :].rearrange("p a t -> p (a t)"),
                               Z[j % 2][:, SEQ:T], ACT.Copy).then_inc(vts_done, 1)
                dst = (O["v"][:, j, :] if i is None else
                       O["v"][:, bass.ds(i * 2 + j, 1), :].rearrange("p a t -> p (a t)"))
                act.dma_start(dst, Z[j % 2][:, 0:T]).then_inc(vt_out[j % 2], 16)

            act.wait_ge(FS[0]["tail_out"], 16)
            with act.Fori(0, KT // 2 - 1) as i:
                for j in range(2):
                    v_out(j, i)
            v_out(KT - 2)
            for k in range(KT):
                if k < KT - 1:
                    act.wait_ge(xn_free, KT - 1 + k + 1)
                else:
                    wait_acc(act, A_V + KT - 1)
                high(C_GMIX1, k)
            v_out(KT - 1)

            act.wait_ge(k_out, 16)
            def turn(hp, first=False, tail=False):
                for t in range(9 if tail else 16):
                    if not tail:
                        s, i = t // 8, TILES[t % 8]
                        for c in range(2):
                            act.wait_ge(nm_ready, hp * 32 + (2 * t + c + 1))
                            pr = PR[c][:, t % (4 - 2 * c), 0:(i + 1) * P]
                            act.activation(pr, pr, ACT.Exp, bias=MX[:, t % 4, 2 + c:3 + c],
                                           accum_out=SSUM[:, s, c, i:i + 1]).then_inc(e_done, 1)
                    v = t - 2
                    if live(v, first, tail):
                        n = TILES[v % 8] + 1
                        act.wait_ge(wt_done, hp * 16 + (v + 1))
                        if v >= 2 or not first:
                            act.wait_ge(pv_done, hp * 16 + (v - 1))
                        if n <= 4:
                            act.activation(WTS[:, v % 2, 0:n * P], PS[:, 4, 0:n * P], ACT.Copy
                                           ).then_inc(wt_read, 1)
                        else:
                            act.activation(WTS[:, v % 2, 0:512], PS[:, 4, :], ACT.Copy)
                            act.activation(WTS[:, v % 2, 512:n * P], PS[:, 5, 0:n * P - 512],
                                           ACT.Copy).then_inc(wt_read, 1)
                    for j in range(2):
                        if t == SAMPLE_STEP[j] + 1 and not tail:
                            act.wait_ge(snm_done, hp * 2 + (j + 1))
                            act.activation(SPR[0:SROWS, :], SPR[0:SROWS, :], ACT.Exp,
                                           bias=SST[:, 1:2], accum_out=SST[:, 2:3]
                                           ).then_inc(sexp_done, 1)
                        if t == SAMPLE_STEP[j] + 3 and not tail:
                            act.wait_ge(st_done, hp * 2 + (j + 1))
                            act.activation(SC1[:, :, :], PS[:, 7, 0:NPG * P].rearrange(
                                "p (g r) -> p g r", g=NPG)[:, :, NS * NH:SROWS], ACT.Copy)
                            act.activation(SCN[:, :], PS[0:TS, 7, NPG * P + NS * NH:
                                                         NPG * P + SROWS], ACT.Copy
                                           ).then_inc(sc1_done, 1)
                    if t in SQUARE_STEP and live(SQUARE_STEP[t], first, tail):
                        h = SQUARE_STEP[t]
                        act.wait_ge(o_read, hp * 16 + (8 * (h + 1) + 1))
                        act.activation(OQS[:, :, :], OQ[:, h % 2, :, :], ACT.Square
                                       ).then_inc(osq_done, 1)
                    if t in VAR_STEP and live(VAR_STEP[t], first, tail):
                        act.wait_ge(var_done, hp * 2 + (VAR_STEP[t] + 1))
                        act.activation(SM[:, 2], SM[:, 1], ACT.Sqrt, scale=1.0 / P
                                       ).then_inc(std_done, 1)
                    if t in OUT_STEP and live(OUT_STEP[t][0], first, tail):
                        h, half = OUT_STEP[t]
                        act.wait_ge(ot_done, hp * 4 + (2 * h + half + 1))
                        act.activation(OT[:, one(hp * 2 + h), half * 512:(half + 1) * 512
                                          ].rearrange("p a t -> p (a t)"),
                                       PS[:, 7, :], ACT.Copy, scale=SUBG[:, :]).then_inc(ot_read, 1)

            turns_of(act, turn)
            act.wait_ge(so_read, NB)
            act.activation(OSQ[:, :, :], OSM[:, :, :], ACT.Square).then_inc(sosq_done, 1)
            act.wait_ge(sored_done, 1)
            act.activation(OSQ[:, :, :].rearrange("p h t -> p (h t)"), PS[:, 1, 0:NH * TS], ACT.Sqrt,
                           scale=1.0 / P, bias=EPSC[:, :]).then_inc(sostd_done, 1)
            act.wait_ge(son_done, 1)
            act.activation(OT[:, :, SEQ:T], OSM[:, :, :], ACT.Copy, scale=SUBG[:, :]
                           ).then_inc(ot_full, 1)
            act.wait_ge(ot_full, 1)
            act.dma_start(X[:, :, :], S["x"]).then_inc(x_back, 16)
            act.dma_start(FST[:, :, :, :], I["ffn_state"][1]).then_inc(fst_in, 16)
            for k in range(KT):
                act.activation(XNH[:, k, :], OT[:, k, :], ACT.Copy).then_inc(nhi_done, 1)

            norm_after_units(3, A_O, C_GFFN1, 2 * (KT - 1))
            act.wait_ge(fst_in, 32)
            ffn(1, A_F1)
            for k in range(KT):
                wait_read(act, down_acc(A_F1, GROUPS - 1, k))
                square(4, k)
            root(4)

        @block.vector
        def _(dve):
            step = Steps(dve, dve_step)
            MUL, ADD, SUB = ALU.mult, ALU.add, ALU.subtract

            def conv_first(src, tmp, taps, bias, hist):
                n = SEQ + NB * (hist + NS)
                step(dve.tensor_scalar(tmp[:, 0:n], src[:, 0:n], taps[0], bias, MUL, ADD))
                for j in range(1, hist):
                    step(dve.scalar_tensor_tensor(tmp[:, 0:n], src[:, j:j + n], taps[j],
                                                  tmp[:, 0:n], MUL, ADD))

            def conv_last(src, tmp, dst, taps, hist, signal):
                dve.scalar_tensor_tensor(dst[:, 0:SEQ], src[:, hist:hist + SEQ], taps[hist],
                                         tmp[:, 0:SEQ], MUL, ADD)
                dve.scalar_tensor_tensor(dst[:, SEQ:T].rearrange("p (b s) -> p b s", b=NB),
                                         samples(src, hist)[:, :, hist:hist + NS], taps[hist],
                                         samples(tmp, hist)[:, :, 0:NS], MUL, ADD
                                         ).then_inc(signal, 1)

            def evac_line(a, line, hist, i=None, m=0):
                wait_acc(dve, a, i, m)
                b = 3 * (a % 2)
                c2, left = 2 * CH, SEQ - 2 * CH
                dve.tensor_tensor(line[:, hist:hist + c2].rearrange("p (c t) -> p c t", c=2),
                                  PS[:, b:b + 2, 0:CH],
                                  RINV[:, 0:c2].rearrange("p (c t) -> p c t", c=2), MUL)
                dve.tensor_tensor(line[:, hist + c2:hist + SEQ], PS[:, b + 2, 0:left],
                                  RINV[:, c2:SEQ], MUL)
                dve.tensor_tensor(samples(line, hist)[:, :, hist:hist + NS],
                                  PS[:, b + 2, left:CH].rearrange("p (b s) -> p b s", b=NB),
                                  RINV[:, SEQ:T].rearrange("p (b s) -> p b s", b=NB), MUL
                                  ).then_inc(acc_free[a % 2], 1)

            def evac(a, line, i=None, m=0):
                wait_acc(dve, a, i, m)
                dve.tensor_tensor(as_acc(line), acc(a), as_acc(RINV[:, :]), MUL
                                  ).then_inc(acc_free[a % 2], 1)

            def add_square(r, k):
                dve.wait_ge(sq_done, KT * r + k + 1)
                if k == 0:
                    dve.tensor_copy(Z[2][:, 0:T], Z[0][:, 0:T]).then_inc(sum_done, 1)
                else:
                    dve.wait_ge(sum_done, KT * r + k)
                    dve.tensor_tensor(Z[2][:, 0:T], Z[2][:, 0:T], Z[k % 2][:, 0:T], ADD
                                      ).then_inc(sum_done, 1)

            def low(m, gain, k):
                dve.wait_ge(nhi_done, KT * m + k + 1)
                dve.scalar_tensor_tensor(XNL[:, k, :], X[:, k, :], col(gain + k),
                                         XNH[:, k, :].bitcast(F32), MUL, SUB).then_inc(nlo_done, 1)

            def inverse(r):
                dve.wait_ge(root_done, 2 * r + 2)
                step(dve.reciprocal(RINV[:, :], RINV[:, :]))

            def lows(m, region):
                for k in range(KT):
                    dve.wait_ge(nhi_done, KT * m + k + 1)
                    dve.tensor_tensor(XNL[:, k, :], region[:, k, :], XNH[:, k, :].bitcast(F32), SUB
                                      ).then_inc(nlo_done, 1)

            def add_to_x(a, k, i=None, m=0, tm=0):
                wait_acc(dve, a, i, m)
                x = X[:, k, :] if not tm else tile(X, k, i, tm)
                dve.tensor_tensor(as_acc(x), acc(a), as_acc(x), ADD).then_inc(acc_free[a % 2], 1)

            dve.memset(TAB[BUCKETS:BUCKETS + 1, :], NEG).then_inc(dve_const, 1)
            dve.memset(Z[4][:, 0:RW - 1], 0.0).then_inc(rec_used, 1)
            dve.memset(Z[5][:, 0:FW - 1], 0.0).then_inc(y_done, 1)
            dve.memset(CROW[:, :], 1.0).then_inc(dve_const, 1)
            for j, q in enumerate((ttr_done, ttr_done, o_read, vtr_read, vtr_read)):
                dve.memset(CARRY[:, 3 + j:4 + j], 0.0).then_inc(q, 1)
            for k in range(KT):
                low(0, C_GMIX0, k)
                add_square(0, k)
            dve.wait_ge(lam_in, 16)
            for j in range(2):
                dve.tensor_tensor_reduce(LAMP[:, j], LAMV[:, 2 * j, :], LAMV[:, 2 * j + 1, :], 1.0,
                                         0.0, MUL, ADD, NLAM[:, j:j + 1]).then_inc(dve_const, 1)
            dve.wait_ge(c_in, 16)
            dve.tensor_scalar(HBA[:, :], COL[:, C_BA:C_BA + KT], 0.5, None, MUL)
            dve.tensor_scalar(HBX[:, :], COL[:, C_BX:C_BX + KT], 0.5, None, MUL)
            dve.tensor_scalar(SUBG[:, :], col(C_SUB), 1.0 - LAM_INIT, None, MUL)
            dve.wait_ge(act_const, 1)
            E, TT, W2, PP = SPT[:, 1], SPT[:, 2], SPT[:, 3], SPT[:, 0]
            step(dve.tensor_scalar(TT, E, 2.0, None, ADD))
            step(dve.reciprocal(TT, TT))
            step(dve.tensor_tensor(TT, TT, E, MUL))
            step(dve.tensor_tensor(W2, TT, TT, MUL))
            step(dve.tensor_scalar(PP, W2, 1.0 / 17, None, MUL))
            for d in (15, 13, 11, 9, 7, 5, 3):
                step(dve.scalar_tensor_tensor(PP, PP, 1.0 / d, W2, ADD, MUL))
            step(dve.scalar_tensor_tensor(PP, PP, 1.0, TT, ADD, MUL))
            step(dve.tensor_scalar(W2, COL[:, C_LAM:C_LAM + KT], -2.0, 0.0, MUL, ALU.max))
            step(dve.scalar_tensor_tensor(SP2[:, :], PP, 4.0, W2, MUL, ADD))
            dve.tensor_scalar(SPM[:, :], SP2[:, :], -2.0, None, MUL).then_inc(scal_done, 1)
            dve.wait_ge(act_const, 2)
            step(dve.tensor_tensor(NLAM[:, 2:3], NLAM[:, 1:2], NLAM[:, 0:1], SUB))
            step(dve.tensor_scalar(NLAM[:, 3:4], NLAM[:, 2:3], LAM_INIT, None, SUB))
            step(dve.tensor_copy(CROW[NS * NH:SROWS, :], NLAM[NS * NH:SROWS, 3:4]))

            inverse(0)
            dve.wait_ge(line_out, 16)
            dve.wait_ge(rst_in, 32)
            with dve.Fori(0, KT) as n:
                step.enter(n, 10)
                dve.wait_ge(y_done, n + 1)
                REC, XC, TI, SQ, A_, S_, G_ = Z[4], Z[0], Z[1], Z[2], Z[3], Z[6], Z[5]
                evac_line(A_RG, REC, RW - 1, n, 4)
                dve.wait_ge(rec_state, n + 1)
                wait_read(dve, A_RG, n, 4)
                taps = [col(C_RGW + j * KT, n) for j in range(RW)]
                conv_first(REC, S_, taps, col(C_RGB, n), RW - 1)
                conv_last(REC, S_, XC, taps, RW - 1, xc_ready)
                dve.tensor_copy(RTAIL[:, bass.ds(n, 1), 0, :].rearrange("p a s -> p (a s)"),
                                REC[:, SEQ:SEQ + RW - 1])
                dve.tensor_copy(RTAIL[:, bass.ds(n, 1), 1:NB + 1, :].rearrange("p a b s -> p (a b) s"),
                                samples(REC, RW - 1)[:, :, NS:NS + RW - 1]).then_inc(rec_used, 1)
                dve.wait_ge(xch_ready, n + 1)
                dve.wait_ge(xc_ready, n + 1)
                dve.tensor_tensor(XCL[:, :], XC[:, 0:T], XCH[:, :].bitcast(F32), SUB
                                  ).then_inc(xcl_ready, 1)
                evac(A_RG + 1, G_[:, 0:T], n, 4)
                wait_read(dve, A_RG + 3, n, 4)
                step(dve.scalar_tensor_tensor(TI[:, 0:T], TI[:, 0:T], 1.0, XC[:, 0:T], ADD, MUL))
                dve.wait_ge(sqrt_ready, n + 1)
                step(dve.scalar_tensor_tensor(SQ[:, 0:T], A_[:, 0:T], 1.0, SQ[:, 0:T], ADD, MUL))
                step(dve.scalar_tensor_tensor(SQ[:, 0:T], SQ[:, 0:T], 0.5, TI[:, 0:T], MUL, MUL))
                dve.tensor_scalar(SQ[:, 0:1], TI[:, 0:1], 0.5, None, MUL)
                first = A_[:, SEQ:T:NS]
                step(dve.tensor_tensor(T8[:, :], first,
                                       H0[:, bass.ds(n, 1), :].rearrange("p a b -> p (a b)"), MUL))
                step(dve.tensor_tensor(SQ[:, SEQ:T:NS], SQ[:, SEQ:T:NS], T8[:, :], ADD))
                dve.memset(A_[:, 0:1], 0.0)
                step(dve.memset(first, 0.0))
                step(dve.tensor_tensor_scan(S_[:, 0:T], A_[:, 0:T], SQ[:, 0:T], 0.0, MUL, ADD))
                dve.tensor_copy(HTAIL[:, bass.ds(n, 1), 0:1].rearrange("p a b -> p (a b)"),
                                S_[:, SEQ - 1:SEQ])
                dve.tensor_copy(HTAIL[:, bass.ds(n, 1), 1:NB + 1].rearrange("p a b -> p (a b)"),
                                S_[:, SEQ + NS - 1:T:NS])
                dve.wait_ge(gel_ready, n + 1)
                dve.tensor_tensor(tile(Y, 0, n), S_[:, 0:T], Z[5][:, 0:T], MUL).then_inc(y_done, 1)
                step.leave(KT)
            lows(1, Y)

            def norm_after_units(r, a0, m, gain):
                for k in range(KT - 1):
                    add_to_x(a0 + k, k)
                    add_square(r, k)
                for k in range(KT - 1):
                    low(m, gain, k)
                add_to_x(a0 + KT - 1, KT - 1)
                low(m, gain, KT - 1)
                add_square(r, KT - 1)
                inverse(r)

            norm_after_units(1, A_OUT, 2, C_GFFN0)

            def ffn(l, a0):
                q = FS[l]

                def taps(g, t, v, i):
                    c = C_FW + l * NFC + v * FT + 2 * g + t
                    return [col(c + j * 2 * FT, None if i is None else i * 4) for j in range(FW + 1)]

                def arrived(g, t, v, i):
                    n = 2 * (2 * g + t) + v
                    if n >= 2:
                        dve.wait_ge(q["u_used"], val(n - 1, i, 8))
                    a = up_acc(a0, g, 2 * t + v)
                    evac_line(a, Z[4 + v], FW - 1, i, 24)
                    dve.wait_ge(q["u_state"], val(n + 1, i, 8))
                    wait_read(dve, a, i, 24)
                    f = 2 * g + t
                    if v:
                        dve.wait_ge(q["vc_ready"], val(f + 1, i, 4))
                    elif f:
                        dve.wait_ge(q["hf_ready"], val(f, i, 4))

                def tails(g, t, v, i):
                    c = v * FT + 2 * g + t
                    at_ = slice(c, c + 1) if i is None else bass.ds(i * 4 + c, 1)
                    src = Z[4 + v]
                    dve.tensor_copy(FTAIL[:, at_, 0, :].rearrange("p a s -> p (a s)"),
                                    src[:, SEQ:SEQ + FW - 1])
                    dve.tensor_copy(FTAIL[:, at_, 1:NB + 1, :].rearrange("p a b s -> p (a b) s"),
                                    samples(src, FW - 1)[:, :, NS:NS + FW - 1]
                                    ).then_inc(q["u_used"], 1)

                def convolved(g, t, v, i):
                    arrived(g, t, v, i)
                    w = taps(g, t, v, i)
                    conv_first(Z[4 + v], Z[6], w, w[FW], FW - 1)
                    conv_last(Z[4 + v], Z[6], Z[v], w, FW - 1, q["gc_ready" if v else "vc_ready"])
                    tails(g, t, v, i)

                def gated(f, i):
                    dve.wait_ge(q["vc_ready"], val(f + 1, i, 4))
                    if f:
                        dve.wait_ge(q["hl_ready"], val(f, i, 4))
                    dve.wait_ge(q["gg_ready"], val(f + 1, i, 4))
                    dve.tensor_tensor(Z[2][:, 0:T], Z[0][:, 0:T], Z[1][:, 0:T], MUL
                                      ).then_inc(q["hf_ready"], 1)

                def low_h(f, i):
                    dve.wait_ge(q["hh_ready"], val(f + 1, i, 4))
                    dve.wait_ge(q["hf_ready"], val(f + 1, i, 4))
                    dve.tensor_tensor(HLO[:, f % 4, :], Z[2][:, 0:T], HHI[:, f % 4, :].bitcast(F32),
                                      SUB).then_inc(q["hl_ready"], 1)

                def group(g, i=None):
                    f = 2 * g

                    def outs(lo, hi):
                        if g:
                            for o in range(lo, hi):
                                add_to_x(down_acc(a0, g - 1, o), o, i, 24)

                    convolved(g, 0, 0, i)
                    convolved(g, 0, 1, i)
                    gated(f, i)
                    low_h(f, i)
                    convolved(g, 1, 0, i)
                    arrived(g, 1, 1, i)
                    w = taps(g, 1, 1, i)
                    conv_first(Z[5], Z[6], w, w[FW], FW - 1)
                    outs(0, 1)
                    conv_last(Z[5], Z[6], Z[1], w, FW - 1, q["gc_ready"])
                    tails(g, 1, 1, i)
                    outs(1, 3)
                    gated(f + 1, i)
                    outs(3, 4)
                    low_h(f + 1, i)
                    outs(4, KT)

                step(dve.memset(Z[4][:, 0:FW - 1], 0.0))
                step(dve.memset(Z[5][:, 0:FW - 1], 0.0))
                group(0)
                with dve.Fori(0, (GROUPS - 2) // 2) as i:
                    step.enter(i, 16)
                    group(1, i)
                    group(2, i)
                    step.leave((GROUPS - 2) // 2)
                group(GROUPS - 1)

            ffn(0, A_F0)

            for k in range(KT):
                add_to_x(down_acc(A_F0, GROUPS - 1, k), k)
                if k:
                    low(3, C_GKV, k - 1)
            low(3, C_GKV, KT - 1)
            for k in range(KT):
                add_square(2, k)
            inverse(2)
            with dve.Fori(0, KT // 2) as i:
                for s in range(2):
                    evac(A_K + s, tile(KTR, s, i, 2), i, 2)
            dve.wait_ge(FS[0]["tail_out"], 16)

            def v_line(j, i=None):
                if j >= 2:
                    dve.wait_ge(vtr_done, val(2 * j - 2, i, 4))
                    dve.wait_ge(vts_done, val(j - 1, i, 2))
                    dve.wait_ge(vt_out[j % 2], val(16 * (j // 2), i, 16))
                evac(A_V + j, Z[j % 2][:, 0:T], i, 2)

            def v_rows(j, i=None):
                at_ = slice(j, j + 1) if i is None else bass.ds(i * 2 + j, 1)
                for b in range(2):
                    dve.wait_ge(vtr_done, val(2 * j + b + 1, i, 4))
                    dve.tensor_copy(V[:, at_, 4 * b:4 * b + 4, :].rearrange("p a t e -> p (a t) e"),
                                    PS[:, 6 + b, :].rearrange("p (t e) -> p t e", t=4)
                                    ).then_inc(vtr_read, 1)

            v_line(0)
            v_line(1)
            with dve.Fori(0, KT // 2 - 2) as i:
                for j in range(2):
                    v_rows(j, i)
                    v_line(j + 2, i)
            v_rows(KT - 4)
            v_line(KT - 2)
            v_rows(KT - 3)
            for k in range(KT - 1):
                low(4, C_GMIX1, k)
            v_line(KT - 1)
            low(4, C_GMIX1, KT - 1)
            v_rows(KT - 2)
            v_rows(KT - 1)
            dve.wait_ge(vtr_done, 2 * KT + 1)
            dve.tensor_copy(VS[:, :, :].rearrange("p (b h) e -> p b h e", b=2),
                            PS[0:TS, 6:8, :].rearrange("p b (h e) -> p b h e", h=4)
                            ).then_inc(vtr_read, 1)
            dve.wait_ge(x_out, 16)
            with dve.Fori(0, KT // 2) as i:
                for s in range(2):
                    wait_acc(dve, A_Q + s, i, 2)
                    dve.scalar_tensor_tensor(as_acc(tile(QT, s, i, 2)), acc(A_Q + s), HD ** -0.5,
                                             as_acc(RINV[:, :]), MUL, MUL
                                             ).then_inc(acc_free[(A_Q + s) % 2], 1)

            wait_acc(dve, A_Q + KT - 1)
            step(dve.memset(SMK[:, :], NEG))
            step(dve.memset(QP[:, :], 0.0))
            step(dve.memset(SPR[:, :], 0.0))
            dve.wait_ge(sb_in, 16 * 2 * NS)
            step(dve.tensor_copy(SMK[:, :].rearrange("p (q x) -> p q x", q=NB)[:, :, 0:NS],
                                 SBI[:, PAST:NKEY].unsqueeze(1).to_broadcast([SROWS, NB, NS])))

            def sample_queries(j, hp):
                for c in range(2):
                    q = slice(c * HD, (c + 1) * HD)
                    last = dve.tensor_copy(
                        QP[q, :].rearrange("p (h x) -> p h x", x=SROWS + 1)[
                            :, :, c * NS * NH:(c + 1) * NS * NH:NH],
                        QT[q, :, some(hp * (2 * NS) + (SEQ + NS * j), NS)])
                last.then_inc(qp_done, 1)

            def sample_maxima(j, hp):
                dve.wait_ge(ss_done, hp * 2 + (j + 1))
                dve.tensor_tensor(SPR[0:SROWS, 0:PAST], PS[0:SROWS, 7, 0:PAST], SBI[:, 0:PAST], ADD)
                step(dve.tensor_tensor(SPR[0:SROWS, PAST:PAST + TS], PS[0:SROWS, 7, PAST:PAST + TS],
                                       SMK[:, some(hp * (2 * TS) + j * TS, TS)], ADD))
                step(dve.reduce_max(SST[:, 0:1], SPR[0:SROWS, :], X_AXIS))
                dve.tensor_scalar(SST[:, 1:2], SST[:, 0:1], -1.0, None, MUL).then_inc(snm_done, 1)

            def sample_weights(j, hp):
                dve.wait_ge(sexp_done, hp * 2 + (j + 1))
                step(dve.reciprocal(SST[:, 3:4], SST[:, 2:3]))
                dve.tensor_scalar(SPR[0:SROWS, :], SPR[0:SROWS, :], SST[:, 3:4], CROW[0:SROWS, :], MUL, MUL
                                  ).then_inc(spn_done, 1)

            def sample_combine(j, hp):
                dve.wait_ge(sc1_done, hp * 2 + (j + 1))
                dve.tensor_tensor(SW[:, :, :], PS[:, 7, 0:NPG * P].rearrange(
                    "p (g r) -> p g r", g=NPG)[:, :, 0:NS * NH], SC1[:, :, :], ADD)
                dve.tensor_tensor(SWN[:, :], PS[0:TS, 7, NPG * P:NPG * P + NS * NH],
                                  SCN[:, :], ADD).then_inc(sw_done, 1)

            def sample_output(j, hp):
                dve.wait_ge(so_done, hp * 2 + (j + 1))
                dve.tensor_copy(OSM[:, :, some(hp * (2 * NS) + NS * j, NS)],
                                PS[:, 7, 0:NH * NS].rearrange("p (h s) -> p h s", h=NH)
                                ).then_inc(so_read, 1)

            def turn(hp, first=False, tail=False):
                for t in range(9 if tail else 16):
                    for j in range(2):
                        if t == SAMPLE_STEP[j] + 6 and not tail:
                            sample_output(j, hp)
                    v = t - 4
                    if live(v, first, tail):
                        h = v // 8
                        dve.wait_ge(pv_done, hp * 16 + (v + 1))
                        if v % 8 == 0 and not first:
                            dve.wait_ge(ot_read, hp * 4 + (2 * h - 1))
                        dve.tensor_copy(OQ[:, h % 2, TILES[v % 8], :], PS[:, 6, 0:P]
                                        ).then_inc(o_read, 1)
                    if not tail:
                        s, i = t // 8, TILES[t % 8]
                        n = (i + 1) * P
                        if t % 8 == 0:
                            dve.wait_ge(bias_in[s], hp * 16 + 16)
                        if t >= 2 or not first:
                            dve.wait_ge(wc_done, hp * 16 + (t - 1))
                        for c in range(2):
                            dve.wait_ge(s_done, hp * 32 + (2 * t + c + 1))
                            dve.memset(CARRY[:, 1 + c:2 + c], 0.0)
                            dve.tensor_tensor_reduce(
                                PR[c][:, t % (4 - 2 * c), 0:n],
                                PS[:, 2 * c:2 * c + 2, :].rearrange("p b n -> p (b n)")[:, 0:n],
                                BIAS[:, s, SEQ - n:SEQ], 1.0, -3e38, ADD, ALU.max,
                                MX[:, t % 4, c:c + 1]).then_inc(ttr_done, 1)
                        for c in range(2):
                            dve.wait_ge(ttr_done, hp * 32 + (2 + 2 * t + c + 1))
                            dve.tensor_scalar(MX[:, t % 4, 2 + c:3 + c], MX[:, t % 4, c:c + 1],
                                              -1.0, None, MUL).then_inc(nm_ready, 1)
                    v = t - 1
                    if live(v, first, tail):
                        s, i = v // 8 % 2, TILES[v % 8]
                        n = (i + 1) * P
                        dve.wait_ge(e_done, hp * 32 + (2 * v + 2))
                        if v > 0 or not first:
                            dve.wait_ge(wc_done, hp * 16 + v)
                        step(dve.reciprocal(SM[:, 3, 0:1], SSUM[:, s, 1, i:i + 1]))
                        step(dve.scalar_tensor_tensor(SM[:, 3, 1:2], SM[:, 3, 0:1],
                                                      NLAM[:, 3:4], SSUM[:, s, 0, i:i + 1], MUL, MUL))
                        dve.scalar_tensor_tensor(PR[0][:, v % 4, 0:n], PR[1][:, v % 2, 0:n],
                                                 SM[:, 3, 1:2], PR[0][:, v % 4, 0:n], MUL, ADD
                                                 ).then_inc(wc_done, 1)
                    for j in range(2):
                        if not tail:
                            if t == SAMPLE_STEP[j] - 1:
                                sample_queries(j, hp)
                            if t == SAMPLE_STEP[j]:
                                sample_maxima(j, hp)
                            if t == SAMPLE_STEP[j] + 1:
                                sample_weights(j, hp)
                            if t == SAMPLE_STEP[j] + 3:
                                sample_combine(j, hp)
                    if t in VAR_STEP and live(VAR_STEP[t], first, tail):
                        h = VAR_STEP[t]
                        dve.wait_ge(osq_done, hp * 2 + (h + 1))
                        step(dve.tensor_reduce(SM[:, 0], OQS[:, :, :], X_AXIS, ADD))
                        s0 = SSUM[:, h % 2, 0, :]
                        step(dve.tensor_tensor(SM[:, 1], s0, s0, MUL))
                        dve.scalar_tensor_tensor(SM[:, 1], SM[:, 1], P * EPS, SM[:, 0], MUL, ADD
                                                 ).then_inc(var_done, 1)
                    if t in SCALE_STEP and live(SCALE_STEP[t], first, tail):
                        h = SCALE_STEP[t]
                        dve.wait_ge(std_done, hp * 2 + (h + 1))
                        step(dve.reciprocal(SM[:, 2], SM[:, 2]))
                        dve.tensor_tensor(OQ[:, h % 2, :, :], OQ[:, h % 2, :, :],
                                          SM[:, 2].unsqueeze(2).to_broadcast([P, 8, P]), MUL
                                          ).then_inc(on_done, 1)

            turns_of(dve, turn, lambda hp: step.enter(hp, 16 * 2 + 2 * 3 + 2 * 3, 1),
                     lambda: step.leave(NH // 2))
            dve.wait_ge(sostd_done, 1)
            step(dve.reciprocal(OSQ[:, :, :], OSQ[:, :, :]))
            dve.tensor_tensor(OSM[:, :, :], OSM[:, :, :], OSQ[:, :, :], MUL).then_inc(son_done, 1)
            dve.wait_ge(ot_full, 1)
            lows(5, OT)
            dve.wait_ge(x_back, 16)
            norm_after_units(3, A_O, 6, C_GFFN1)
            ffn(1, A_F1)
            for k in range(KT):
                add_to_x(down_acc(A_F1, GROUPS - 1, k), k)
                add_square(4, k)
            inverse(4)
            for k in range(KT):
                dve.scalar_tensor_tensor(Y[:, k, :], X[:, k, :], col(C_GOUT + k), RINV[:, :],
                                         MUL, MUL).then_inc(yt_done, 1)


_OUTPUTS = {
    "y": (P, KT, T), "rg_h": (P, KT, NB + 1), "rg_conv": (P, KT, NB + 1, RW - 1),
    "ffn_conv": (2, P, 2 * FT, NB + 1, FW - 1), "k": (P, KT, T), "v": (P, KT, T),
}


def _tiles(a, rest=()):
    a = np.asarray(a)
    return a.reshape(a.shape[0] // P, P, *a.shape[1:]).swapaxes(0, 1)


def _weight_units(w):
    k, n = w.shape
    return w.reshape(k // P, P, n // P, P).transpose(2, 1, 0, 3)


def _ffn_units(up, down):
    u = _weight_units(up)
    d = down.reshape(GROUPS, 2, P, 2, 4, P).transpose(0, 3, 2, 4, 1, 5).reshape(GROUPS, 2, P, KT, P)
    ups = [np.stack([u[f], u[FT + f]]) for f in range(FT)]
    parts = [ups[0], ups[1]]
    for g in range(GROUPS):
        if g + 1 < GROUPS:
            parts += [ups[2 * g + 2], ups[2 * g + 3]]
        parts.append(d[g])
    return np.concatenate(parts)


def _one_hot():
    rel = REL0 - np.arange(LINE)
    n = np.maximum(rel, 0)
    exact = BUCKETS // 2
    nf = np.maximum(n, 1).astype(np.float32)
    large = exact + (np.log(nf / np.float32(exact)) / np.float32(np.log(MAXDIST / exact))
                     * np.float32(BUCKETS - exact)).astype(np.int32)
    bucket = np.where(n < exact, n, np.minimum(large, BUCKETS - 1))
    hot = np.zeros((BUCKETS + 1, LINE), np.float32)
    hot[np.where(rel >= 0, bucket, BUCKETS), np.arange(LINE)] = 1.0
    return hot


def kernel(x_prompt, x_sample, state_rglru_h, state_rglru_conv, state_ffn_conv, cache_k, cache_v,
           page_table, rel_bias, norm_mix, norm_ffn, final_norm, rg_w_in, rg_conv_w, rg_conv_b,
           rg_w_a, rg_b_a, rg_w_x, rg_b_x, rg_lambda, rg_w_out, kv_norm, w_kv, attn_w_q, lam_q1,
           lam_k1, lam_q2, lam_k2, attn_subln, attn_w_o, ffn_w_up, ffn_conv_w, ffn_conv_b,
           ffn_w_down):
    import concourse.bacc as bacc
    from concourse.bass_utils import run_bass_kernel_spmd

    f = {k: np.asarray(v) for k, v in locals().items() if k not in ("bacc", "run_bass_kernel_spmd")}
    x = np.concatenate([f["x_prompt"].reshape(SEQ, D), f["x_sample"].reshape(TS, D)])

    w_in = _weight_units(f["rg_w_in"][0])
    gates = np.zeros((KT, P, KT, P), np.float32)
    gates[:, :, 0] = f["rg_w_a"][0]
    gates[:, :, 1] = f["rg_w_x"][0]
    rg = np.stack([w_in[KT:], w_in[:KT], gates], 1).reshape(3 * KT, P, KT, P)
    w = np.concatenate([
        rg, _weight_units(f["rg_w_out"][0]), _ffn_units(f["ffn_w_up"][0], f["ffn_w_down"][0]),
        _weight_units(f["w_kv"]), _weight_units(f["attn_w_q"][0]), _weight_units(f["attn_w_o"][0]),
        _ffn_units(f["ffn_w_up"][1], f["ffn_w_down"][1])])

    def cols(*vectors):
        return np.concatenate([_tiles(v) for v in vectors], 1)

    columns = cols(
        f["norm_mix"][0], f["norm_ffn"][0], f["kv_norm"], f["norm_mix"][1], f["norm_ffn"][1],
        f["final_norm"], *f["rg_conv_w"][0], f["rg_conv_b"][0], f["rg_b_a"][0], f["rg_b_x"][0],
        f["rg_lambda"][0], f["attn_subln"][0], *f["ffn_conv_w"][0], f["ffn_conv_b"][0],
        *f["ffn_conv_w"][1], f["ffn_conv_b"][1])
    lam = np.stack([f["lam_q1"][0], f["lam_k1"][0], f["lam_q2"][0], f["lam_k2"][0]])

    inputs = {
        "x": _tiles(x.T),
        "w": w,
        "columns": columns,
        "lam": np.broadcast_to(lam, (P, 4, HD)),
        "rel_bias": f["rel_bias"],
        "one_hot": _one_hot(),
        "rg_conv_state": _tiles(f["state_rglru_conv"][0].transpose(2, 0, 1)),
        "rg_h_state": _tiles(f["state_rglru_h"][0].T),
        "ffn_state": np.stack([_tiles(s.transpose(2, 0, 1)) for s in f["state_ffn_conv"]]),
        "cache_k": f["cache_k"].reshape(NPOOL, PAGE, NH, P).transpose(0, 3, 2, 1),
        "cache_v": f["cache_v"],
        "page_table": f["page_table"].reshape(1, NB * NPG),
    }
    inputs = {k: np.ascontiguousarray(v) for k, v in inputs.items()}

    nc = bacc.Bacc("TRN2", target_bir_lowering=False, num_devices=1, dynamic_dma_scratch_size=1024)
    dt = mybir.dt
    I = {k: nc.dram_tensor(f"in_{k}", v.shape, dt.from_np(v.dtype), kind="ExternalInput").ap()
         for k, v in inputs.items()}
    O = {k: nc.dram_tensor(f"out_{k}", s, dt.float32, kind="ExternalOutput").ap()
         for k, s in _OUTPUTS.items()}
    S = {k: nc.dram_tensor(f"scratch_{k}", s, dt.float32, kind="Internal").ap()
         for k, s in {"x": (P, KT, T), "line": (NH, P * LINE)}.items()}
    program(nc, I, O, S)
    r = run_bass_kernel_spmd(nc, [{f"in_{k}": v for k, v in inputs.items()}], core_ids=[0])
    out = {k: r.results[0][f"out_{k}"] for k in _OUTPUTS}

    def rows(a):
        return a.transpose(2, 1, 0).reshape(a.shape[2], -1)

    y, k, v = rows(out["y"]), rows(out["k"]), rows(out["v"])
    h = out["rg_h"].transpose(2, 1, 0).reshape(NB + 1, D)
    rc = out["rg_conv"].transpose(2, 3, 1, 0).reshape(NB + 1, RW - 1, D)
    fc = out["ffn_conv"].transpose(0, 3, 4, 2, 1).reshape(2, NB + 1, FW - 1, 2 * DFF)
    c = np.ascontiguousarray
    return (c(y[:SEQ].reshape(1, SEQ, D)), c(y[SEQ:].reshape(NB, NS, D)),
            c(h[None, :1]), c(rc[None, :1]), c(fc[:, :1]),
            c(k[:SEQ].reshape(1, SEQ, NH, 2, HD)), c(v[:SEQ].reshape(1, SEQ, NH, 2 * HD)),
            c(h[None, 1:]), c(rc[None, 1:]), c(fc[:, 1:]),
            c(k[SEQ:].reshape(NB, NS, NH, 2, HD)), c(v[SEQ:].reshape(NB, NS, NH, 2 * HD)))
```
